# Optimizing a Trainium2 kernel written in Bass

```python
import jax, jax.numpy as jnp
from jax import lax
import numpy as np

D_MODEL = 1024
BATCH = 1
SEQ = 128
DEPTH = 2
DEC_BATCH = 1
DEC_SEQ = 256
PAST_LEN = 128

GRID_W = 64
N_MIXERS = 2
EPS = 1e-6
N_MOD = 9
D_FF = 2816
FFN_RES = 0.5
D_RNN = 1280
RG_BLOCKS = 10
RG_BLOCK = D_RNN // RG_BLOCKS
CONV_W = 4
CONV_PAD_L = (CONV_W - 1) // 2
RG_C = 8.0
GLA_HEADS = 4
GLA_QK = D_MODEL // 2
GLA_V = D_MODEL
GLA_DK = GLA_QK // GLA_HEADS
GLA_DV = GLA_V // GLA_HEADS
GLA_RANK = 16
GLA_TAU = 16.0
GLA_CHUNK = 32
GLA_IN = 2 * GLA_QK + 2 * GLA_V + 2 * GLA_RANK

kernel_name = "hybrid_rglru_gla_diffusion_step"

def rms_norm(x, g):
    xf = x.astype(jnp.float32)
    y = xf * lax.rsqrt(jnp.mean(xf * xf, axis=-1, keepdims=True) + EPS)
    return (y * g.astype(jnp.float32)).astype(x.dtype)

def ada_mod(cvec, w, b):
    m = jax.nn.silu(cvec) @ w + b
    return m.reshape(-1, 1, N_MOD, D_MODEL)

def modulated(x, mod, gains, j):
    return rms_norm(x, gains[j]) * (1.0 + mod[:, :, 3 * j + 1]) + mod[:, :, 3 * j]

def swiglu(h, w_in, w_out):
    g, u = jnp.split(h @ w_in, 2, axis=-1)
    return (jax.nn.silu(g) * u) @ w_out

def half_ffn(x, mod, gains, j, w_in, w_out):
    return x + FFN_RES * mod[:, :, 3 * j + 2] * swiglu(modulated(x, mod, gains, j), w_in, w_out)

def centred_dwconv(x, w, b):
    y = lax.conv_general_dilated(x, w[:, None, :], window_strides=(1,),
                                 padding=[(CONV_PAD_L, CONV_W - 1 - CONV_PAD_L)],
                                 dimension_numbers=('NWC', 'WIO', 'NWC'),
                                 feature_group_count=x.shape[-1])
    return y + b

def rglru_scan(xc, w_a, b_a, w_i, b_i, lam, h0, reverse):
    bsz, t_len, _ = xc.shape
    f32 = jnp.float32
    xf = xc.astype(f32)
    xb = xf.reshape(bsz, t_len, RG_BLOCKS, RG_BLOCK)
    r = jax.nn.sigmoid(jnp.einsum('btnk,nkj->btnj', xb, w_a.astype(f32)).reshape(bsz, t_len, D_RNN) + b_a.astype(f32))
    gi = jax.nn.sigmoid(jnp.einsum('btnk,nkj->btnj', xb, w_i.astype(f32)).reshape(bsz, t_len, D_RNN) + b_i.astype(f32))
    log_a = -RG_C * r * jax.nn.softplus(-lam.astype(f32))
    a = jnp.exp(log_a)
    u = jnp.sqrt(-jnp.expm1(2.0 * log_a)) * (gi * xf)

    def step(h, inp):
        a_t, u_t = inp
        h = a_t * h + u_t
        return h, h

    h_last, hs = lax.scan(step, h0.astype(f32), (a.swapaxes(0, 1), u.swapaxes(0, 1)), reverse=reverse)
    return hs.swapaxes(0, 1), h_last

def rglru_mixer(h, w_in, conv_w, conv_b, w_a, b_a, w_i, b_i, lam, w_out, h0_f, h0_b):
    gate_br, x_br = jnp.split(h @ w_in, 2, axis=-1)
    xc = centred_dwconv(x_br, conv_w, conv_b)
    y_f, s_f = rglru_scan(xc, w_a[0], b_a[0], w_i[0], b_i[0], lam[0], h0_f, False)
    y_b, s_b = rglru_scan(xc, w_a[1], b_a[1], w_i[1], b_i[1], lam[1], h0_b, True)
    y = (y_f + y_b).astype(h.dtype) * jax.nn.gelu(gate_br)
    return y @ w_out, jnp.stack([s_f, s_b], axis=1)

def gla_chunked(q, k, v, log_g, s0):
    bsz, t_len, n_h = q.shape[0], q.shape[1], q.shape[2]
    n_chunks = t_len // GLA_CHUNK

    def chunk(a):
        return a.reshape((bsz, n_chunks, GLA_CHUNK) + a.shape[2:])

    q, k, v, log_g = chunk(q), chunk(k), chunk(v), chunk(log_g)
    b = jnp.cumsum(log_g, axis=2)
    b_last = b[:, :, -1:]
    causal = jnp.tril(jnp.ones((GLA_CHUNK, GLA_CHUNK), dtype=bool))[None, None, :, :, None, None]
    rel = jnp.where(causal, b[:, :, :, None] - b[:, :, None, :], -jnp.inf)
    scores = jnp.einsum('bnihd,bnjhd,bnijhd->bnhij', q, k, jnp.exp(rel))
    o_intra = jnp.einsum('bnhij,bnjhv->bnihv', scores, v)
    u = jnp.einsum('bnchk,bnchv->bnhkv', k * jnp.exp(b_last - b), v)
    a_chunk = jnp.exp(b_last[:, :, 0])

    def step(s, inp):
        a_n, u_n = inp
        return a_n[..., None] * s + u_n, s

    s_final, s_enter = lax.scan(step, s0, (jnp.moveaxis(a_chunk, 1, 0), jnp.moveaxis(u, 1, 0)))
    s_enter = jnp.moveaxis(s_enter, 0, 1)
    o_inter = jnp.einsum('bnchk,bnhkv->bnchv', q * jnp.exp(b), s_enter)
    return (o_intra + o_inter).reshape(bsz, t_len, n_h, v.shape[-1]), s_final

def gla_mixer(h, w_in, w_g2, b_g, g_norm, w_out, s0_f, s0_b):
    bsz, t_len, _ = h.shape
    f32 = jnp.float32
    proj = h @ w_in
    q, k, v, r, z_f, z_b = jnp.split(proj, [GLA_QK, 2 * GLA_QK, 2 * GLA_QK + GLA_V,
                                          2 * GLA_QK + 2 * GLA_V, 2 * GLA_QK + 2 * GLA_V + GLA_RANK], axis=-1)
    q = q.astype(f32).reshape(bsz, t_len, GLA_HEADS, GLA_DK) * (GLA_DK ** -0.5)
    k = k.astype(f32).reshape(bsz, t_len, GLA_HEADS, GLA_DK)
    v = v.astype(f32).reshape(bsz, t_len, GLA_HEADS, GLA_DV)

    def log_gate(z, w2, bias):
        zz = z.astype(f32) @ w2.astype(f32) + bias.astype(f32)
        return (-jax.nn.softplus(-zz) / GLA_TAU).reshape(bsz, t_len, GLA_HEADS, GLA_DK)

    def flip(t):
        return jnp.flip(t, axis=1)

    o_f, s_f = gla_chunked(q, k, v, log_gate(z_f, w_g2[0], b_g[0]), s0_f.astype(f32))
    o_b, s_b = gla_chunked(flip(q), flip(k), flip(v), flip(log_gate(z_b, w_g2[1], b_g[1])), s0_b.astype(f32))
    o = o_f + flip(o_b)
    o = o * lax.rsqrt(jnp.mean(o * o, axis=-1, keepdims=True) + EPS) * g_norm.astype(f32).reshape(GLA_HEADS, GLA_DV)
    o = o.reshape(bsz, t_len, GLA_V).astype(h.dtype) * jax.nn.silu(r)
    return o @ w_out, jnp.stack([s_f, s_b], axis=1)

def to_col_major(x, rows):
    bsz, t_len, d = x.shape
    return x.reshape(bsz, rows, GRID_W, d).swapaxes(1, 2).reshape(bsz, t_len, d)

def from_col_major(x, rows):
    bsz, t_len, d = x.shape
    return x.reshape(bsz, GRID_W, rows, d).swapaxes(1, 2).reshape(bsz, t_len, d)

def setup_inputs(seed: int = 0) -> dict:
    key = jax.random.key(seed)
    ks = iter(jax.random.split(key, 32))
    n_a = (DEPTH + 1) // 2
    n_b = DEPTH // 2
    f32 = jnp.float32

    def nrm(shape, scale):
        return jax.random.normal(next(ks), shape, f32) * scale

    x_prompt = nrm((BATCH, SEQ, D_MODEL), 1.0)
    x_sample = nrm((DEC_BATCH, DEC_SEQ, D_MODEL), 1.0)
    c = nrm((DEC_BATCH, D_MODEL), 1.0)
    state_rglru = nrm((DEC_BATCH, n_a, 2, D_RNN), 1.0)
    state_gla = nrm((DEC_BATCH, n_b, 2, GLA_HEADS, GLA_DK, GLA_DV), 1.0)
    c_ctx = nrm((D_MODEL,), 1.0)
    ada_w = nrm((DEPTH, D_MODEL, N_MOD * D_MODEL), 0.5 * D_MODEL ** -0.5)
    ada_b = nrm((DEPTH, N_MOD * D_MODEL), 0.02)
    norm_g = 1.0 + nrm((DEPTH, 3, D_MODEL), 0.05)
    ffn_w_in = nrm((DEPTH, 2, D_MODEL, 2 * D_FF), D_MODEL ** -0.5)
    ffn_w_out = nrm((DEPTH, 2, D_FF, D_MODEL), D_FF ** -0.5)
    rg_w_in = nrm((n_a, D_MODEL, 2 * D_RNN), D_MODEL ** -0.5)
    rg_conv_w = nrm((n_a, CONV_W, D_RNN), CONV_W ** -0.5)
    rg_conv_b = nrm((n_a, D_RNN), 0.02)
    rg_w_a = nrm((n_a, 2, RG_BLOCKS, RG_BLOCK, RG_BLOCK), RG_BLOCK ** -0.5)
    rg_b_a = nrm((n_a, 2, D_RNN), 0.02)
    rg_w_i = nrm((n_a, 2, RG_BLOCKS, RG_BLOCK, RG_BLOCK), RG_BLOCK ** -0.5)
    rg_b_i = nrm((n_a, 2, D_RNN), 0.02)
    a_init = jax.random.uniform(next(ks), (n_a, 2, D_RNN), f32, minval=0.9, maxval=0.999) ** (1.0 / RG_C)
    rg_lambda = jnp.log(a_init) - jnp.log1p(-a_init)
    rg_w_out = nrm((n_a, D_RNN, D_MODEL), D_RNN ** -0.5)
    gla_w_in = nrm((n_b, D_MODEL, GLA_IN), D_MODEL ** -0.5)
    gla_w_g2 = nrm((n_b, 2, GLA_RANK, GLA_QK), GLA_RANK ** -0.5)
    gla_b_g = nrm((n_b, 2, GLA_QK), 0.02)
    gla_norm = 1.0 + nrm((n_b, GLA_V), 0.05)
    gla_w_out = nrm((n_b, GLA_V, D_MODEL), GLA_V ** -0.5)
    final_norm = 1.0 + nrm((D_MODEL,), 0.05)
    return {"x_prompt": x_prompt, "x_sample": x_sample, "c": c, "state_rglru": state_rglru,
            "state_gla": state_gla, "c_ctx": c_ctx, "ada_w": ada_w, "ada_b": ada_b, "norm_g": norm_g,
            "ffn_w_in": ffn_w_in, "ffn_w_out": ffn_w_out, "rg_w_in": rg_w_in, "rg_conv_w": rg_conv_w,
            "rg_conv_b": rg_conv_b, "rg_w_a": rg_w_a, "rg_b_a": rg_b_a, "rg_w_i": rg_w_i, "rg_b_i": rg_b_i,
            "rg_lambda": rg_lambda, "rg_w_out": rg_w_out, "gla_w_in": gla_w_in, "gla_w_g2": gla_w_g2,
            "gla_b_g": gla_b_g, "gla_norm": gla_norm, "gla_w_out": gla_w_out, "final_norm": final_norm}

def reference(x_prompt, x_sample, c, state_rglru, state_gla, c_ctx, ada_w, ada_b, norm_g, ffn_w_in, ffn_w_out,
              rg_w_in, rg_conv_w, rg_conv_b, rg_w_a, rg_b_a, rg_w_i, rg_b_i, rg_lambda, rg_w_out,
              gla_w_in, gla_w_g2, gla_b_g, gla_norm, gla_w_out, final_norm):
    rows = x_sample.shape[1] // GRID_W
    n_prompt = x_prompt.shape[0]
    rg_states, gla_states = [], []
    xp, xs = x_prompt, x_sample
    for i in range(DEPTH):
        mod_p = ada_mod(c_ctx, ada_w[i], ada_b[i])
        mod_s = ada_mod(c, ada_w[i], ada_b[i])
        xp = half_ffn(xp, mod_p, norm_g[i], 0, ffn_w_in[i, 0], ffn_w_out[i, 0])
        xs = half_ffn(xs, mod_s, norm_g[i], 0, ffn_w_in[i, 0], ffn_w_out[i, 0])
        hp = modulated(xp, mod_p, norm_g[i], 1)
        hs = modulated(xs, mod_s, norm_g[i], 1)
        j = i // N_MIXERS
        if i % N_MIXERS == 0:
            rg = (rg_w_in[j], rg_conv_w[j], rg_conv_b[j], rg_w_a[j], rg_b_a[j], rg_w_i[j], rg_b_i[j],
                  rg_lambda[j], rg_w_out[j])
            zero = jnp.zeros((n_prompt, D_RNN), jnp.float32)
            yp, st = rglru_mixer(hp, *rg, zero, zero)
            ys, _ = rglru_mixer(hs, *rg, state_rglru[:, j, 0], state_rglru[:, j, 1])
            rg_states.append(st.astype(x_prompt.dtype))
        else:
            gl = (gla_w_in[j], gla_w_g2[j], gla_b_g[j], gla_norm[j], gla_w_out[j])
            zero = jnp.zeros((n_prompt, GLA_HEADS, GLA_DK, GLA_DV), jnp.float32)
            yp, st = gla_mixer(hp, *gl, zero, zero)
            ys_cm, _ = gla_mixer(to_col_major(hs, rows), *gl, state_gla[:, j, 0], state_gla[:, j, 1])
            ys = from_col_major(ys_cm, rows)
            gla_states.append(st.astype(x_prompt.dtype))
        xp = xp + mod_p[:, :, 5] * yp
        xs = xs + mod_s[:, :, 5] * ys
        xp = half_ffn(xp, mod_p, norm_g[i], 2, ffn_w_in[i, 1], ffn_w_out[i, 1])
        xs = half_ffn(xs, mod_s, norm_g[i], 2, ffn_w_in[i, 1], ffn_w_out[i, 1])
    y_prompt = rms_norm(xp, final_norm)
    y_sample = rms_norm(xs, final_norm)
    new_state_rglru = jnp.stack(rg_states, axis=1)
    new_state_gla = jnp.stack(gla_states, axis=1)
    return (y_prompt, y_sample, new_state_rglru, new_state_gla)


_drawn_inputs = setup_inputs


def setup_inputs(seed=0):
    import zlib

    import numpy as np

    out = dict(_drawn_inputs(seed))
    spreads = {}
    factors = {'state_gla': 6.757, 'rg_b_a': 8.0, 'rg_b_i': 7.551, 'gla_b_g': 5.195, 'gla_norm': 6.323}
    for name, (base, spread) in spreads.items():
        noise = np.random.default_rng([zlib.crc32(name.encode()), seed]).standard_normal(out[name].shape)
        drawn = base * np.exp(spread * noise) if base else spread * noise
        out[name] = __import__('jax').numpy.asarray(drawn.astype(out[name].dtype))
    for name, factor in factors.items():
        out[name] = (out[name] * factor).astype(out[name].dtype)
    return out
```

```python
from contextlib import ExitStack

import numpy as np

import concourse.bass as bass
from concourse import mybir

F32 = mybir.dt.float32
F32R = mybir.dt.float32r
U8 = mybir.dt.uint8
ACT = mybir.ActivationFunctionType
ALU = mybir.AluOpType

P = 128
D = 1024
DC = D // P
TP, TS = 128, 256
T = TP + TS
GROUPS = [(0, TP, 0), (TP, TS, 1)]
GRID_W = 64
ROWS = TS // GRID_W
EPS = 1e-6
N_MOD = 9
DF = 2816
FC = DF // P
DR = 1280
RC = DR // P
CW = 4
HEADS = 4
DV = 256
RANK = 16
TAU = 16.0
QSCALE = float(P) ** -0.5
NT = T // P
LEVELS = [64, 32, 16, 8, 4, 2, 1]
NLEV = len(LEVELS)

XPAD = 1 + TP + 2 + TS + 2
XW = TP + 2 + TS
XGROUPS = [(0, TP, 0), (TP + 2, TS, 1)]
HALF = RC // 2

RING = 4
KH = FC // 2
WMAX = KH * P
PHASES = [("ffn_in0", 2 * FC, DC * P), ("ffn_out0", 2 * DC, WMAX), ("rg_in", 2 * RC, DC * P),
          ("rg_gates", 4, RC * P), ("rg_out", DC, RC * P),
          ("ffn_in1", 2 * FC, DC * P), ("ffn_out1", 2 * DC, WMAX),
          ("ffn_in2", 2 * FC, DC * P), ("ffn_out2", 2 * DC, WMAX),
          ("gla_qk", DC, DC * P), ("gla_v", DC, DC * P), ("gla_r", DC, DC * P), ("gla_out", DC, DC * P),
          ("ffn_in3", 2 * FC, DC * P), ("ffn_out3", 2 * DC, WMAX)]
BASE, WIDTH, COUNT = {}, [], {}
for _name, _n, _w in PHASES:
    assert _n % RING == 0
    BASE[_name], COUNT[_name] = len(WIDTH), _n
    WIDTH += [_w] * _n
BLOCKS = len(WIDTH)

ADA_PER_LAYER = N_MOD * DC
ADA_START, ADA_FFN, ADA_RG, ADA_GATES = 2 * DC, 2 * FC, 2 * RC, [12, 8]
assert ADA_START + 2 * ADA_FFN + ADA_RG + sum(ADA_GATES) == 2 * ADA_PER_LAYER
ADA_RING = 2

SMALL = {}
_at = 0
for _name, _w in [("c", 2 * DC), ("ada_b", 2 * ADA_PER_LAYER), ("norm_g", 6 * DC), ("final_g", DC),
                  ("conv_w", RC * CW), ("conv_b", RC), ("gate_b", 4 * RC), ("lam", 2 * RC), ("h0", 2 * RC),
                  ("gla_b", 2 * HEADS), ("gla_g", DC), ("wz", DC * 2 * RANK), ("ident", P)]:
    SMALL[_name] = (_at, _at + _w)
    _at += _w
SMALL_W = _at


def build(nc, d):
    ctx = ExitStack()

    def sb(name, shape, dt=F32, scope=None):
        return (scope or ctx).enter_context(nc.sbuf_tensor(name, shape, dt))

    def sem(name):
        return ctx.enter_context(nc.semaphore(name))

    with ctx:
        x = sb("x", [P, DC, T])
        raw = sb("raw", [P, RING, WMAX])
        w_hi_sb = sb("w_hi_sb", [P, RING, WMAX], F32R)
        w_lo_sb = sb("w_lo_sb", [P, RING, WMAX], F32R)
        ada_raw = sb("ada_raw", [P, ADA_RING, DC * P])
        small = sb("small", [P, SMALL_W])
        csil = sb("csil", [P, DC, 2])
        mod = sb("mod", [P, 2, ADA_PER_LAYER, 2])
        gain = sb("gain", [P, 6, DC, 2])
        halfgate = sb("halfgate", [P, 4, DC, 2])
        ones = sb("ones", [P, P])
        eps = sb("eps", [P, 1])
        rgc = sb("rgc", [P, 12, 2 * RC])
        rg_state = sb("rg_state", [P, 2, RC])
        tmp_a = sb("tmp_a", [P, 2, XW])
        tmp_b = sb("tmp_b", [P, 2, XW])
        ss = sb("ss", [P, T])
        sq = sb("sq", [P, T])
        rinv = sb("rinv", [P, T])
        hbuf_scope = ExitStack()
        h_hi = sb("h_hi", [P, DC, T], F32R, hbuf_scope)
        h_lo = sb("h_lo", [P, DC, T], F32R, hbuf_scope)
        ffn_scope = ExitStack()
        a_hi = sb("a_hi", [P, FC, T], F32R, ffn_scope)
        a_lo = sb("a_lo", [P, FC, T], F32R, ffn_scope)
        ffn_scope.close()
        rg_scope = ExitStack()
        xc = sb("xc", [P, RC, XW], F32, rg_scope)
        xc_hi = sb("xc_hi", [P, RC, XW], F32R, rg_scope)
        xc_lo = sb("xc_lo", [P, RC, XW], F32R, rg_scope)
        gate = sb("gate", [P, RC, T], F32, rg_scope)
        rg_scope.close()
        gla_scope = ExitStack()
        qk = sb("qk", [P, HEADS, 2, T], F32, gla_scope)
        vt = sb("vt", [P, NT, HEADS * DV], F32, gla_scope)
        sr = sb("sr", [P, DC, T], F32, gla_scope)
        bcum = sb("bcum", [P, HEADS, 2, T], F32, gla_scope)
        ebuf = sb("ebuf", [P, 2, 2, T], F32, gla_scope)
        scores = sb("scores", [P, T], F32, gla_scope)
        qfb = sb("qfb", [P, 2, TS], F32, gla_scope)
        kbar = sb("kbar", [P, 4, P], F32, gla_scope)
        kbar_t = sb("kbar_t", [P, 4, P], F32, gla_scope)
        wg2 = sb("wg2", [2 * RANK, 2, HEADS * P], F32, gla_scope)
        gla_scope.close()
        hbuf_scope.close()
        rgb_scope = ExitStack()
        ga = sb("ga", [P, HALF, XW], F32, rgb_scope)
        gv = sb("gv", [P, HALF, XW], F32, rgb_scope)
        gix = sb("gix", [P, HALF, XW], F32, rgb_scope)
        rgb_scope.close()
        out_scope = ExitStack()
        y_out = sb("y_out", [P, DC, T], F32, out_scope)
        out_scope.close()
        sb("span_all", [P, 2 * DC * T + 2 * FC * T], F32, ctx)
        extra = sb("extra", [P, HALF * XW], F32, ctx)
        xpad = extra[:, 0:2 * XPAD].rearrange("p (a b) -> p a b", a=2)
        yf = extra[:, :].rearrange("p (n t) -> p n t", n=HALF)
        pst = extra[:, 0:2 * DV].rearrange("p (a b) -> p a b", a=2)
        mst = extra[:, 2 * DV:4 * DV].rearrange("p (a b) -> p a b", a=2)
        bl = extra[:, 4 * DV:4 * DV + 8]
        zt = extra[:, 4 * DV + 8:4 * DV + 8 + NT * 2 * RANK].rearrange("p (a b) -> p a b", a=NT)
        zT = extra[0:2 * RANK, 4 * DV + 104:4 * DV + 104 + T]
        masks = sb("masks", [P, NLEV, P], U8, ctx)
        reset = sb("reset", [P, T], F32, ctx)
        wz_hi = sb("wz_hi", [P, DC, 2 * RANK], F32R, ctx)
        wz_lo = sb("wz_lo", [P, DC, 2 * RANK], F32R, ctx)

        bank = [ctx.enter_context(nc.psum_tensor(f"bank{i}", [P, 512], F32)) for i in range(8)]
        ada_ps = [bank[4][:, 0:2 * ADA_PER_LAYER].rearrange("p (j c) -> p j c", c=2),
                  bank[5][:, 0:2 * ADA_PER_LAYER].rearrange("p (j c) -> p j c", c=2)]
        sum_ps = bank[6][:, 0:T]

        def sm(name):
            a, b = SMALL[name]
            return small[:, a:b]

        csm = sm("c").rearrange("p (k c) -> p k c", c=2)
        ada_b = sm("ada_b").rearrange("p (l j) -> p l j", l=2)
        norm_g = sm("norm_g").rearrange("p (n k) -> p n k", k=DC)
        final_g = sm("final_g")
        conv_w = sm("conv_w").rearrange("p (m k) -> p m k", k=CW)
        conv_b = sm("conv_b")
        lam = sm("lam")
        h0 = sm("h0").rearrange("p (d m) -> p d m", d=2)
        gla_b = sm("gla_b").rearrange("p (d h) -> p d h", d=2)
        gla_g = sm("gla_g")
        wz = sm("wz").rearrange("p (k z) -> p k z", k=DC)
        ident = sm("ident")
        hb = rgc[:, 0:2, :]
        cc, cc2, ncc = rgc[:, 2, :], rgc[:, 3, :], rgc[:, 4, :]
        s0 = ada_raw[:, :, :].rearrange("p a b -> p (a b)").rearrange("p (h d v) -> p h d v", h=HEADS, d=2)

        small_loaded = sem("small_loaded")
        masks_loaded = sem("masks_loaded")
        masks_made = sem("masks_made")
        wg2_loaded = sem("wg2_loaded")
        x_loaded = sem("x_loaded")
        s0_loaded = sem("s0_loaded")
        out_done = sem("out_done")
        w_loaded = [sem(f"w_loaded{s}") for s in range(RING)]
        w_hi = sem("w_hi")
        w_split = sem("w_split")
        w_used = sem("w_used")
        drained = sem("drained")
        ada_loaded = [sem(f"ada_loaded{s}") for s in range(ADA_RING)]
        ada_used = sem("ada_used")
        csil_ready = sem("csil_ready")
        consts = sem("consts")
        mods_ready = sem("mods_ready")
        x_ready = sem("x_ready")
        pool_seq = sem("pool_seq")
        dve_seq = sem("dve_seq")
        act_seq = sem("act_seq")
        ss_ready = sem("ss_ready")
        sum_done = sem("sum_done")
        std_ready = sem("std_ready")
        y_ready = sem("y_ready")
        hhi_ready = sem("hhi_ready")
        h_ready = sem("h_ready")
        silu_ready = sem("silu_ready")
        ahi_ready = sem("ahi_ready")
        a_ready = sem("a_ready")
        xpad_ready = sem("xpad_ready")
        conv_done = sem("conv_done")
        xchi_ready = sem("xchi_ready")
        xc_ready = sem("xc_ready")
        gate_done = sem("gate_done")
        gate_drained = sem("gate_drained")
        rg_act = sem("rg_act")
        rg_dve = sem("rg_dve")
        rg_sqrt = sem("rg_sqrt")
        rg_y = sem("rg_y")
        rg_yhi = sem("rg_yhi")
        rg_yready = sem("rg_yready")
        rgc_ready = sem("rgc_ready")
        gelu_ready = sem("gelu_ready")
        z_done = sem("z_done")
        z_copied = sem("z_copied")
        zz_done = sem("zz_done")
        sp_ready = sem("sp_ready")
        zz_drained = sem("zz_drained")
        b_ready = sem("b_ready")
        v_copied = sem("v_copied")
        d_ready = sem("d_ready")
        e_ready = sem("e_ready")
        qkt_ready = sem("qkt_ready")
        s_done = sem("s_done")
        s_drained = sem("s_drained")
        bl_ready = sem("bl_ready")
        ei_ready = sem("ei_ready")
        kbar_ready = sem("kbar_ready")
        kt_done = sem("kt_done")
        kt_copied = sem("kt_copied")
        u_done = sem("u_done")
        u_copied = sem("u_copied")
        st_ready = sem("st_ready")
        o_done = sem("o_done")
        o_copied = sem("o_copied")
        r_copied = sem("r_copied")
        state_out = sem("state_out")
        osum = sem("osum")
        osum_done = sem("osum_done")
        ostd = sem("ostd")
        osr = sem("osr")
        og = sem("og")
        oghi = sem("oghi")
        og_ready = sem("og_ready")

        class Seq:

            def __init__(self, eng, s):
                self.eng, self.s, self.n, self.i, self.per = eng, s, 0, None, 0

            def value(self):
                return self.n if self.i is None else self.i * self.per + self.n

            def mark(self, ins):
                ins.then_inc(self.s, 1)
                self.n += 1

            def wait(self):
                self.eng.wait_ge(self.s, self.value())

            def step(self, ins):
                self.mark(ins)
                self.wait()

        NORMS = [("ffn_in0", 0), ("rg_in", 1), ("ffn_in1", 2), ("ffn_in2", 3), ("gla_qk", 4), ("ffn_in3", 5)]

        def layer_of(q):
            return q // 3, q % 3

        def col_major(ap, q, n):
            if q == 4 and n == TS:
                return ap.rearrange("p (w r) -> p r w", w=GRID_W)
            return ap

        def row_major(ap, q, n):
            if q == 4 and n == TS:
                return ap.rearrange("p (r w) -> p r w", r=ROWS)
            return ap

        block = ctx.enter_context(nc.Block())

        @block.sync
        def _(sp):
            def load_block(src, i, b, n):
                s = b % RING
                sp.dma_start(raw[:, s, 0:src.shape[2]],
                             src[bass.ds(RING * i + b, 1)].rearrange("a p k -> p (a k)")).then_inc(w_loaded[s], 16)

            def load_ada(first, i, b):
                s = b % ADA_RING
                sp.dma_start(ada_raw[:, s, :],
                             d["ada_w"][bass.ds(RING * i + b + first, 1)].rearrange("a p k -> p (a k)")
                             ).then_inc(ada_loaded[s], 16)

            def phase(name, src, ada=None, start=0, end=None):
                base, n = BASE[name], COUNT[name]
                if base == 0:
                    for b in range(RING):
                        load_block(src, 0, b, b)
                        sp.wait_ge(ada_used, ada + b - ADA_RING + 1)
                        load_ada(ada, 0, b)
                    start = 1
                with sp.Fori(start, n // RING if end is None else end) as i:
                    for b in range(RING):
                        sp.wait_ge(w_split, RING * i + (base + b - RING + 1))
                        load_block(src, i, b, None)
                        if ada is not None:
                            sp.wait_ge(ada_used, RING * i + (ada + b - ADA_RING + 1))
                            load_ada(ada, i, b)

            def ada_run(first, n):
                with sp.Fori(0, n // RING) as i:
                    for b in range(RING):
                        sp.wait_ge(ada_used, RING * i + (first + b - ADA_RING + 1))
                        load_ada(first, i, b)

            sp.dma_start(small[:, :], d["small"]).then_inc(small_loaded, 16)
            for b in range(ADA_RING):
                load_ada(0, 0, b)
            sp.dma_start(x[:, :, :], d["x"]).then_inc(x_loaded, 16)
            for b in range(ADA_RING, ADA_START):
                sp.wait_ge(ada_used, b - ADA_RING + 1)
                load_ada(0, 0, b)
            n_ada = ADA_START
            phase("ffn_in0", d["ffn_in"][0], n_ada)
            n_ada += ADA_FFN
            phase("ffn_out0", d["ffn_out"][0])
            phase("rg_in", d["rg_in"], n_ada)
            n_ada += ADA_RG
            phase("rg_gates", d["rg_gates"])
            phase("rg_out", d["rg_out"], end=1)
            for n in ADA_GATES:
                ada_run(n_ada, n)
                n_ada += n
            phase("rg_out", d["rg_out"], start=1)
            phase("ffn_in1", d["ffn_in"][1], n_ada)
            n_ada += ADA_FFN
            sp.wait_ge(ada_used, n_ada)
            sp.dma_start(ada_raw[:, :, :].rearrange("p a b -> p (a b)"), d["s0"]).then_inc(s0_loaded, 16)
            phase("ffn_out1", d["ffn_out"][1])
            phase("ffn_in2", d["ffn_in"][2])
            phase("ffn_out2", d["ffn_out"][2])
            phase("gla_qk", d["gla_qk"])
            phase("gla_v", d["gla_v"])
            phase("gla_r", d["gla_r"])
            phase("gla_out", d["gla_out"])
            phase("ffn_in3", d["ffn_in"][3])
            phase("ffn_out3", d["ffn_out"][3])
            for m in range(DC):
                sp.wait_ge(h_ready, 8 * 6 + m + 1)
                sp.dma_start(d["y"][:, m, :], y_out[:, m, :]).then_inc(out_done, 16)
            sp.wait_ge(out_done, 16 * DC)
            sp.wait_ge(state_out, 16 * (HEADS + 1))

        @block.gpsimd
        def _(pool):
            seq = Seq(pool, pool_seq)
            pool.memset(ones[:, :], 1.0).then_inc(consts, 1)
            pool.memset(eps[:, :], EPS).then_inc(consts, 1)
            pool.memset(reset[:, :], 1.0).then_inc(consts, 1)
            pool.wait_ge(consts, 3)
            pool.memset(reset[:, :].rearrange("p (n t) -> p n t", t=P)[:, :, 0:1], 0.0).then_inc(consts, 1)

            def sum_squares(q):
                if q == 0:
                    pool.wait_ge(x_loaded, 16)
                for m in range(DC):
                    if q:
                        pool.wait_ge(x_ready, DC * (q - 1) + m + 1)
                    if m == 0:
                        if q:
                            pool.wait_ge(sum_done, q)
                        seq.step(nc.gpsimd.tensor_tensor(ss[:, :], x[:, m, :], x[:, m, :], ALU.mult))
                        continue
                    seq.step(nc.gpsimd.tensor_tensor(sq[:, :], x[:, m, :], x[:, m, :], ALU.mult))
                    add = nc.gpsimd.tensor_tensor(ss[:, :], ss[:, :], sq[:, :], ALU.add)
                    if m == DC - 1:
                        add.then_inc(ss_ready, 1)
                    else:
                        seq.step(add)

            for q in range(5):
                sum_squares(q)
            for hd in range(HEADS):
                pool.wait_ge(b_ready, 2 * hd + 2)
                for l, s in enumerate(LEVELS):
                    n = hd * NLEV + l
                    if n >= 2:
                        pn = n - 2
                        pool.wait_ge(s_done, pn // NLEV * (NLEV + 1) + pn % NLEV + 2)
                    f, b = (bcum[:, hd, j, :].rearrange("p (n h s) -> p n h s", h=2, s=s) for j in range(2))
                    eq, ek = (ebuf[:, n % 2, j, :].rearrange("p (n h s) -> p n h s", h=2, s=s) for j in range(2))
                    nb = T // (2 * s)
                    ref_f = f[:, :, 0, s - 1:s].to_broadcast([P, nb, s])
                    ref_b = b[:, :, 1, 0:1].to_broadcast([P, nb, s])
                    nc.gpsimd.tensor_tensor(eq[:, :, 1, :], f[:, :, 1, :], ref_f, ALU.subtract)
                    nc.gpsimd.tensor_tensor(eq[:, :, 0, :], b[:, :, 0, :], ref_b, ALU.subtract)
                    nc.gpsimd.tensor_tensor(ek[:, :, 0, :], ref_f, f[:, :, 0, :], ALU.subtract)
                    nc.gpsimd.tensor_tensor(ek[:, :, 1, :], ref_b, b[:, :, 1, :], ALU.subtract).then_inc(d_ready, 1)
            for hd in range(HEADS):
                pool.wait_ge(o_copied, hd + 1)
                if hd:
                    pool.wait_ge(osum_done, hd)
                nc.gpsimd.tensor_tensor(ss[:, :], qk[:, hd, 0, :], qk[:, hd, 0, :], ALU.mult)
                seq.step(nc.gpsimd.tensor_tensor(sq[:, :], qk[:, hd, 1, :], qk[:, hd, 1, :], ALU.mult))
                nc.gpsimd.tensor_tensor(ss[:, :], ss[:, :], sq[:, :], ALU.add).then_inc(osum, 1)
            for q in (5, 6):
                sum_squares(q)

        @block.tensor
        def _(pe):
            def tile(out, slot, ks, hi, lo, start, stop, at=0):
                for j, k in enumerate(ks):
                    w = slice((at + j) * P, (at + j + 1) * P)
                    pe.matmul(out, w_hi_sb[:, slot, w], hi[k], start=start and j == 0, stop=False)
                    pe.matmul(out, w_hi_sb[:, slot, w], lo[k], start=False, stop=False)
                    last = pe.matmul(out, w_lo_sb[:, slot, w], hi[k], start=False,
                                     stop=stop and j == len(ks) - 1)
                return last

            h_chunks = ([h_hi[:, k, :] for k in range(DC)], [h_lo[:, k, :] for k in range(DC)])
            a_chunks = ([a_hi[:, k, :] for k in range(FC)], [a_lo[:, k, :] for k in range(FC)])
            y_chunks = ([xc_hi[:, k, 0:T] for k in range(RC)], [xc_lo[:, k, 0:T] for k in range(RC)])

            def ada_block(layer, j, b, n):
                s = b % ADA_RING
                pe.wait_ge(ada_loaded[s], n)
                for k in range(DC):
                    last = pe.matmul(ada_ps[layer][:, j, :], ada_raw[:, s, k * P:(k + 1) * P], csil[:, k, :],
                                     start=k == 0, stop=k == DC - 1)
                last.then_inc(ada_used, 1)

            def ada_at(first, i, b):
                layer = first // ADA_PER_LAYER
                j = first - layer * ADA_PER_LAYER + b
                n = 16 * ((first + b) // ADA_RING + 1)
                if i is None:
                    ada_block(layer, slice(j, j + 1), b, n)
                else:
                    ada_block(layer, bass.ds(RING * i + j, 1), b, i * (16 * RING // ADA_RING) + n)

            def norm(q):
                pe.wait_ge(ss_ready, q + 1)
                if q == 0:
                    pe.wait_ge(consts, 1)
                pe.matmul(sum_ps, ones[:, :], ss[:, :], start=True, stop=True).then_inc(sum_done, 1)

            def one_tile_blocks(name, chunks, ks, ada=None, banks=RING, loop=True):
                base, n = BASE[name], COUNT[name]

                def body(i, wait_bank=True):
                    for b in range(RING):
                        off = base + b
                        if wait_bank:
                            pe.wait_ge(drained, (RING * i if i is not None else 0) + (off - banks + 1))
                        pe.wait_ge(w_split, (RING * i if i is not None else 0) + off + 1)
                        tile(bank[b % banks][:, 0:T], b, ks, *chunks, True, True).then_inc(w_used, 1)
                        if ada is not None:
                            ada_at(ada, i, b)

                start = 0
                if base == 0:
                    body(None, wait_bank=False)
                    start = 1
                else:
                    pe.wait_ge(drained, base)
                with pe.Fori(start, n // RING) as i:
                    body(i)

            def ffn_out(name):
                base, n = BASE[name], COUNT[name]
                pe.wait_ge(drained, base)
                with pe.Fori(0, n // RING) as i:
                    for b in range(RING):
                        half, t = b % 2, b // 2
                        if half == 0:
                            pe.wait_ge(drained, RING * i + (base + b - 2))
                        pe.wait_ge(w_split, RING * i + (base + b + 1))
                        tile(bank[t][:, 0:T], b, range(KH * half, KH * half + KH), *a_chunks,
                             half == 0, half == 1).then_inc(w_used, 1)

            def ffn(f, q, ada=None):
                norm(q)
                pe.wait_ge(h_ready, DC * (q + 1))
                one_tile_blocks(f"ffn_in{f}", h_chunks, range(DC), ada)
                pe.wait_ge(a_ready, FC * (f + 1))
                ffn_out(f"ffn_out{f}")

            pe.wait_ge(csil_ready, 1)
            for b in range(ADA_START):
                ada_at(0, None, b) if b < RING else ada_block(0, slice(b, b + 1), b, 16 * (b // ADA_RING + 1))
            n_ada = ADA_START
            ffn(0, 0, n_ada)
            n_ada += ADA_FFN

            norm(1)
            pe.wait_ge(h_ready, DC * 2)
            base = BASE["rg_in"]
            pe.wait_ge(drained, base)
            for i in range(COUNT["rg_in"] // RING):
                for b in range(RING):
                    pe.wait_ge(drained, RING * i + base + b - RING + 1)
                    pe.wait_ge(w_split, RING * i + base + b + 1)
                    tile(bank[b][:, 0:T], b, range(DC), *h_chunks, True, True).then_inc(w_used, 1)
                    j = n_ada + RING * i + b
                    ada_block(j // ADA_PER_LAYER, slice(j % ADA_PER_LAYER, j % ADA_PER_LAYER + 1), j,
                              16 * (j // ADA_RING + 1))
            n_ada += ADA_RG
            base = BASE["rg_gates"]
            pe.wait_ge(drained, base)
            pe.wait_ge(xc_ready, RC)
            for b in range(4):
                pe.wait_ge(w_split, base + b + 1)
                for t in range(RC):
                    g = b * RC + t
                    m = (b // 2) * HALF + t // 2
                    if g >= RING:
                        pe.wait_ge(gate_drained, g - RING + 1)
                    last = tile(bank[g % RING][:, 0:XW], b, [0], [xc_hi[:, m, :]], [xc_lo[:, m, :]], True, True, t)
                    last.then_inc(w_used if t == RC - 1 else gate_done, 1)
            for n in ADA_GATES:
                with pe.Fori(0, n // RING) as i:
                    for b in range(RING):
                        ada_at(n_ada, i, b)
                n_ada += n
            pe.wait_ge(rg_yready, 2)
            one_tile_blocks("rg_out", y_chunks, range(RC))

            ffn(1, 2, n_ada)
            ffn(2, 3)

            norm(4)
            pe.wait_ge(h_ready, DC * 5)
            pe.wait_ge(drained, BASE["gla_qk"])
            for t in range(NT):
                out = bank[4][:, t * 2 * RANK:(t + 1) * 2 * RANK]
                tok = slice(t * P, (t + 1) * P)
                for k in range(DC):
                    pe.matmul(out, h_hi[:, k, tok], wz_hi[:, k, :], start=k == 0, stop=False)
                    pe.matmul(out, h_hi[:, k, tok], wz_lo[:, k, :], start=False, stop=False)
                    last = pe.matmul(out, h_lo[:, k, tok], wz_hi[:, k, :], start=False, stop=k == DC - 1)
            last.then_inc(z_done, 1)
            pe.wait_ge(z_copied, 1)
            for t in range(NT):
                last = pe.transpose(bank[5][0:2 * RANK, t * P:(t + 1) * P], zt[:, t, :], ident)
            last.then_inc(z_done, 1)
            pe.wait_ge(z_copied, 2)
            pe.wait_ge(wg2_loaded, 16)
            base = BASE["gla_qk"]

            def zz(u):
                hd, dr = u // 2, u % 2
                if u >= 2:
                    pe.wait_ge(zz_drained, u - 1)
                pe.matmul(bank[4 + u % 2][:, 0:T], wg2[:, dr, hd * P:(hd + 1) * P], zT, start=True,
                          stop=True).then_inc(zz_done, 1)

            zz(0)
            for b in range(DC):
                if b + 1 < DC:
                    zz(b + 1)
                pe.wait_ge(drained, max(base + b - RING + 1, base))
                pe.wait_ge(w_split, base + b + 1)
                tile(bank[b % RING][:, 0:T], b % RING, range(DC), *h_chunks, True, True).then_inc(w_used, 1)
            base = BASE["gla_v"]
            v_banks = [0, 1, 2, 3, 6, 7]
            pe.wait_ge(drained, base)
            for b in range(DC):
                pe.wait_ge(w_split, base + b + 1)
                s = b % RING
                for t in range(NT):
                    tok = slice(t * P, (t + 1) * P)
                    for half in range(2):
                        out = bank[v_banks[2 * t + half]][:, :]
                        c = slice(512 * half, 512 * half + 512)
                        pe.matmul(out, h_hi[:, b, tok], w_hi_sb[:, s, c], start=b == 0, stop=False)
                        pe.matmul(out, h_hi[:, b, tok], w_lo_sb[:, s, c], start=False, stop=False)
                        last = pe.matmul(out, h_lo[:, b, tok], w_hi_sb[:, s, c], start=False, stop=b == DC - 1)
                last.then_inc(w_used, 1)
            pe.wait_ge(drained, BASE["gla_r"])
            pe.wait_ge(s0_loaded, 16)
            for hd in range(HEADS):
                for l in range(NLEV + 1):
                    n = hd * (NLEV + 1) + l
                    if n >= 2:
                        pe.wait_ge(s_drained, n - 1)
                    else:
                        pe.wait_ge(zz_drained, 2 * HEADS)
                    if l:
                        pe.wait_ge(qkt_ready, hd * NLEV + l)
                        e = ebuf[:, (hd * NLEV + l - 1) % 2, :, :]
                    else:
                        e = qk[:, hd, :, :]
                    for t in range(NT):
                        tok = slice(t * P, (t + 1) * P)
                        last = pe.matmul(bank[4 + n % 2][:, tok], e[:, 1, tok], e[:, 0, tok], start=True, stop=True)
                    last.then_inc(s_done, 1)
                    if l == 3:
                        for b in (2 * hd, 2 * hd + 1):
                            nb = BASE["gla_r"] + b
                            pe.wait_ge(drained, max(nb - 1, BASE["gla_r"]))
                            pe.wait_ge(w_split, nb + 1)
                            tile(bank[b % 2][:, 0:T], b % RING, range(DC), *h_chunks, True, True).then_inc(w_used, 1)
                pe.wait_ge(kbar_ready, hd + 1)
                if hd:
                    pe.wait_ge(st_ready, hd)
                for j in range(4):
                    last = pe.transpose(bank[2][:, j * P:(j + 1) * P], kbar[:, j, :], ident)
                last.then_inc(kt_done, 1)
                pe.wait_ge(kt_copied, hd + 1)
                if hd:
                    pe.wait_ge(u_copied, hd)
                for j, t in enumerate((0, 0, 1, 2)):
                    last = pe.matmul(bank[3 - j // 2][:, (j % 2) * DV:(j % 2 + 1) * DV], kbar_t[:, j, :],
                                     vt[:, t, hd * DV:(hd + 1) * DV], start=True, stop=True)
                last.then_inc(u_done, 1)
                pe.wait_ge(st_ready, hd + 1)
                pe.wait_ge(s_drained, (hd + 1) * (NLEV + 1))
                if hd:
                    pe.wait_ge(o_copied, hd)
                for c in range(2):
                    vc = slice(hd * DV + c * P, hd * DV + (c + 1) * P)
                    cc_ = slice(c * P, (c + 1) * P)
                    for t in range(NT):
                        tok = slice(t * P, (t + 1) * P)
                        out = bank[6 + c][:, tok]
                        last = pe.matmul(out, vt[:, t, vc], scores[:, tok], start=True, stop=t == 0)
                        if t:
                            stok = slice((t - 1) * P, t * P)
                            sf = s0[:, hd, 0, cc_] if t == 1 else mst[:, 0, cc_]
                            sbk = s0[:, hd, 1, cc_] if t == 2 else mst[:, 1, cc_]
                            pe.matmul(out, sf, qfb[:, 0, stok], start=False, stop=False)
                            last = pe.matmul(out, sbk, qfb[:, 1, stok], start=False, stop=True)
                last.then_inc(o_done, 1)
            for hd in range(HEADS):
                pe.wait_ge(osum, hd + 1)
                if hd == 0:
                    pe.wait_ge(u_copied, HEADS)
                    pe.wait_ge(drained, BASE["gla_out"])
                pe.matmul(bank[hd][:, 0:T], ones[:, :], ss[:, :], start=True, stop=True).then_inc(osum_done, 1)
            pe.wait_ge(og_ready, DC)
            one_tile_blocks("gla_out", h_chunks, range(DC))

            norm(5)
            pe.wait_ge(h_ready, DC * 6)
            one_tile_blocks("ffn_in3", h_chunks, range(DC))
            pe.wait_ge(a_ready, FC * 4)
            ffn_out("ffn_out3")
            norm(6)

        @block.scalar
        def _(act):
            A = nc.scalar.activation
            seq = Seq(act, act_seq)

            def hi_of(n, i=None, per=0):
                s = n % RING
                off = 0 if i is None else i
                act.wait_ge(w_loaded[s], off * 16 + 16 * (n // RING + 1))
                if i is not None or n >= RING:
                    act.wait_ge(w_used, off * RING + (n - RING + 1))
                w = WIDTH[n]
                A(w_hi_sb[:, s, 0:w], raw[:, s, 0:w], ACT.Copy).then_inc(w_hi, 1)

            def ahead(n):
                if n + 2 < BLOCKS:
                    hi_of(n + 2)

            def norm(q):
                act.wait_ge(sum_done, q + 1)
                if q == 0:
                    act.wait_ge(consts, 2)
                A(rinv[:, :], sum_ps, ACT.Sqrt, bias=eps[:, :], scale=1.0 / D).then_inc(std_ready, 1)
                if q == 6:
                    return
                layer, j = layer_of(q)
                for m in range(DC):
                    act.wait_ge(y_ready, DC * q + m + 1)
                    for t0, n, g in GROUPS:
                        shift = mod[:, layer, 3 * j * DC + m, g:g + 1]
                        last = A(col_major(h_hi[:, m, t0:t0 + n], q, n), row_major(tmp_a[:, m % 2, t0:t0 + n], q, n),
                                 ACT.Identity, bias=shift)
                    last.then_inc(hhi_ready, 1)

            def ffn_in(f):
                base = BASE[f"ffn_in{f}"]

                def pair(i, p, peeled):
                    off = 0 if i is None else i
                    act.wait_ge(w_used, off * RING + (base + 2 * p + 1))
                    A(tmp_b[:, p % 2, 0:T], bank[(2 * p) % RING][:, 0:T], ACT.Silu).then_inc(silu_ready, 1)

                def round_pair(i, p):
                    off = 0 if i is None else i
                    act.wait_ge(drained, off * RING + (base + 2 * p + 2))
                    act.wait_ge(consts, 1)
                    out = a_hi[:, p, :] if i is None else a_hi[:, bass.ds(i * 2 + p, 1), :].rearrange("p a t -> p (a t)")
                    A(out, tmp_a[:, p % 2, 0:T], ACT.Copy).then_inc(ahi_ready, 1)

                def turn(i, last):
                    for p in range(2):
                        if last:
                            ahead(base + 2 * (FC - 2 + p))
                        else:
                            hi_of(base + 2 * p + 2, i)
                        ii, pp = (None, FC - 2 + p) if last else (i, p)
                        pair(ii, pp, False)
                        if last:
                            ahead(base + 2 * (FC - 2 + p) + 1)
                        else:
                            hi_of(base + 2 * p + 3, i)
                        round_pair(ii, pp)

                start = 0
                if base == 0:
                    for p in range(2):
                        hi_of(2 * p + 2)
                        pair(None, p, True)
                        hi_of(2 * p + 3)
                        round_pair(None, p)
                    start = 1
                with act.Fori(start, FC // 2 - 1) as i:
                    turn(i, False)
                turn(None, True)

            def only_weights(name):
                for b in range(COUNT[name]):
                    ahead(BASE[name] + b)

            act.wait_ge(small_loaded, 16)
            A(csil[:, :, :], csm, ACT.Silu).then_inc(csil_ready, 1)
            hi_of(0)
            hi_of(1)
            A(wz_hi[:, :, :], wz, ACT.Copy).then_inc(csil_ready, 1)
            act.dma_start(extra[:, 0:NLEV * P], d["masks"]).then_inc(masks_loaded, 16)
            act.wait_ge(masks_loaded, 16)
            A(masks[:, :, :], extra[:, 0:NLEV * P].rearrange("p (a b) -> p a b", a=NLEV), ACT.Copy).then_inc(masks_made, 1)
            A(rgc[:, 5, :], lam, ACT.Abs).then_inc(act_seq, 1)
            seq.n += 1
            seq.wait()
            A(rgc[:, 6, :], rgc[:, 5, :], ACT.Exp, scale=-1.0).then_inc(rgc_ready, 1)
            act.wait_ge(rgc_ready, 2)
            A(rgc[:, 8, :], rgc[:, 7, :], ACT.Ln).then_inc(rgc_ready, 1)

            norm(0)
            ffn_in(0)
            only_weights("ffn_out0")

            norm(1)
            base = BASE["rg_in"]
            for b in range(2 * RC):
                m = b // 2
                ahead(base + b)
                if b % 2 == 0:
                    act.wait_ge(w_used, base + b + 1)
                    if m >= 2:
                        act.wait_ge(conv_done, m - 1)
                    for (t0, n, _), at in zip(GROUPS, (1, 1 + TP + 2)):
                        last = A(xpad[:, m % 2, at:at + n], bank[b % RING][:, t0:t0 + n], ACT.Copy)
                    last.then_inc(xpad_ready, 1)
                else:
                    act.wait_ge(conv_done, m + 1)
                    A(xc_hi[:, m, :], xc[:, m, :], ACT.Copy).then_inc(xchi_ready, 1)
            act.wait_ge(drained, BASE["rg_gates"])
            A(gate[:, :, :], gate[:, :, :], ACT.Gelu_apprx_tanh).then_inc(gelu_ready, 1)
            base = BASE["rg_gates"]
            act.wait_ge(rgc_ready, 4)
            for b in range(4):
                half, dr = b // 2, b % 2
                ahead(base + b)
                for n in range(HALF):
                    m = half * HALF + n
                    col = slice(dr * RC + m, dr * RC + m + 1)
                    c = b * HALF + n
                    if c >= 2:
                        act.wait_ge(rg_dve, c - 1)
                    for kind, out in ((0, tmp_a[:, c % 2, :]), (1, gix[:, n, :])):
                        g = b * RC + 2 * n + kind
                        if g % RC == RC - 1:
                            act.wait_ge(w_used, base + b + 1)
                        else:
                            act.wait_ge(gate_done, g - b + 1)
                        if b and n == 0 and kind == 0:
                            act.wait_ge(rg_y, b)
                        A(out, bank[g % RING][:, 0:XW], ACT.Tanh, bias=rgc[:, kind, col],
                          scale=0.5).then_inc(gate_drained, 1)
                    act.wait_ge(gate_drained, b * RC + 2 * n + 1)
                    A(ga[:, n, :], tmp_a[:, c % 2, :], ACT.Exp, bias=rgc[:, 2, col], scale=rgc[:, 2, col])
                    A(gv[:, n, :], tmp_a[:, c % 2, :], ACT.Exp, bias=rgc[:, 3, col], scale=rgc[:, 3, col])
                    A(tmp_b[:, c % 2, :], tmp_a[:, c % 2, :], ACT.Tanh, bias=rgc[:, 4, col],
                      scale=rgc[:, 4, col]).then_inc(rg_act, 1)
                act.wait_ge(rg_dve, (b + 1) * HALF)
                A(gv[:, :, :], gv[:, :, :], ACT.Sqrt, scale=0.25).then_inc(rg_sqrt, 1)
                if dr == 1:
                    act.wait_ge(rg_y, b + 1)
                    mm = slice(half * HALF, (half + 1) * HALF)
                    A(xc_hi[:, mm, 0:T], gate[:, mm, :], ACT.Copy).then_inc(rg_yhi, 1)
            act.wait_ge(rg_y, 4)
            act.dma_start(d["rg_state"], rg_state[:, :, :]).then_inc(state_out, 16)
            only_weights("rg_out")

            norm(2)
            ffn_in(1)
            only_weights("ffn_out1")
            norm(3)
            ffn_in(2)
            only_weights("ffn_out2")

            norm(4)
            act.wait_ge(x_ready, 4 * DC)
            act.dma_start(wg2[:, :, :], d["wg2"]).then_inc(wg2_loaded, 16)
            act.wait_ge(z_done, 1)
            A(zt[:, :, :], bank[4][:, 0:NT * 2 * RANK].rearrange("p (a b) -> p a b", a=NT), ACT.Copy).then_inc(z_copied, 1)
            act.wait_ge(z_done, 2)
            A(zT, bank[5][0:2 * RANK, 0:T], ACT.Copy).then_inc(z_copied, 1)
            nc.scalar.preload_act_table_set("natural_log_exp_and_others")
            for b in range(DC):
                ahead(BASE["gla_qk"] + b)
                hd, dr = b // 2, b % 2
                act.wait_ge(zz_done, b + 1)
                if b >= 2:
                    act.wait_ge(b_ready, b - 1)
                t = tmp_a[:, b % 2, 0:T]
                seq.step(A(t, bank[4 + b % 2][:, 0:T], ACT.Abs, bias=gla_b[:, dr, hd:hd + 1]))
                seq.step(A(t, t, ACT.Exp, scale=-1.0))
                A(t, t, ACT.Ln, bias=1.0).then_inc(sp_ready, 1)
            only_weights("gla_v")
            act.wait_ge(w_used, BASE["gla_r"])
            for j, bk in enumerate([0, 1, 2, 3, 6, 7]):
                last = A(vt[:, j // 2, 512 * (j % 2):512 * (j % 2) + 512], bank[bk][:, :], ACT.Copy)
            last.then_inc(v_copied, 1)
            for hd in range(HEADS):
                for l in range(NLEV):
                    n = hd * NLEV + l
                    act.wait_ge(d_ready, n + 1)
                    e = ebuf[:, n % 2, :, :]
                    A(e, e, ACT.Exp, scale=1.0 / TAU).then_inc(e_ready, 1)
                    if l in (2, 4):
                        ahead(BASE["gla_r"] + 2 * hd + l // 2 - 1)
                    if l == 6:
                        for b in (2 * hd, 2 * hd + 1):
                            act.wait_ge(w_used, BASE["gla_r"] + b + 1)
                            A(sr[:, b, :], bank[b % 2][:, 0:T], ACT.Copy).then_inc(r_copied, 1)
                act.wait_ge(bl_ready, hd + 1)
                if hd:
                    act.wait_ge(o_done, hd)
                for j in range(2):
                    A(qfb[:, j, :], bcum[:, hd, j, TP:T], ACT.Exp, scale=1.0 / TAU)
                for j, (t, dr) in enumerate(((0, 0), (0, 1), (1, 0), (2, 1))):
                    A(kbar[:, j, :], bcum[:, hd, dr, t * P:(t + 1) * P], ACT.Exp, bias=bl[:, j:j + 1],
                      scale=-1.0 / TAU)
                A(bl[:, 4:6], bl[:, 2:4], ACT.Exp).then_inc(ei_ready, 1)
                act.wait_ge(kt_done, hd + 1)
                A(kbar_t[:, :, :], bank[2][:, :].rearrange("p (a b) -> p a b", a=4), ACT.Copy).then_inc(kt_copied, 1)
                act.wait_ge(u_done, hd + 1)
                if hd:
                    act.wait_ge(state_out, 16 * (hd + 1))
                A(pst[:, :, :], bank[3][:, :].rearrange("p (a b) -> p a b", a=2), ACT.Copy).then_inc(u_copied, 1)
                act.wait_ge(u_copied, hd + 1)
                act.dma_start(d["gla_state"][hd], pst[:, :, :]).then_inc(state_out, 16)
                act.wait_ge(o_done, hd + 1)
                for c in range(2):
                    last = A(qk[:, hd, c, :], bank[6 + c][:, 0:T], ACT.Copy)
                last.then_inc(o_copied, 1)
            for hd in range(HEADS):
                act.wait_ge(osum_done, hd + 1)
                A(bcum[:, hd, 0, :], bank[hd][:, 0:T], ACT.Sqrt, bias=eps[:, :], scale=1.0 / DV).then_inc(ostd, 1)
            act.wait_ge(r_copied, DC)
            A(sr[:, :, :], sr[:, :, :], ACT.Silu).then_inc(osr, 1)
            for m in range(DC):
                act.wait_ge(og, m + 1)
                A(h_hi[:, m, :], sr[:, m, :], ACT.Copy).then_inc(oghi, 1)
            only_weights("gla_out")

            norm(5)
            ffn_in(3)
            only_weights("ffn_out3")
            norm(6)

        @block.vector
        def _(dve):
            V = nc.vector
            seq = Seq(dve, dve_seq)

            def lo_of(n, i=None):
                s = n % RING
                off = 0 if i is None else i
                w = WIDTH[n]
                dve.wait_ge(w_hi, off * RING + (n + 1))
                V.tensor_tensor(w_lo_sb[:, s, 0:w], raw[:, s, 0:w], w_hi_sb[:, s, 0:w].bitcast(F32),
                                ALU.subtract).then_inc(w_split, 1)

            def ahead(n):
                if n + 2 < BLOCKS:
                    lo_of(n + 2)

            def take_mods(layer, j0, j1, n):
                dve.wait_ge(ada_used, n)
                bias = ada_b[:, layer, j0:j1].rearrange("p (j a) -> p j a", a=1).to_broadcast([P, j1 - j0, 2])
                seq.step(V.tensor_tensor(mod[:, layer, j0:j1, :], ada_ps[layer][:, j0:j1, :], bias, ALU.add))

            def make_gain(q):
                layer, j = layer_of(q)
                g = norm_g[:, q, :].rearrange("p (k a) -> p k a", a=1).to_broadcast([P, DC, 2])
                seq.step(V.scalar_tensor_tensor(gain[:, q, :, :], mod[:, layer, (3 * j + 1) * DC:(3 * j + 2) * DC, :],
                                                1.0, g, ALU.add, ALU.mult))

            def make_halfgate(f):
                layer, j = f // 2, 2 * (f % 2)
                seq.step(V.tensor_scalar(halfgate[:, f, :, :], mod[:, layer, (3 * j + 2) * DC:(3 * j + 3) * DC, :],
                                         0.5, None, ALU.mult))

            def norm(q):
                dve.wait_ge(std_ready, q + 1)
                seq.step(V.reciprocal(rinv[:, :], rinv[:, :]))
                if q == 6:
                    for m in range(DC):
                        V.scalar_tensor_tensor(y_out[:, m, :], x[:, m, :], final_g[:, m:m + 1], rinv[:, :],
                                               ALU.mult, ALU.mult).then_inc(h_ready, 1)
                    return
                layer, j = layer_of(q)

                def scaled(m):
                    for t0, n, g in GROUPS:
                        last = V.scalar_tensor_tensor(tmp_a[:, m % 2, t0:t0 + n], x[:, m, t0:t0 + n],
                                                      gain[:, q, m, g:g + 1], rinv[:, t0:t0 + n], ALU.mult, ALU.mult)
                    last.then_inc(y_ready, 1)

                def low(m):
                    dve.wait_ge(hhi_ready, DC * q + m + 1)
                    for t0, n, g in GROUPS:
                        shift = mod[:, layer, 3 * j * DC + m, g:g + 1]
                        last = V.scalar_tensor_tensor(col_major(h_lo[:, m, t0:t0 + n], q, n),
                                                      row_major(tmp_a[:, m % 2, t0:t0 + n], q, n), shift,
                                                      col_major(h_hi[:, m, t0:t0 + n].bitcast(F32), q, n),
                                                      ALU.add, ALU.subtract)
                    last.then_inc(h_ready, 1)

                scaled(0)
                for m in range(DC):
                    if m + 1 < DC:
                        if m:
                            dve.wait_ge(h_ready, DC * q + m)
                        scaled(m + 1)
                    low(m)

            def ffn_in(f):
                base = BASE[f"ffn_in{f}"]

                def pair(i, p):
                    off = 0 if i is None else i
                    dve.wait_ge(silu_ready, off * 2 + (FC * f + p + 1))
                    dve.wait_ge(w_used, off * RING + (base + 2 * p + 2))
                    dve.wait_ge(w_split, off * RING + min(base + 2 * p + 4, BLOCKS))
                    V.tensor_tensor(tmp_a[:, p % 2, 0:T], tmp_b[:, p % 2, 0:T], bank[(2 * p + 1) % RING][:, 0:T],
                                    ALU.mult).then_inc(drained, 2)

                def low_pair(i, p):
                    off = 0 if i is None else i
                    dve.wait_ge(ahi_ready, off * 2 + (FC * f + p + 1))
                    at = slice(p, p + 1) if i is None else bass.ds(i * 2 + p, 1)
                    lo, hi = (b[:, at, :].rearrange("p a t -> p (a t)") for b in (a_lo, a_hi))
                    V.tensor_tensor(lo, tmp_a[:, p % 2, 0:T], hi.bitcast(F32), ALU.subtract).then_inc(a_ready, 1)

                def turn(i, last):
                    for p in range(2):
                        ii, pp = (None, FC - 2 + p) if last else (i, p)
                        if last:
                            ahead(base + 2 * pp)
                            ahead(base + 2 * pp + 1)
                        else:
                            lo_of(base + 2 * p + 2, i)
                            lo_of(base + 2 * p + 3, i)
                        pair(ii, pp)
                        low_pair(ii, pp)

                with dve.Fori(0, FC // 2 - 1) as i:
                    turn(i, False)
                turn(None, True)

            def update_x(m, q, bk, scale_of):
                for t0, n, g in GROUPS:
                    last = V.scalar_tensor_tensor(row_major(x[:, m, t0:t0 + n], q, n),
                                                  col_major(bank[bk][:, t0:t0 + n], q, n), scale_of(m, g),
                                                  row_major(x[:, m, t0:t0 + n], q, n), ALU.mult, ALU.add)
                last.then_inc(x_ready, 1)

            def ffn_out(f):
                base = BASE[f"ffn_out{f}"]
                for b in range(2 * DC):
                    ahead(base + b)
                    if b % 2:
                        m = b // 2
                        dve.wait_ge(w_used, base + b + 1)
                        update_x(m, None, m % 2, lambda m, g: halfgate[:, f, m, g:g + 1])
                        n_x[0] += 1
                        dve.wait_ge(x_ready, n_x[0])
                        V.sem_inc(drained, 2)

            def mixer_out(name, layer, q):
                base = BASE[name]
                for b in range(DC):
                    ahead(base + b)
                    dve.wait_ge(w_used, base + b + 1)
                    update_x(b, q, b % RING, lambda m, g: mod[:, layer, 5 * DC + m, g:g + 1])
                    n_x[0] += 1
                    dve.wait_ge(x_ready, n_x[0])
                    V.sem_inc(drained, 1)

            n_x = [0]
            dve.wait_ge(small_loaded, 16)
            dve.wait_ge(rgc_ready, 1)
            V.tensor_scalar(rgc[:, 7, :], rgc[:, 6, :], 1.0, None, ALU.add).then_inc(rgc_ready, 1)
            lo_of(0)
            lo_of(1)
            dve.wait_ge(csil_ready, 2)
            seq.step(V.tensor_tensor(wz_lo[:, :, :], wz, wz_hi[:, :, :].bitcast(F32), ALU.subtract))
            dve.wait_ge(rgc_ready, 3)
            seq.step(V.tensor_scalar(rgc[:, 9, :], rgc[:, 7, :], -1.0, None, ALU.add))
            seq.step(V.tensor_tensor(rgc[:, 9, :], rgc[:, 6, :], rgc[:, 9, :], ALU.subtract))
            seq.step(V.reciprocal(rgc[:, 10, :], rgc[:, 7, :]))
            seq.step(V.tensor_tensor(rgc[:, 9, :], rgc[:, 9, :], rgc[:, 10, :], ALU.mult))
            seq.step(V.tensor_tensor(rgc[:, 9, :], rgc[:, 9, :], rgc[:, 8, :], ALU.add))
            seq.step(V.tensor_scalar(rgc[:, 11, :], lam, -1.0, 0.0, ALU.mult, ALU.max))
            seq.step(V.tensor_tensor(rgc[:, 9, :], rgc[:, 9, :], rgc[:, 11, :], ALU.add))
            seq.step(V.tensor_scalar(rgc[:, 2, :], rgc[:, 9, :], -4.0, None, ALU.mult))
            V.tensor_scalar(rgc[:, 3, :], rgc[:, 9, :], -8.0, None, ALU.mult)
            V.tensor_scalar(rgc[:, 4, :], rgc[:, 9, :], 4.0, None, ALU.mult)
            V.tensor_scalar(rgc[:, 0:2, :], sm("gate_b").rearrange("p (a b) -> p a b", a=2), 0.5, None,
                            ALU.mult).then_inc(rgc_ready, 1)

            take_mods(0, 0, ADA_START, ADA_START)
            make_gain(0)
            norm(0)
            ffn_in(0)
            n_ada = ADA_START + ADA_FFN
            take_mods(0, ADA_START, n_ada, n_ada)
            make_halfgate(0)
            make_gain(1)
            ffn_out(0)

            for j in range(2):
                last = V.memset(xpad[:, j, :], 0.0)
            seq.step(last)
            norm(1)
            base = BASE["rg_in"]
            for b in range(2 * RC):
                m = b // 2
                ahead(base + b)
                if b % 2 == 0:
                    dve.wait_ge(xpad_ready, m + 1)
                    xr = xpad[:, m % 2, :]
                    seq.step(V.tensor_scalar(xc[:, m, :], xr[:, 0:XW], conv_w[:, m, 0:1], conv_b[:, m:m + 1],
                                             ALU.mult, ALU.add))
                    for k in range(1, CW):
                        ins = V.scalar_tensor_tensor(xc[:, m, :], xr[:, k:k + XW], conv_w[:, m, k:k + 1],
                                                     xc[:, m, :], ALU.mult, ALU.add)
                        if k < CW - 1:
                            seq.step(ins)
                        else:
                            ins.then_inc(conv_done, 1)
                    V.sem_inc(drained, 1)
                else:
                    dve.wait_ge(w_used, base + b + 1)
                    V.tensor_copy(gate[:, m, :], bank[b % RING][:, 0:T]).then_inc(drained, 1)
                    dve.wait_ge(xchi_ready, m + 1)
                    V.tensor_tensor(xc_lo[:, m, :], xc[:, m, :], xc_hi[:, m, :].bitcast(F32),
                                    ALU.subtract).then_inc(xc_ready, 1)
            base = BASE["rg_gates"]
            for b in range(4):
                half, dr = b // 2, b % 2
                ahead(base + b)
                for n in range(HALF):
                    m = half * HALF + n
                    c = b * HALF + n
                    dve.wait_ge(rg_act, c + 1)
                    V.scalar_tensor_tensor(gix[:, n, :], gix[:, n, :], 1.0, xc[:, m, :], ALU.add, ALU.mult)
                    V.scalar_tensor_tensor(gv[:, n, :], gv[:, n, :], 1.0, tmp_b[:, c % 2, :], ALU.add,
                                           ALU.mult).then_inc(rg_dve, 1)
                dve.wait_ge(rg_sqrt, b + 1)
                seq.step(V.tensor_tensor(gix[:, :, :], gix[:, :, :], gv[:, :, :], ALU.mult))
                for n in range(HALF):
                    m = half * HALF + n
                    for t0, w, g in XGROUPS:
                        ini = 0.0 if g == 0 else h0[:, dr, m:m + 1]
                        if dr == 0:
                            sl = slice(t0, t0 + w)
                            out = yf[:, n, sl]
                        else:
                            sl = slice(t0 + w - 1, t0 - 1 if t0 else None, -1)
                            out = gv[:, n, sl]
                        last = V.tensor_tensor_scan(out, ga[:, n, sl], gix[:, n, sl], ini, ALU.mult, ALU.add)
                seq.step(last)
                mm = slice(half * HALF, (half + 1) * HALF)
                src = yf[:, :, TP - 1] if dr == 0 else gv[:, :, 0]
                cp = V.tensor_copy(rg_state[:, dr, mm], src)
                if dr == 0:
                    cp.then_inc(rg_y, 1)
                    continue
                seq.step(cp)
                if half == 0:
                    dve.wait_ge(gelu_ready, 1)
                for t0, w, g in XGROUPS:
                    last = V.tensor_tensor(yf[:, :, t0:t0 + w], yf[:, :, t0:t0 + w], gv[:, :, t0:t0 + w], ALU.add)
                seq.step(last)
                for (t0, w, g), c0 in zip(XGROUPS, (0, TP)):
                    last = V.tensor_tensor(gate[:, mm, c0:c0 + w], yf[:, :, t0:t0 + w], gate[:, mm, c0:c0 + w],
                                           ALU.mult)
                last.then_inc(rg_y, 1)
                dve.wait_ge(rg_yhi, half + 1)
                V.tensor_tensor(xc_lo[:, mm, 0:T], gate[:, mm, :], xc_hi[:, mm, 0:T].bitcast(F32),
                                ALU.subtract).then_inc(rg_yready, 1)
            V.sem_inc(drained, 4)
            n_ada = ADA_PER_LAYER
            take_mods(0, ADA_START + ADA_FFN, ADA_PER_LAYER, n_ada)
            make_gain(2)
            make_halfgate(1)
            mixer_out("rg_out", 0, 1)

            norm(2)
            ffn_in(1)
            take_mods(1, 0, ADA_PER_LAYER, 2 * ADA_PER_LAYER)
            for q in (3, 4, 5):
                make_gain(q)
            make_halfgate(2)
            make_halfgate(3)
            ffn_out(1)
            norm(3)
            ffn_in(2)
            ffn_out(2)

            norm(4)
            dve.wait_ge(consts, 4)
            for b in range(DC):
                ahead(BASE["gla_qk"] + b)
                hd, dr = b // 2, b % 2
                dve.wait_ge(sp_ready, b + 1)
                lg = tmp_b[:, b % 2, 0:T]
                ins = V.tensor_scalar(lg, bank[4 + b % 2][:, 0:T], gla_b[:, dr, hd:hd + 1], 0.0, ALU.add, ALU.min)
                ins.then_inc(zz_drained, 1)
                dve.wait_ge(zz_drained, b + 1)
                seq.step(V.tensor_tensor(lg, lg, tmp_a[:, b % 2, 0:T], ALU.subtract))
                back = slice(None, None, -1) if dr else slice(None)
                V.tensor_tensor_scan(bcum[:, hd, dr, back], reset[:, :], lg[:, back], 0.0, ALU.mult,
                                     ALU.add).then_inc(b_ready, 1)
                dve.wait_ge(w_used, BASE["gla_qk"] + b + 1)
                V.tensor_scalar(qk[:, b % HEADS, b // HEADS, :], bank[b % RING][:, 0:T],
                                QSCALE if b < HEADS else 1.0, None, ALU.mult).then_inc(drained, 1)
            for b in range(DC):
                ahead(BASE["gla_v"] + b)
            dve.wait_ge(v_copied, 1)
            V.sem_inc(drained, DC)
            dve.wait_ge(masks_made, 1)
            dve.wait_ge(s0_loaded, 16)
            for hd in range(HEADS):
                if hd:
                    dve.wait_ge(st_ready, hd)
                for j, (dr, t) in enumerate(((0, P - 1), (1, 0), (0, 2 * P - 1), (1, 2 * P))):
                    last = V.tensor_scalar(bl[:, j:j + 1], bcum[:, hd, dr, t:t + 1], 1.0 / TAU, None, ALU.mult)
                last.then_inc(bl_ready, 1)

                def merge(l):
                    n = hd * (NLEV + 1) + l
                    dve.wait_ge(s_done, n + 1)
                    ps = bank[4 + n % 2][:, 0:T]
                    if l == 0:
                        if hd:
                            dve.wait_ge(o_done, hd)
                        V.tensor_scalar(scores[:, :], ps, 2.0, None, ALU.mult).then_inc(s_drained, 1)
                    else:
                        dve.wait_ge(s_drained, n)
                        mask = masks[:, l - 1:l, :].to_broadcast([P, NT, P])
                        V.copy_predicated(scores[:, :].rearrange("p (a b) -> p a b", a=NT), mask,
                                          ps.rearrange("p (a b) -> p a b", a=NT)).then_inc(s_drained, 1)

                for l in range(NLEV):
                    n = hd * NLEV + l
                    dve.wait_ge(e_ready, n + 1)
                    e = ebuf[:, n % 2, :, :]
                    V.tensor_tensor(e, e, qk[:, hd, :, :], ALU.mult).then_inc(qkt_ready, 1)
                    if l in (2, 4):
                        ahead(BASE["gla_r"] + 2 * hd + l // 2 - 1)
                    merge(l)
                for b in range(2):
                    dve.wait_ge(r_copied, 2 * hd + b + 1)
                    V.sem_inc(drained, 1)
                merge(NLEV)
                dve.wait_ge(ei_ready, hd + 1)
                qs = qk[:, hd, 0:1, TP:T].to_broadcast([P, 2, TS])
                V.tensor_tensor(qfb[:, :, :], qfb[:, :, :], qs, ALU.mult)
                k0 = qk[:, hd, 1:2, 0:P].to_broadcast([P, 2, P])
                V.tensor_tensor(kbar[:, 0:2, :], kbar[:, 0:2, :], k0, ALU.mult)
                k12 = qk[:, hd, 1, P:T].rearrange("p (a b) -> p a b", a=2)
                V.tensor_tensor(kbar[:, 2:4, :], kbar[:, 2:4, :], k12, ALU.mult).then_inc(kbar_ready, 1)
                dve.wait_ge(u_done, hd + 1)
                for j in range(2):
                    last = V.scalar_tensor_tensor(mst[:, j, :], s0[:, hd, j, :], bl[:, 4 + j:5 + j],
                                                  bank[2][:, j * DV:(j + 1) * DV], ALU.mult, ALU.add)
                last.then_inc(st_ready, 1)
            for hd in range(HEADS):
                dve.wait_ge(ostd, hd + 1)
                seq.step(V.reciprocal(bcum[:, hd, 1, :], bcum[:, hd, 0, :]))
                for c in range(2):
                    last = V.scalar_tensor_tensor(qk[:, hd, c, :], qk[:, hd, c, :], gla_g[:, 2 * hd + c:2 * hd + c + 1],
                                                  bcum[:, hd, 1, :], ALU.mult, ALU.mult)
                seq.step(last)
                if hd == 0:
                    dve.wait_ge(osr, 1)
                for c in range(2):
                    m = 2 * hd + c
                    V.tensor_tensor(sr[:, m, :], sr[:, m, :], qk[:, hd, c, :], ALU.mult).then_inc(og, 1)
            for m in range(DC):
                dve.wait_ge(oghi, m + 1)
                V.tensor_tensor(h_lo[:, m, :], sr[:, m, :], h_hi[:, m, :].bitcast(F32), ALU.subtract).then_inc(og_ready, 1)
            mixer_out("gla_out", 1, 4)

            norm(5)
            ffn_in(3)
            ffn_out(3)
            norm(6)


def lay_out(i):
    c_ = np.ascontiguousarray

    def cols(v):
        v = np.asarray(v)
        v = v.reshape(v.shape[:-1] + (v.shape[-1] // P, P))
        return c_(np.moveaxis(v, -1, 0))

    def m_tiles(w, m_first=None):
        k, n = w.shape
        return c_(w.reshape(k // P, P, n // P, P).transpose(2, 1, 0, 3).reshape(n // P, P, k))

    x = np.concatenate([i["x_prompt"][0], i["x_sample"][0]], axis=0)
    o = {"x": c_(x.reshape(T, DC, P).transpose(2, 1, 0))}
    o["ada_w"] = np.concatenate([m_tiles(i["ada_w"][l]) for l in range(2)], axis=0)
    fi, fo = [], []
    for l in range(2):
        for j in range(2):
            w = i["ffn_w_in"][l, j].reshape(DC, P, 2, FC, P).transpose(3, 2, 1, 0, 4)
            fi.append(w.reshape(2 * FC, P, DC * P))
            w = i["ffn_w_out"][l, j].reshape(2, KH, P, DC, P).transpose(3, 0, 2, 1, 4)
            fo.append(w.reshape(2 * DC, P, WMAX))
    o["ffn_in"], o["ffn_out"] = c_(np.stack(fi)), c_(np.stack(fo))
    w = m_tiles(i["rg_w_in"][0]).reshape(2, RC, P, DC * P)
    o["rg_in"] = c_(np.stack([w[1], w[0]], axis=1).reshape(2 * RC, P, DC * P))
    g = np.stack([i["rg_w_a"][0], i["rg_w_i"][0]])
    g = g.reshape(2, 2, 2, HALF, P, P).transpose(2, 1, 4, 3, 0, 5)
    o["rg_gates"] = c_(g.reshape(4, P, RC * P))
    o["rg_out"] = m_tiles(i["rg_w_out"][0])
    w = i["gla_w_in"][0]
    o["gla_qk"] = m_tiles(w[:, 0:1024])
    o["gla_v"] = c_(w[:, 1024:2048].reshape(DC, P, 1024))
    o["gla_r"] = m_tiles(w[:, 2048:3072])
    o["gla_out"] = m_tiles(i["gla_w_out"][0])
    o["s0"] = c_(i["state_gla"][0, 0].transpose(2, 1, 0, 3).reshape(P, HEADS * 2 * DV))
    g2 = np.zeros((2 * RANK, 2, HEADS * P), np.float32)
    for dr in range(2):
        g2[dr * RANK:(dr + 1) * RANK, dr] = i["gla_w_g2"][0, dr]
    o["wg2"] = g2
    t = np.arange(P)
    o["masks"] = c_(np.stack([(t[:, None] ^ t[None, :]) // s == 1 for s in LEVELS], axis=1).astype(np.float32)).reshape(P, NLEV * P)
    wz = w[:, 3072:3072 + 2 * RANK].reshape(DC, P, 2 * RANK).transpose(1, 0, 2)
    parts = {"c": np.stack([cols(i["c_ctx"]), cols(i["c"][0])], axis=-1), "ada_b": cols(i["ada_b"]),
             "norm_g": cols(i["norm_g"]), "final_g": cols(i["final_norm"]),
             "conv_w": np.swapaxes(cols(i["rg_conv_w"][0]), 1, 2), "conv_b": cols(i["rg_conv_b"][0]),
             "gate_b": np.stack([cols(i["rg_b_a"][0]), cols(i["rg_b_i"][0])], axis=1), "lam": cols(i["rg_lambda"][0]),
             "h0": cols(i["state_rglru"][0, 0]), "gla_b": cols(i["gla_b_g"][0]), "gla_g": cols(i["gla_norm"][0]),
             "wz": wz, "ident": np.eye(P, dtype=np.float32)}
    o["small"] = c_(np.concatenate([parts[k].reshape(P, -1) for k in SMALL], axis=1))
    return o


def kernel(**inputs):
    import concourse.bacc as _bacc
    from concourse.bass_utils import run_bass_kernel_spmd as _run

    arrays = lay_out({k: np.asarray(v) for k, v in inputs.items()})
    nc = _bacc.Bacc("TRN2", target_bir_lowering=False, num_devices=1)
    d = {k: nc.dram_tensor(f"in_{k}", v.shape, mybir.dt.from_np(v.dtype), kind="ExternalInput").ap()
         for k, v in arrays.items()}
    outs = {"y": (P, DC, T), "rg_state": (P, 2, RC), "gla_state": (HEADS, P, 2, DV)}
    for k, s in outs.items():
        d[k] = nc.dram_tensor(f"out_{k}", s, F32, kind="ExternalOutput").ap()
    build(nc, d)
    r = _run(nc, [{f"in_{k}": v for k, v in arrays.items()}], core_ids=[0]).results[0]
    y = r["out_y"].transpose(2, 1, 0).reshape(T, D)
    rg = r["out_rg_state"].transpose(1, 2, 0).reshape(1, 1, 2, DR)
    gla = r["out_gla_state"].transpose(2, 0, 1, 3).reshape(1, 1, 2, HEADS, P, DV)
    c_ = np.ascontiguousarray
    return c_(y[None, :TP]), c_(y[None, TP:]), c_(rg), c_(gla)
```

```python
from contextlib import ExitStack

import numpy as np

import concourse.bass as bass
from concourse import mybir

F32 = mybir.dt.float32
F32R = mybir.dt.float32r
U8 = mybir.dt.uint8
ACT = mybir.ActivationFunctionType
ALU = mybir.AluOpType

P = 128
D = 1024
DC = D // P
TP, TS = 128, 256
T = TP + TS
GROUPS = [(0, TP, 0), (TP, TS, 1)]
GRID_W = 64
ROWS = TS // GRID_W
EPS = 1e-6
N_MOD = 9
DF = 2816
FC = DF // P
DR = 1280
RC = DR // P
CW = 4
HEADS = 4
DV = 256
RANK = 16
TAU = 16.0
QSCALE = float(P) ** -0.5
NT = T // P
LEVELS = [64, 32, 16, 8, 4, 2, 1]
NLEV = len(LEVELS)

XPAD = 1 + TP + 2 + TS + 2
XW = TP + 2 + TS
XGROUPS = [(0, TP, 0), (TP + 2, TS, 1)]
HALF = RC // 2

RING = 4
KH = FC // 2
WMAX = KH * P
PHASES = [("ffn_in0", 2 * FC, DC * P), ("ffn_out0", 2 * DC, WMAX), ("rg_in", 2 * RC, DC * P),
          ("rg_gates", 4, RC * P), ("rg_out", DC, RC * P),
          ("ffn_in1", 2 * FC, DC * P), ("ffn_out1", 2 * DC, WMAX),
          ("ffn_in2", 2 * FC, DC * P), ("ffn_out2", 2 * DC, WMAX),
          ("gla_qk", DC, DC * P), ("gla_v", DC, DC * P), ("gla_r", DC, DC * P), ("gla_out", DC, DC * P),
          ("ffn_in3", 2 * FC, DC * P), ("ffn_out3", 2 * DC, WMAX)]
BASE, WIDTH, COUNT = {}, [], {}
for _name, _n, _w in PHASES:
    assert _n % RING == 0
    BASE[_name], COUNT[_name] = len(WIDTH), _n
    WIDTH += [_w] * _n
BLOCKS = len(WIDTH)

ADA_PER_LAYER = N_MOD * DC
ADA_START, ADA_IN, ADA_OUT = 2 * DC, 2 * FC, 2 * DC
ADA_LAST = 2 * ADA_PER_LAYER - ADA_START - 2 * (ADA_IN + ADA_OUT)
assert ADA_LAST == DC
ADA_PE = 6
ADA_ORDER = [0, 1, 6, 7, 2, 8, 9, 10, 3, 4, 11, 12, 5, 13, 14, 15]
ADA_RING = 2

SMALL = {}
_at = 0
for _name, _w in [("c", 2 * DC), ("ada_b", 2 * ADA_PER_LAYER), ("norm_g", 6 * DC), ("final_g", DC),
                  ("conv_w", RC * CW), ("conv_b", RC), ("gate_b", 4 * RC), ("lam", 2 * RC), ("h0", 2 * RC),
                  ("gla_b", 2 * HEADS), ("gla_g", DC), ("wz", DC * 2 * RANK), ("ident", P)]:
    SMALL[_name] = (_at, _at + _w)
    _at += _w
SMALL_W = _at


def build(nc, d):
    ctx = ExitStack()

    def sb(name, shape, dt=F32, scope=None):
        return (scope or ctx).enter_context(nc.sbuf_tensor(name, shape, dt))

    def sem(name):
        return ctx.enter_context(nc.semaphore(name))

    with ctx:
        x = sb("x", [P, DC, T])
        raw = sb("raw", [P, RING, WMAX])
        w_hi_sb = sb("w_hi_sb", [P, RING, WMAX], F32R)
        w_lo_sb = sb("w_lo_sb", [P, RING, WMAX], F32R)
        ada_raw = sb("ada_raw", [P, ADA_RING, DC * P])
        small = sb("small", [P, SMALL_W])
        csil = sb("csil", [P, DC, 2])
        mod_all = sb("mod_all", [P, 2 * ADA_PER_LAYER, 2])
        mod = mod_all[:, :, :].rearrange("p (l j) c -> p l j c", l=2)
        mod_turn = sb("mod_turn", [P, RING, 2])
        gain = sb("gain", [P, 6, DC, 2])
        halfgate = sb("halfgate", [P, 4, DC, 2])
        ones = sb("ones", [P, P])
        eps = sb("eps", [P, 1])
        rgc = sb("rgc", [P, 12, 2 * RC])
        rg_state = sb("rg_state", [P, 2, RC])
        tmp_a = sb("tmp_a", [P, 2, XW])
        tmp_b = sb("tmp_b", [P, 2, XW])
        ss = sb("ss", [P, T])
        sq = sb("sq", [P, T])
        sq_last = sb("sq_last", [P, T])
        diag = sb("diag", [P, NT, P])
        rstd = sb("rstd", [P, HEADS * NT])
        hbuf_scope = ExitStack()
        h_hi = sb("h_hi", [P, DC, T], F32R, hbuf_scope)
        h_lo = sb("h_lo", [P, DC, T], F32R, hbuf_scope)
        ffn_scope = ExitStack()
        a_hi = sb("a_hi", [P, FC, T], F32R, ffn_scope)
        a_lo = sb("a_lo", [P, FC, T], F32R, ffn_scope)
        ffn_scope.close()
        first_scope = ExitStack()
        ada_first = sb("ada_first", [P, ADA_START, DC * P], F32, first_scope)
        first_scope.close()
        rg_scope = ExitStack()
        xc = sb("xc", [P, RC, XW], F32, rg_scope)
        xc_hi = sb("xc_hi", [P, RC, XW], F32R, rg_scope)
        xc_lo = sb("xc_lo", [P, RC, XW], F32R, rg_scope)
        gate = sb("gate", [P, RC, T], F32, rg_scope)
        rg_scope.close()
        gla_scope = ExitStack()
        qk = sb("qk", [P, HEADS, 2, T], F32, gla_scope)
        vt = sb("vt", [P, NT, HEADS * DV], F32, gla_scope)
        sr = sb("sr", [P, DC, T], F32, gla_scope)
        bcum = sb("bcum", [P, HEADS, 2, T], F32, gla_scope)
        ebuf = sb("ebuf", [P, 2, 2, T], F32, gla_scope)
        scores = sb("scores", [P, T], F32, gla_scope)
        qfb = sb("qfb", [P, 2, TS], F32, gla_scope)
        kbar = sb("kbar", [P, 4, P], F32, gla_scope)
        kbar_t = sb("kbar_t", [P, 4, P], F32, gla_scope)
        wg2 = sb("wg2", [2 * RANK, 2, HEADS * P], F32, gla_scope)
        gla_scope.close()
        hbuf_scope.close()
        rgb_scope = ExitStack()
        ga = sb("ga", [P, HALF, XW], F32, rgb_scope)
        gv = sb("gv", [P, HALF, XW], F32, rgb_scope)
        gix = sb("gix", [P, HALF, XW], F32, rgb_scope)
        rgb_scope.close()
        out_scope = ExitStack()
        y_out = sb("y_out", [P, DC, T], F32, out_scope)
        out_scope.close()
        mask_in = y_out[:, :, :].rearrange("p m t -> p (m t)")[:, 0:NLEV * P]
        sb("span_all", [P, 2 * DC * T + 2 * FC * T], F32, ctx)
        extra = sb("extra", [P, 2 * D], F32, ctx)
        crow = extra[:, :].rearrange("p (c k) -> p c k", c=2)
        xpad = extra[:, 0:2 * XPAD].rearrange("p (a b) -> p a b", a=2)
        yf = extra[:, 0:HALF * XW].rearrange("p (n t) -> p n t", n=HALF)
        pst = extra[:, 0:2 * DV].rearrange("p (a b) -> p a b", a=2)
        mst = extra[:, 2 * DV:4 * DV].rearrange("p (a b) -> p a b", a=2)
        at = 4 * DV
        bl = extra[:, at:at + 4 * HEADS].rearrange("p (h j) -> p h j", h=HEADS)
        ebl = extra[:, at + 4 * HEADS:at + 6 * HEADS].rearrange("p (h j) -> p h j", h=HEADS)
        at += 6 * HEADS
        zt = extra[:, at:at + NT * 2 * RANK].rearrange("p (a b) -> p a b", a=NT)
        at += NT * 2 * RANK
        zT = extra[0:2 * RANK, at:at + T]
        masks = sb("masks", [P, NLEV, P], U8, ctx)
        reset = sb("reset", [P, T], F32, ctx)
        wz_hi = sb("wz_hi", [P, DC, 2 * RANK], F32R, ctx)
        wz_lo = sb("wz_lo", [P, DC, 2 * RANK], F32R, ctx)

        bank = [ctx.enter_context(nc.psum_tensor(f"bank{i}", [P, 512], F32)) for i in range(4)]
        wide = ctx.enter_context(nc.psum_tensor("wide", [P, 1024], F32))
        bank += [wide[:, 0:512], wide[:, 512:1024]]
        bank += [ctx.enter_context(nc.psum_tensor(f"bank{i}", [P, 512], F32)) for i in (6, 7)]
        ada_ps = bank[7][:, 0:2 * ADA_PE].rearrange("p (j c) -> p j c", c=2)
        sum_ps = bank[6][:, 0:NT]
        rinv = bank[6][:, P:P + T]

        def sm(name):
            a, b = SMALL[name]
            return small[:, a:b]

        csm = sm("c").rearrange("p (k c) -> p k c", c=2)
        ada_b = sm("ada_b")
        norm_g = sm("norm_g").rearrange("p (n k) -> p n k", k=DC)
        final_g = sm("final_g")
        conv_w = sm("conv_w").rearrange("p (m k) -> p m k", k=CW)
        conv_b = sm("conv_b")
        lam = sm("lam")
        h0 = sm("h0").rearrange("p (d m) -> p d m", d=2)
        gla_b = sm("gla_b").rearrange("p (d h) -> p d h", d=2)
        gla_g = sm("gla_g")
        wz = sm("wz").rearrange("p (k z) -> p k z", k=DC)
        ident = sm("ident")
        hb = rgc[:, 0:2, :]
        cc, cc2, ncc = rgc[:, 2, :], rgc[:, 3, :], rgc[:, 4, :]
        s0 = ada_raw[:, :, :].rearrange("p a b -> p (a b)").rearrange("p (h d v) -> p h d v", h=HEADS, d=2)

        small_loaded = sem("small_loaded")
        masks_loaded = sem("masks_loaded")
        masks_made = sem("masks_made")
        wg2_loaded = sem("wg2_loaded")
        x_loaded = sem("x_loaded")
        s0_loaded = sem("s0_loaded")
        out_done = sem("out_done")
        w_loaded = [sem(f"w_loaded{s}") for s in range(RING)]
        w_hi = sem("w_hi")
        w_split = sem("w_split")
        w_used = sem("w_used")
        drained = sem("drained")
        ada_loaded = [sem(f"ada_loaded{s}") for s in range(ADA_RING)]
        ada_first_loaded = [sem(f"ada_first_loaded{s}") for s in range(RING)]
        ada_used = sem("ada_used")
        csil_ready = sem("csil_ready")
        ada_half = sem("ada_half")
        ada_by_dve = sem("ada_by_dve")
        turn_taken = sem("turn_taken")
        crow_loaded = sem("crow_loaded")
        crow_ready = sem("crow_ready")
        consts = sem("consts")
        mods_ready = sem("mods_ready")
        x_ready = sem("x_ready")
        pool_seq = sem("pool_seq")
        dve_seq = sem("dve_seq")
        act_seq = sem("act_seq")
        ss_ready = sem("ss_ready")
        sum_done = sem("sum_done")
        std_ready = sem("std_ready")
        sq_ready = sem("sq_ready")
        diag_ready = sem("diag_ready")
        rinv_ready = sem("rinv_ready")
        y_ready = sem("y_ready")
        hhi_ready = sem("hhi_ready")
        h_ready = sem("h_ready")
        silu_ready = sem("silu_ready")
        ahi_ready = sem("ahi_ready")
        a_ready = sem("a_ready")
        xpad_ready = sem("xpad_ready")
        conv_done = sem("conv_done")
        xchi_ready = sem("xchi_ready")
        xc_ready = sem("xc_ready")
        gate_done = sem("gate_done")
        gate_drained = sem("gate_drained")
        rg_act = sem("rg_act")
        rg_dve = sem("rg_dve")
        rg_sqrt = sem("rg_sqrt")
        rg_y = sem("rg_y")
        rg_yhi = sem("rg_yhi")
        rg_yready = sem("rg_yready")
        rgc_ready = sem("rgc_ready")
        gelu_ready = sem("gelu_ready")
        z_done = sem("z_done")
        z_copied = sem("z_copied")
        zz_done = sem("zz_done")
        sp_ready = sem("sp_ready")
        zz_drained = sem("zz_drained")
        b_ready = sem("b_ready")
        v_copied = sem("v_copied")
        d_ready = sem("d_ready")
        e_ready = sem("e_ready")
        qkt_ready = sem("qkt_ready")
        s_done = sem("s_done")
        s_drained = sem("s_drained")
        bl_ready = sem("bl_ready")
        ei_ready = sem("ei_ready")
        kbar_ready = sem("kbar_ready")
        rg_a = sem("rg_a")
        rg_a2 = sem("rg_a2")
        qe_ready = sem("qe_ready")
        q_ready = sem("q_ready")
        odiag = sem("odiag")
        obc = sem("obc")
        kt_done = sem("kt_done")
        kt_copied = sem("kt_copied")
        u_done = sem("u_done")
        u_copied = sem("u_copied")
        st_ready = sem("st_ready")
        o_done = sem("o_done")
        o_copied = sem("o_copied")
        r_copied = sem("r_copied")
        state_out = sem("state_out")
        osum = sem("osum")
        osum_done = sem("osum_done")
        ostd = sem("ostd")
        osr = sem("osr")
        og = sem("og")
        oghi = sem("oghi")
        og_ready = sem("og_ready")

        class Seq:

            def __init__(self, eng, s):
                self.eng, self.s, self.n, self.i, self.per = eng, s, 0, None, 0

            def value(self):
                return self.n if self.i is None else self.i * self.per + self.n

            def mark(self, ins):
                ins.then_inc(self.s, 1)
                self.n += 1

            def wait(self):
                self.eng.wait_ge(self.s, self.value())

            def step(self, ins):
                self.mark(ins)
                self.wait()

        NORMS = [("ffn_in0", 0), ("rg_in", 1), ("ffn_in1", 2), ("ffn_in2", 3), ("gla_qk", 4), ("ffn_in3", 5)]

        def layer_of(q):
            return q // 3, q % 3

        def col_major(ap, q, n):
            if q == 4 and n == TS:
                return ap.rearrange("p (w r) -> p r w", w=GRID_W)
            return ap

        def row_major(ap, q, n):
            if q == 4 and n == TS:
                return ap.rearrange("p (r w) -> p r w", r=ROWS)
            return ap

        V_BANKS = [0, 1, 2, 3, 6, 7]
        TURN_AT, STATE_AT, OUT_AT, SUM_AT = [8, 10, 12, 14], [9, 11, 13, 15], [10, 12, 14], [12, 14]
        score_buf = [tmp_b[:, 0, 0:T], tmp_b[:, 1, 0:T], scores[:, :]]
        osum_ps = bank[1][:, T:T + HEADS * NT]
        diags = [diag[:, :, :], sq_last[:, :].rearrange("p (a b) -> p a b", a=NT)]

        block = ctx.enter_context(nc.Block())

        @block.sync
        def _(sp):
            def load_block(src, i, b):
                s = b % RING
                sp.dma_start(raw[:, s, 0:src.shape[2]],
                             src[bass.ds(RING * i + b, 1)].rearrange("a p k -> p (a k)")).then_inc(w_loaded[s], 16)

            def phase(name, src):
                base = BASE[name]
                start = 0 if base else 1
                with sp.Fori(start, COUNT[name] // RING) as i:
                    for b in range(RING):
                        sp.wait_ge(w_split, RING * i + (base + b - RING + 1))
                        load_block(src, i, b)

            sp.dma_start(small[:, :], d["small"]).then_inc(small_loaded, 16)
            sp.dma_start(x[:, :, :], d["x"]).then_inc(x_loaded, 16)
            sp.dma_start(extra[:, :], d["c_row"].to_broadcast([P, 2 * D])).then_inc(crow_loaded, 16)
            per = ADA_START // RING
            for s in range(RING):
                sp.dma_start(ada_first[:, per * s:per * s + per, :],
                             d["ada_w"][per * s:per * s + per].rearrange("a p k -> p a k")
                             ).then_inc(ada_first_loaded[s], 16)
            for b in range(RING):
                load_block(d["ffn_in"][0], 0, b)
            phase("ffn_in0", d["ffn_in"][0])
            phase("ffn_out0", d["ffn_out"][0])
            for name in ("rg_in", "rg_gates", "rg_out"):
                phase(name, d[name])
            for f in (1, 2):
                if f == 1:
                    sp.wait_ge(rg_y, 4)
                    sp.dma_start(extra[:, :], d["c_row"].to_broadcast([P, 2 * D])).then_inc(crow_loaded, 16)
                phase(f"ffn_in{f}", d["ffn_in"][f])
                phase(f"ffn_out{f}", d["ffn_out"][f])
            for name in ("gla_qk", "gla_v", "gla_r", "gla_out"):
                phase(name, d[name])
                if name == "gla_qk":
                    sp.wait_ge(ada_used, 2 * ADA_PER_LAYER)
                    sp.dma_start(ada_raw[:, :, :].rearrange("p a b -> p (a b)"), d["s0"]).then_inc(s0_loaded, 16)
            phase("ffn_in3", d["ffn_in"][3])
            phase("ffn_out3", d["ffn_out"][3])
            for m in range(DC):
                sp.wait_ge(h_ready, 8 * 6 + m + 1)
                sp.dma_start(d["y"][:, m, :], y_out[:, m, :]).then_inc(out_done, 16)
            sp.wait_ge(out_done, 16 * DC)
            sp.wait_ge(state_out, 16 * (HEADS + 1))

        @block.gpsimd
        def _(pool):
            seq = Seq(pool, pool_seq)
            pool.memset(ones[:, :], 1.0).then_inc(consts, 1)
            pool.memset(eps[:, :], EPS).then_inc(consts, 1)
            pool.memset(reset[:, :], 1.0).then_inc(consts, 1)
            pool.wait_ge(consts, 3)
            pool.memset(reset[:, :].rearrange("p (n t) -> p n t", t=P)[:, :, 0:1], 0.0).then_inc(consts, 1)

            def ada_run(first, n):
                with pool.Fori(0, n // ADA_RING) as i:
                    for b in range(ADA_RING):
                        pool.wait_ge(ada_used, ADA_RING * i + (first + b - ADA_RING + 1))
                        pool.wait_ge(consts, 1)
                        pool.dma_start(ada_raw[:, b, :],
                                       d["ada_w"][bass.ds(ADA_RING * i + (first + b), 1)].rearrange("a p k -> p (a k)")
                                       ).then_inc(ada_loaded[b], 16)

            def ada_load(n):
                pool.wait_ge(ada_used, n - ADA_RING + 1)
                pool.dma_start(ada_raw[:, n % ADA_RING, :], d["ada_w"][n]).then_inc(ada_loaded[n % ADA_RING], 16)

            def sum_squares(q, ada=None, per=0):
                if q == 0:
                    pool.wait_ge(x_loaded, 16)
                for n in range(per):
                    ada_load(ada + n)
                for m in range(DC - 1):
                    for n in range(per):
                        ada_load(ada + per * (m + 1) + n)
                    if q:
                        pool.wait_ge(x_ready, DC * (q - 1) + m + 1)
                    if m == 0:
                        if q:
                            pool.wait_ge(sum_done, q)
                        seq.step(nc.gpsimd.tensor_tensor(ss[:, :], x[:, m, :], x[:, m, :], ALU.mult))
                        continue
                    seq.step(nc.gpsimd.tensor_tensor(sq[:, :], x[:, m, :], x[:, m, :], ALU.mult))
                    add = nc.gpsimd.tensor_tensor(ss[:, :], ss[:, :], sq[:, :], ALU.add)
                    if m == DC - 2:
                        add.then_inc(ss_ready, 1)
                    else:
                        seq.step(add)

            sum_squares(0)
            n_ada = ADA_START
            for q in (1, 2, 3, 4):
                if q == 2:
                    for c in range(2 * RC):
                        pool.wait_ge(rg_a, c + 1)
                        n = c % HALF
                        nc.gpsimd.tensor_tensor(gv[:, n, :], ga[:, n, :], ga[:, n, :], ALU.mult).then_inc(rg_a2, 1)
                    sum_squares(q)
                elif q == 4:
                    sum_squares(q, n_ada, 1)
                else:
                    ada_run(n_ada, ADA_IN)
                    sum_squares(q, n_ada + ADA_IN, 2)
                    n_ada += ADA_IN + ADA_OUT

            def squares(hd):
                pool.wait_ge(o_copied, hd + 1)
                if hd:
                    pool.wait_ge(osum_done, hd)
                nc.gpsimd.tensor_tensor(ss[:, :], qk[:, hd, 0, :], qk[:, hd, 0, :], ALU.mult)
                nc.gpsimd.tensor_tensor(sq[:, :], qk[:, hd, 1, :], qk[:, hd, 1, :], ALU.mult).then_inc(osum, 1)

            for hd in range(HEADS):
                pool.wait_ge(b_ready, 2 * hd + 2)
                if hd == HEADS - 1:
                    squares(0)
                for l, s in enumerate(LEVELS):
                    n = hd * NLEV + l
                    if hd == HEADS - 1 and l == 3:
                        squares(1)
                    if n >= 2:
                        pn = n - 2
                        pool.wait_ge(s_done, pn // NLEV * (NLEV + 1) + pn % NLEV + 2)
                    f, b = (bcum[:, hd, j, :].rearrange("p (n h s) -> p n h s", h=2, s=s) for j in range(2))
                    eq, ek = (ebuf[:, n % 2, j, :].rearrange("p (n h s) -> p n h s", h=2, s=s) for j in range(2))
                    nb = T // (2 * s)
                    ref_f = f[:, :, 0, s - 1:s].to_broadcast([P, nb, s])
                    ref_b = b[:, :, 1, 0:1].to_broadcast([P, nb, s])
                    nc.gpsimd.tensor_tensor(eq[:, :, 1, :], f[:, :, 1, :], ref_f, ALU.subtract)
                    nc.gpsimd.tensor_tensor(eq[:, :, 0, :], b[:, :, 0, :], ref_b, ALU.subtract)
                    nc.gpsimd.tensor_tensor(ek[:, :, 0, :], ref_f, f[:, :, 0, :], ALU.subtract)
                    nc.gpsimd.tensor_tensor(ek[:, :, 1, :], ref_b, b[:, :, 1, :], ALU.subtract).then_inc(d_ready, 1)
            for hd in range(2, HEADS):
                squares(hd)
            for q in (5, 6):
                sum_squares(q)

        @block.tensor
        def _(pe):
            def tile(out, slot, ks, hi, lo, start, stop, at=0):
                for j, k in enumerate(ks):
                    w = slice((at + j) * P, (at + j + 1) * P)
                    pe.matmul(out, w_hi_sb[:, slot, w], hi[k], start=start and j == 0, stop=False)
                    pe.matmul(out, w_hi_sb[:, slot, w], lo[k], start=False, stop=False)
                    last = pe.matmul(out, w_lo_sb[:, slot, w], hi[k], start=False,
                                     stop=stop and j == len(ks) - 1)
                return last

            h_chunks = ([h_hi[:, k, :] for k in range(DC)], [h_lo[:, k, :] for k in range(DC)])
            a_chunks = ([a_hi[:, k, :] for k in range(FC)], [a_lo[:, k, :] for k in range(FC)])
            y_chunks = ([xc_hi[:, k, 0:T] for k in range(RC)], [xc_lo[:, k, 0:T] for k in range(RC)])

            def norm(q):
                pe.wait_ge(ss_ready, q + 1)
                if q == 0:
                    pe.wait_ge(consts, 1)
                pe.wait_ge(sq_ready, q + 1)
                for t in range(NT):
                    tok = slice(t * P, (t + 1) * P)
                    pe.matmul(sum_ps[:, t:t + 1], ss[:, tok], ones[:, 0:1], start=True, stop=False)
                    last = pe.matmul(sum_ps[:, t:t + 1], sq_last[:, tok], ones[:, 0:1], start=False, stop=True)
                last.then_inc(sum_done, 1)
                pe.wait_ge(diag_ready, q + 1)
                pe.matmul(rinv, ones[:, :], diag[:, :, :].rearrange("p a b -> p (a b)"), start=True,
                          stop=True).then_inc(rinv_ready, 1)

            def arriving(base, ks, chunks, ready, n0):
                for b in range(RING):
                    pe.wait_ge(w_split, base + b + 1)
                early = 5
                for k in range(early):
                    pe.wait_ge(ready, n0 + k + 1)
                    for b in range(RING):
                        tile(bank[b][:, 0:T], b, [k], *chunks, k == 0, False, k)
                pe.wait_ge(ready, n0 + len(ks))
                for b in range(RING):
                    tile(bank[b][:, 0:T], b, ks[early:], *chunks, False, True, early).then_inc(w_used, 1)

            def one_tile_blocks(name, chunks, ks, ready, n0):
                base, n = BASE[name], COUNT[name]
                if base:
                    pe.wait_ge(drained, base)
                arriving(base, ks, chunks, ready, n0)
                with pe.Fori(1, n // RING) as i:
                    for b in range(RING):
                        pe.wait_ge(drained, RING * i + (base + b - RING + 1))
                        pe.wait_ge(w_split, RING * i + (base + b + 1))
                        tile(bank[b][:, 0:T], b, ks, *chunks, True, True).then_inc(w_used, 1)

            def ffn_out(name):
                base, n = BASE[name], COUNT[name]
                pe.wait_ge(drained, base)
                with pe.Fori(0, n // RING) as i:
                    for b in range(RING):
                        half, t = b % 2, b // 2
                        if half == 0:
                            pe.wait_ge(drained, RING * i + (base + b - 2))
                        pe.wait_ge(w_split, RING * i + (base + b + 1))
                        tile(bank[t][:, 0:T], b, range(KH * half, KH * half + KH), *a_chunks,
                             half == 0, half == 1).then_inc(w_used, 1)

            def ffn(f, q):
                norm(q)
                one_tile_blocks(f"ffn_in{f}", h_chunks, range(DC), h_ready, DC * q)
                pe.wait_ge(a_ready, FC * (f + 1))
                ffn_out(f"ffn_out{f}")

            pe.wait_ge(csil_ready, 1)
            for n, j in enumerate(ADA_ORDER):
                if j < ADA_PE:
                    pe.wait_ge(ada_first_loaded[n * RING // ADA_START], 16)
                    for k in range(DC):
                        last = pe.matmul(ada_ps[:, j, :], ada_first[:, n, k * P:(k + 1) * P], csil[:, k, :],
                                         start=k == 0, stop=k == DC - 1)
                    last.then_inc(ada_used, 1)
            ffn(0, 0)

            norm(1)
            one_tile_blocks("rg_in", h_chunks, range(DC), h_ready, DC)
            base = BASE["rg_gates"]
            pe.wait_ge(drained, base)
            pe.wait_ge(xc_ready, RC)
            for b in range(4):
                pe.wait_ge(w_split, base + b + 1)
                for t in range(RC):
                    g = b * RC + t
                    m = (b // 2) * HALF + t // 2
                    if g >= RING:
                        pe.wait_ge(gate_drained, g - RING + 1)
                    last = tile(bank[g % RING][:, 0:XW], b, [0], [xc_hi[:, m, :]], [xc_lo[:, m, :]], True, True, t)
                    last.then_inc(w_used if t == RC - 1 else gate_done, 1)
            one_tile_blocks("rg_out", y_chunks, range(RC), rg_yready, 0)

            ffn(1, 2)
            ffn(2, 3)

            norm(4)
            base = BASE["gla_qk"]
            pe.wait_ge(drained, base)
            arriving(base, range(DC), h_chunks, h_ready, DC * 4)
            for t in range(NT):
                out = bank[4][:, t * 2 * RANK:(t + 1) * 2 * RANK]
                tok = slice(t * P, (t + 1) * P)
                for k in range(DC):
                    pe.matmul(out, h_hi[:, k, tok], wz_hi[:, k, :], start=k == 0, stop=False)
                    pe.matmul(out, h_hi[:, k, tok], wz_lo[:, k, :], start=False, stop=False)
                    last = pe.matmul(out, h_lo[:, k, tok], wz_hi[:, k, :], start=False, stop=k == DC - 1)
            last.then_inc(z_done, 1)
            for b in range(RING, DC):
                pe.wait_ge(drained, base + b - RING + 1)
                pe.wait_ge(w_split, base + b + 1)
                tile(bank[b % RING][:, 0:T], b % RING, range(DC), *h_chunks, True, True).then_inc(w_used, 1)
                if b == RING:
                    pe.wait_ge(z_copied, 1)
                    for t in range(NT):
                        last = pe.transpose(bank[5][0:2 * RANK, t * P:(t + 1) * P], zt[:, t, :], ident)
                    last.then_inc(z_done, 1)
                    pe.wait_ge(z_copied, 2)
                    pe.wait_ge(wg2_loaded, 16)
                hd = b - RING
                for dr in range(2):
                    u = 2 * hd + dr
                    if u >= 2:
                        pe.wait_ge(zz_drained, u - 1)
                    pe.matmul(bank[4 + dr][:, 0:T], wg2[:, dr, hd * P:(hd + 1) * P], zT, start=True,
                              stop=True).then_inc(zz_done, 1)

            def value_block(b):
                base = BASE["gla_v"]
                pe.wait_ge(w_split, base + b + 1)
                if b == 0:
                    pe.wait_ge(drained, base)
                s = b % RING
                for t in range(NT):
                    tok = slice(t * P, (t + 1) * P)
                    for half in range(2):
                        out = bank[V_BANKS[2 * t + half]][:, :]
                        c = slice(512 * half, 512 * half + 512)
                        pe.matmul(out, h_hi[:, b, tok], w_hi_sb[:, s, c], start=b == 0, stop=False)
                        pe.matmul(out, h_hi[:, b, tok], w_lo_sb[:, s, c], start=False, stop=False)
                        last = pe.matmul(out, h_lo[:, b, tok], w_hi_sb[:, s, c], start=False, stop=b == DC - 1)
                last.then_inc(w_used, 1)

            def r_block(b):
                n = BASE["gla_r"] + b
                if b < 2:
                    pe.wait_ge(drained, BASE["gla_r"])
                else:
                    pe.wait_ge(r_copied, b - 1)
                pe.wait_ge(w_split, n + 1)
                tile(bank[b % 2][:, 0:T], b % RING, range(DC), *h_chunks, True, True).then_inc(w_used, 1)

            def level(n):
                hd, l = divmod(n, NLEV + 1)
                if n >= 2:
                    pe.wait_ge(s_drained, n - 1)
                else:
                    pe.wait_ge(zz_drained, 2 * HEADS)
                if l:
                    pe.wait_ge(qkt_ready, hd * NLEV + l)
                    e = ebuf[:, (hd * NLEV + l - 1) % 2, :, :]
                else:
                    e = qk[:, hd, :, :]
                for t in range(NT):
                    tok = slice(t * P, (t + 1) * P)
                    last = pe.matmul(bank[4 + n % 2][:, tok], e[:, 1, tok], e[:, 0, tok], start=True, stop=True)
                last.then_inc(s_done, 1)

            def turn_keys(hd):
                pe.wait_ge(kbar_ready, hd + 1)
                if hd:
                    pe.wait_ge(st_ready, hd)
                for j in range(4):
                    last = pe.transpose(bank[2][:, j * P:(j + 1) * P], kbar[:, j, :], ident)
                last.then_inc(kt_done, 1)

            def chunk_states(hd):
                pe.wait_ge(kt_copied, hd + 1)
                if hd:
                    pe.wait_ge(u_copied, hd)
                for j, t in enumerate((0, 0, 1, 2)):
                    last = pe.matmul(bank[3 - j // 2][:, (j % 2) * DV:(j % 2 + 1) * DV], kbar_t[:, j, :],
                                     vt[:, t, hd * DV:(hd + 1) * DV], start=True, stop=True)
                last.then_inc(u_done, 1)

            def outputs(hd):
                pe.wait_ge(st_ready, hd + 1)
                pe.wait_ge(q_ready, hd + 1)
                pe.wait_ge(s_drained, (hd + 1) * (NLEV + 1))
                if hd:
                    pe.wait_ge(o_copied, hd)
                for c in range(2):
                    vc = slice(hd * DV + c * P, hd * DV + (c + 1) * P)
                    cs = slice(c * P, (c + 1) * P)
                    for t in range(NT):
                        tok = slice(t * P, (t + 1) * P)
                        out = bank[6 + c][:, tok]
                        last = pe.matmul(out, vt[:, t, vc], score_buf[hd % 3][:, tok], start=True, stop=t == 0)
                        if t:
                            stok = slice((t - 1) * P, t * P)
                            sf = s0[:, hd, 0, cs] if t == 1 else mst[:, 0, cs]
                            sbk = s0[:, hd, 1, cs] if t == 2 else mst[:, 1, cs]
                            pe.matmul(out, sf, qfb[:, 0, stok], start=False, stop=False)
                            last = pe.matmul(out, sbk, qfb[:, 1, stok], start=False, stop=True)
                last.then_inc(o_done, 1)

            def output_sums(hd, r_blocks):
                pe.wait_ge(osum, hd + 1)
                pe.wait_ge(r_copied, r_blocks // 2 * 2)
                for t in range(NT):
                    tok = slice(t * P, (t + 1) * P)
                    out = osum_ps[:, hd * NT + t:hd * NT + t + 1]
                    pe.matmul(out, ss[:, tok], ones[:, 0:1], start=True, stop=False)
                    last = pe.matmul(out, sq[:, tok], ones[:, 0:1], start=False, stop=True)
                last.then_inc(osum_done, 1)

            for s in range(2 * DC):
                if s < DC:
                    value_block(s)
                else:
                    r_block(s - DC)
                level(2 * s)
                level(2 * s + 1)
                if s == DC + 1:
                    pe.wait_ge(s0_loaded, 16)
                if s in OUT_AT:
                    outputs(OUT_AT.index(s))
                if s in SUM_AT:
                    output_sums(SUM_AT.index(s), s - DC + 1)
                if s in TURN_AT:
                    turn_keys(TURN_AT.index(s))
                if s in STATE_AT:
                    chunk_states(STATE_AT.index(s))
            outputs(HEADS - 1)
            for hd in range(len(SUM_AT), HEADS):
                output_sums(hd, DC)
            for hd in range(HEADS):
                pe.wait_ge(odiag, hd + 1)
                if hd == 0:
                    pe.wait_ge(r_copied, DC)
                    pe.wait_ge(u_copied, HEADS)
                pe.matmul(bank[hd][:, 0:T], ones[:, :], diags[hd % 2].rearrange("p a b -> p (a b)"), start=True,
                          stop=True).then_inc(obc, 1)
            one_tile_blocks("gla_out", h_chunks, range(DC), og_ready, 0)

            norm(5)
            one_tile_blocks("ffn_in3", h_chunks, range(DC), h_ready, DC * 5)
            pe.wait_ge(a_ready, FC * 4)
            ffn_out("ffn_out3")
            norm(6)

        @block.scalar
        def _(act):
            A = nc.scalar.activation
            seq = Seq(act, act_seq)

            def hi_of(n, i=None, per=0):
                s = n % RING
                off = 0 if i is None else i
                act.wait_ge(w_loaded[s], off * 16 + 16 * (n // RING + 1))
                if i is not None or n >= RING:
                    act.wait_ge(w_used, off * RING + (n - RING + 1))
                w = WIDTH[n]
                A(w_hi_sb[:, s, 0:w], raw[:, s, 0:w], ACT.Copy).then_inc(w_hi, 1)

            def ahead(n):
                if n + RING < BLOCKS:
                    hi_of(n + RING)

            def norm_stats(q):
                if q == 0:
                    act.wait_ge(x_loaded, 16)
                    act.wait_ge(consts, 2)
                else:
                    act.wait_ge(x_ready, DC * q)
                A(sq_last[:, :], x[:, DC - 1, :], ACT.Square).then_inc(sq_ready, 1)
                nc.scalar.preload_act_table_set("sqrt_and_others")
                act.wait_ge(sum_done, q + 1)
                A(rstd[:, 0:NT], sum_ps, ACT.Sqrt, bias=eps[:, :], scale=1.0 / D).then_inc(std_ready, 1)

            def norm_apply(q, tables):
                nc.scalar.preload_act_table_set(tables)
                layer, j = layer_of(q)
                for m in range(DC):
                    act.wait_ge(y_ready, DC * q + m + 1)
                    for t0, n, g in GROUPS:
                        shift = mod[:, layer, 3 * j * DC + m, g:g + 1]
                        last = A(col_major(h_hi[:, m, t0:t0 + n], q, n), row_major(tmp_a[:, m % 2, t0:t0 + n], q, n),
                                 ACT.Identity, bias=shift)
                    last.then_inc(hhi_ready, 1)

            def norm(q, tables):
                norm_stats(q)
                norm_apply(q, tables)

            def ffn_in(f):
                base = BASE[f"ffn_in{f}"]

                def turn(i):
                    off = 0 if i is None else i
                    for p in range(2):
                        pp = FC - 2 + p if i is None else p
                        act.wait_ge(w_used, off * RING + (base + 2 * pp + 1))
                        A(tmp_b[:, p, 0:T], bank[2 * p][:, 0:T], ACT.Silu).then_inc(silu_ready, 1)
                        for b in range(2):
                            if i is None:
                                ahead(base + 2 * pp + b)
                            else:
                                hi_of(base + 2 * p + b + RING, i)
                        act.wait_ge(drained, off * RING + (base + 2 * pp + 2))
                        act.wait_ge(consts, 1)
                        out = a_hi[:, pp, :] if i is None else \
                            a_hi[:, bass.ds(i * 2 + p, 1), :].rearrange("p a t -> p (a t)")
                        A(out, tmp_a[:, p, 0:T], ACT.Copy).then_inc(ahi_ready, 1)

                with act.Fori(0, FC // 2 - 1) as i:
                    turn(i)
                turn(None)

            def only_weights(name):
                for b in range(COUNT[name]):
                    ahead(BASE[name] + b)

            def copy_states(hd):
                act.wait_ge(u_done, hd + 1)
                if hd:
                    act.wait_ge(state_out, 16 * (hd + 1))
                A(pst[:, :, :], bank[3][:, :].rearrange("p (a b) -> p a b", a=2), ACT.Copy).then_inc(u_copied, 1)
                act.wait_ge(u_copied, hd + 1)
                act.dma_start(d["gla_state"][hd], pst[:, :, :]).then_inc(state_out, 16)

            def copy_outputs(hd):
                act.wait_ge(o_done, hd + 1)
                for c in range(2):
                    last = A(qk[:, hd, c, :], bank[6 + c][:, 0:T], ACT.Copy)
                last.then_inc(o_copied, 1)

            act.wait_ge(small_loaded, 16)
            A(csil[:, :, :], csm, ACT.Silu).then_inc(csil_ready, 1)
            act.wait_ge(crow_loaded, 16)
            A(crow, crow, ACT.Silu).then_inc(crow_ready, 1)
            norm_stats(0)
            for n in range(RING):
                hi_of(n)
            A(wz_hi[:, :, :], wz, ACT.Copy).then_inc(csil_ready, 1)
            act.dma_start(mask_in, d["masks"]).then_inc(masks_loaded, 16)
            act.wait_ge(masks_loaded, 16)
            A(masks[:, :, :], mask_in.rearrange("p (a b) -> p a b", a=NLEV), ACT.Copy).then_inc(masks_made, 1)
            A(rgc[:, 5, :], lam, ACT.Abs).then_inc(act_seq, 1)
            seq.n += 1
            seq.wait()
            A(rgc[:, 6, :], rgc[:, 5, :], ACT.Exp, scale=-1.0).then_inc(rgc_ready, 1)
            act.wait_ge(rgc_ready, 2)
            A(rgc[:, 8, :], rgc[:, 7, :], ACT.Ln).then_inc(rgc_ready, 1)

            act.wait_ge(masks_made, 1)
            norm_apply(0, "silu_and_others")
            ffn_in(0)
            only_weights("ffn_out0")

            norm(1, "gelu_apprx_tanh_and_others")
            base = BASE["rg_in"]
            for b in range(2 * RC):
                m = b // 2
                if b % 2 == 0:
                    act.wait_ge(w_used, base + b + 1)
                    if m >= 2:
                        act.wait_ge(conv_done, m - 1)
                    for (t0, n, _), at in zip(GROUPS, (1, 1 + TP + 2)):
                        last = A(xpad[:, m % 2, at:at + n], bank[b % RING][:, t0:t0 + n], ACT.Copy)
                    last.then_inc(xpad_ready, 1)
                else:
                    act.wait_ge(conv_done, m + 1)
                    A(xc_hi[:, m, :], xc[:, m, :], ACT.Copy).then_inc(xchi_ready, 1)
                ahead(base + b)
            act.wait_ge(drained, BASE["rg_gates"])
            A(gate[:, :, :], gate[:, :, :], ACT.Gelu_apprx_tanh).then_inc(gelu_ready, 1)
            base = BASE["rg_gates"]
            act.wait_ge(rgc_ready, 4)
            for b in range(4):
                half, dr = b // 2, b % 2
                for n in range(HALF):
                    m = half * HALF + n
                    col = slice(dr * RC + m, dr * RC + m + 1)
                    c = b * HALF + n
                    if c >= 2:
                        act.wait_ge(rg_dve, c - 1)
                    for kind, out in ((0, tmp_a[:, c % 2, :]), (1, gix[:, n, :])):
                        g = b * RC + 2 * n + kind
                        if g % RC == RC - 1:
                            act.wait_ge(w_used, base + b + 1)
                        else:
                            act.wait_ge(gate_done, g - b + 1)
                        if b and n == 0 and kind == 0:
                            act.wait_ge(rg_y, b)
                        A(out, bank[g % RING][:, 0:XW], ACT.Tanh, bias=rgc[:, kind, col],
                          scale=0.5).then_inc(gate_drained, 1)
                    act.wait_ge(gate_drained, b * RC + 2 * n + 1)
                    A(ga[:, n, :], tmp_a[:, c % 2, :], ACT.Exp, bias=rgc[:, 2, col],
                      scale=rgc[:, 2, col]).then_inc(rg_a, 1)
                    A(tmp_b[:, c % 2, :], tmp_a[:, c % 2, :], ACT.Tanh, bias=rgc[:, 4, col],
                      scale=rgc[:, 4, col]).then_inc(rg_act, 1)
                ahead(base + b)
                act.wait_ge(rg_dve, (b + 1) * HALF)
                A(gv[:, :, :], gv[:, :, :], ACT.Sqrt, scale=0.25).then_inc(rg_sqrt, 1)
                if dr == 1:
                    act.wait_ge(rg_y, b + 1)
                    mm = slice(half * HALF, (half + 1) * HALF)
                    A(xc_hi[:, mm, 0:T], gate[:, mm, :], ACT.Copy).then_inc(rg_yhi, 1)
            act.wait_ge(rg_y, 4)
            act.dma_start(d["rg_state"], rg_state[:, :, :]).then_inc(state_out, 16)
            only_weights("rg_out")

            norm_stats(2)
            nc.scalar.preload_act_table_set("silu_and_others")
            act.wait_ge(crow_loaded, 32)
            A(crow, crow, ACT.Silu).then_inc(crow_ready, 1)
            norm_apply(2, "silu_and_others")
            ffn_in(1)
            only_weights("ffn_out1")
            norm(3, "silu_and_others")
            ffn_in(2)
            only_weights("ffn_out2")

            act.wait_ge(x_ready, 4 * DC)
            act.dma_start(wg2[:, :, :], d["wg2"]).then_inc(wg2_loaded, 16)
            norm(4, "natural_log_exp_and_others")
            for b in range(RING):
                ahead(BASE["gla_qk"] + b)
            act.wait_ge(z_done, 1)
            A(zt, bank[4][:, 0:NT * 2 * RANK].rearrange("p (a b) -> p a b", a=NT), ACT.Copy).then_inc(z_copied, 1)
            act.wait_ge(z_done, 2)
            A(zT, bank[5][0:2 * RANK, 0:T], ACT.Copy).then_inc(z_copied, 1)
            for u in range(2 * HEADS):
                hd, dr = u // 2, u % 2
                act.wait_ge(zz_done, u + 1)
                if u >= 2:
                    act.wait_ge(b_ready, u - 1)
                t = tmp_a[:, dr, 0:T]
                seq.step(A(t, bank[4 + dr][:, 0:T], ACT.Abs, bias=gla_b[:, dr, hd:hd + 1]))
                seq.step(A(t, t, ACT.Exp, scale=-1.0))
                A(t, t, ACT.Ln, bias=1.0).then_inc(sp_ready, 1)
                if dr:
                    ahead(BASE["gla_qk"] + RING + hd)
            for s in range(2 * DC):
                for n in (2 * s, 2 * s + 1):
                    hd, l = divmod(n, NLEV + 1)
                    if l:
                        n = hd * NLEV + l - 1
                        act.wait_ge(d_ready, n + 1)
                        e = ebuf[:, n % 2, :, :]
                        A(e, e, ACT.Exp, scale=1.0 / TAU).then_inc(e_ready, 1)
                if s - 1 in TURN_AT:
                    hd = TURN_AT.index(s - 1)
                    act.wait_ge(kt_done, hd + 1)
                    A(kbar_t[:, :, :], bank[2][:, :].rearrange("p (a b) -> p a b", a=4), ACT.Copy
                      ).then_inc(kt_copied, 1)
                    if hd:
                        act.wait_ge(o_done, hd)
                    for j in range(2):
                        last = A(qfb[:, j, :], bcum[:, hd, j, TP:T], ACT.Exp, scale=1.0 / TAU)
                    last.then_inc(qe_ready, 1)
                if s - 1 in STATE_AT:
                    copy_states(STATE_AT.index(s - 1))
                if s - 1 in OUT_AT:
                    copy_outputs(OUT_AT.index(s - 1))
                if s in TURN_AT:
                    hd = TURN_AT.index(s)
                    if hd == 0:
                        act.wait_ge(bl_ready, 1)
                        A(ebl, bl[:, :, 2:4], ACT.Exp)
                    if hd:
                        act.wait_ge(kt_copied, hd)
                    for j, (t, dr) in enumerate(((0, 0), (0, 1), (1, 0), (2, 1))):
                        last = A(kbar[:, j, :], bcum[:, hd, dr, t * P:(t + 1) * P], ACT.Exp, bias=bl[:, hd, j:j + 1],
                                 scale=-1.0 / TAU)
                    last.then_inc(ei_ready, 1)
                ahead(BASE["gla_v"] + s)
                if s == DC - 1:
                    act.wait_ge(w_used, BASE["gla_r"])
                    for j in range(3):
                        last = A(vt[:, j // 2, 512 * (j % 2):512 * (j % 2) + 512], bank[V_BANKS[j]][:, :], ACT.Copy)
                    last.then_inc(v_copied, 1)
                if s >= DC:
                    act.wait_ge(w_used, BASE["gla_v"] + s + 1)
                    A(sr[:, s - DC, :], bank[s % 2][:, 0:T], ACT.Copy).then_inc(r_copied, 1)
            copy_states(HEADS - 1)
            act.wait_ge(r_copied, DC)
            A(sr[:, :, :], sr[:, :, :], ACT.Silu).then_inc(osr, 1)
            copy_outputs(HEADS - 1)
            nc.scalar.preload_act_table_set("sqrt_and_others")
            act.wait_ge(osum_done, HEADS)
            A(rstd[:, :], osum_ps, ACT.Sqrt, bias=eps[:, :], scale=1.0 / DV).then_inc(ostd, 1)
            for m in range(DC):
                act.wait_ge(og, m + 1)
                A(h_hi[:, m, :], sr[:, m, :], ACT.Copy).then_inc(oghi, 1)
            only_weights("gla_out")

            norm(5, "silu_and_others")
            ffn_in(3)
            only_weights("ffn_out3")
            norm_stats(6)

        @block.vector
        def _(dve):
            V = nc.vector
            seq = Seq(dve, dve_seq)

            def lo_of(n, i=None):
                s = n % RING
                off = 0 if i is None else i
                w = WIDTH[n]
                dve.wait_ge(w_hi, off * RING + (n + 1))
                V.tensor_tensor(w_lo_sb[:, s, 0:w], raw[:, s, 0:w], w_hi_sb[:, s, 0:w].bitcast(F32),
                                ALU.subtract).then_inc(w_split, 1)

            def ahead(n):
                if n + RING < BLOCKS:
                    lo_of(n + RING)

            def take_mods(j0, j1, n, src=None):
                dve.wait_ge(ada_used, n)
                bias = ada_b[:, j0:j1].rearrange("p (j a) -> p j a", a=1).to_broadcast([P, j1 - j0, 2])
                out = mod_all[:, j0:j1, :]
                seq.step(V.tensor_tensor(out, out if src is None else src, bias, ALU.add))

            def ada_block(w, out, n, done, before):
                if before is not None:
                    dve.wait_ge(done, before)
                V.tensor_tensor_reduce(wide[:, :], w, crow[:, 0, :], 1.0, 0.0, ALU.mult, ALU.add,
                                       accum_out=out[:, 0:1]).then_inc(ada_half, 1)
                dve.wait_ge(ada_half, n + 1)
                V.tensor_tensor_reduce(wide[:, :], w, crow[:, 1, :], 1.0, 0.0, ALU.mult, ALU.add,
                                       accum_out=out[:, 1:2]).then_inc(done, 1)

            def ada_at(first, b, i=None):
                n = first + b
                s = n % ADA_RING
                off = 0 if i is None else RING * i
                dve.wait_ge(ada_loaded[s], (0 if i is None else i * (16 * RING // ADA_RING))
                            + 16 * ((n - ADA_START) // ADA_RING + 1))
                ada_block(ada_raw[:, s, :], mod_all[:, n, :] if i is None else mod_turn[:, b, :],
                          off + (n - ADA_PE), ada_used, off + n)

            def make_gain(q):
                layer, j = layer_of(q)
                g = norm_g[:, q, :].rearrange("p (k a) -> p k a", a=1).to_broadcast([P, DC, 2])
                seq.step(V.scalar_tensor_tensor(gain[:, q, :, :], mod[:, layer, (3 * j + 1) * DC:(3 * j + 2) * DC, :],
                                                1.0, g, ALU.add, ALU.mult))

            def make_halfgate(f):
                layer, j = f // 2, 2 * (f % 2)
                seq.step(V.tensor_scalar(halfgate[:, f, :, :], mod[:, layer, (3 * j + 2) * DC:(3 * j + 3) * DC, :],
                                         0.5, None, ALU.mult))

            def norm_stats(q):
                dve.wait_ge(std_ready, q + 1)
                seq.step(V.reciprocal(rstd[:, 0:NT], rstd[:, 0:NT]))
                V.tensor_tensor(diag[:, :, :], ident.rearrange("p (a b) -> p a b", a=1).to_broadcast([P, NT, P]),
                                rstd[:, 0:NT].rearrange("p (a b) -> p a b", b=1).to_broadcast([P, NT, P]),
                                ALU.mult).then_inc(diag_ready, 1)

            def norm(q):
                norm_stats(q)
                norm_apply(q)

            def norm_apply(q):
                dve.wait_ge(rinv_ready, q + 1)
                if q == 6:
                    for m in range(DC):
                        V.scalar_tensor_tensor(y_out[:, m, :], x[:, m, :], final_g[:, m:m + 1], rinv,
                                               ALU.mult, ALU.mult).then_inc(h_ready, 1)
                    return
                layer, j = layer_of(q)

                def scaled(m):
                    for t0, n, g in GROUPS:
                        last = V.scalar_tensor_tensor(tmp_a[:, m % 2, t0:t0 + n], x[:, m, t0:t0 + n],
                                                      gain[:, q, m, g:g + 1], rinv[:, t0:t0 + n], ALU.mult, ALU.mult)
                    last.then_inc(y_ready, 1)

                def low(m):
                    dve.wait_ge(hhi_ready, DC * q + m + 1)
                    for t0, n, g in GROUPS:
                        shift = mod[:, layer, 3 * j * DC + m, g:g + 1]
                        last = V.scalar_tensor_tensor(col_major(h_lo[:, m, t0:t0 + n], q, n),
                                                      row_major(tmp_a[:, m % 2, t0:t0 + n], q, n), shift,
                                                      col_major(h_hi[:, m, t0:t0 + n].bitcast(F32), q, n),
                                                      ALU.add, ALU.subtract)
                    last.then_inc(h_ready, 1)

                scaled(0)
                for m in range(DC):
                    if m + 1 < DC:
                        if m:
                            dve.wait_ge(h_ready, DC * q + m)
                        scaled(m + 1)
                    low(m)

            def ffn_in(f, ada=None):
                base = BASE[f"ffn_in{f}"]

                def ada_part(i, b):
                    if ada is None:
                        return
                    if i is None:
                        ada_at(ada + ADA_IN - RING, b)
                        return
                    if b == 0:
                        dve.wait_ge(turn_taken, i + (ADA_IN // RING * min(f, 1) + 1))
                    ada_at(ada, b, i)
                    if b == RING - 1:
                        dve.wait_ge(ada_used, RING * i + (ada + RING))
                        V.tensor_copy(mod_all[:, bass.ds(RING * i + ada, RING), :],
                                      mod_turn[:, :, :]).then_inc(turn_taken, 1)

                def turn(i):
                    off = 0 if i is None else i
                    for p in range(2):
                        pp = FC - 2 + p if i is None else p

                        def weights(b):
                            if i is None:
                                ahead(base + 2 * pp + b)
                            else:
                                lo_of(base + 2 * p + b + RING, i)

                        weights(0)
                        dve.wait_ge(silu_ready, off * 2 + (FC * f + pp + 1))
                        dve.wait_ge(w_used, off * RING + (base + 2 * pp + 2))
                        dve.wait_ge(w_split, off * RING + min(base + 2 * pp + RING + 1, BLOCKS))
                        V.tensor_tensor(tmp_a[:, p, 0:T], tmp_b[:, p, 0:T], bank[2 * p + 1][:, 0:T],
                                        ALU.mult).then_inc(drained, 2)
                        weights(1)
                        ada_part(i, 2 * p)
                        dve.wait_ge(ahi_ready, off * 2 + (FC * f + pp + 1))
                        at = slice(pp, pp + 1) if i is None else bass.ds(i * 2 + p, 1)
                        lo, hi = (b[:, at, :].rearrange("p a t -> p (a t)") for b in (a_lo, a_hi))
                        V.tensor_tensor(lo, tmp_a[:, p, 0:T], hi.bitcast(F32), ALU.subtract).then_inc(a_ready, 1)
                        ada_part(i, 2 * p + 1)

                if ada is not None:
                    V.sem_inc(turn_taken, 1)
                with dve.Fori(0, FC // 2 - 1) as i:
                    turn(i)
                turn(None)

            def update_x(m, q, bk, scale_of):
                for t0, n, g in GROUPS:
                    last = V.scalar_tensor_tensor(row_major(x[:, m, t0:t0 + n], q, n),
                                                  col_major(bank[bk][:, t0:t0 + n], q, n), scale_of(m, g),
                                                  row_major(x[:, m, t0:t0 + n], q, n), ALU.mult, ALU.add)
                last.then_inc(x_ready, 1)

            def ffn_out(f, ada=None, per=0):
                base = BASE[f"ffn_out{f}"]
                for b in range(2 * DC):
                    if b % 2:
                        m = b // 2
                        dve.wait_ge(w_used, base + b + 1)
                        update_x(m, None, m % 2, lambda m, g: halfgate[:, f, m, g:g + 1])
                        n_x[0] += 1
                        dve.wait_ge(x_ready, n_x[0])
                        V.sem_inc(drained, 2)
                    ahead(base + b)
                    if per == 2 or (per and b % 2):
                        ada_at(ada, b * per // 2)

            def mixer_out(name, layer, q):
                base = BASE[name]
                for b in range(DC):
                    dve.wait_ge(w_used, base + b + 1)
                    update_x(b, q, b % RING, lambda m, g: mod[:, layer, 5 * DC + m, g:g + 1])
                    n_x[0] += 1
                    dve.wait_ge(x_ready, n_x[0])
                    V.sem_inc(drained, 1)
                    ahead(base + b)

            n_x = [0]
            dve.wait_ge(small_loaded, 16)
            for n, j in enumerate(ADA_ORDER):
                if j >= ADA_PE:
                    if n < ADA_START // RING:
                        dve.wait_ge(crow_ready, 1)
                    dve.wait_ge(ada_first_loaded[n * RING // ADA_START], 16)
                    ada_block(ada_first[:, n, :], mod_all[:, j, :], j - ADA_PE, ada_by_dve, j - ADA_PE or None)
                if n == 7:
                    norm_stats(0)
            for n in range(RING):
                lo_of(n)
            dve.wait_ge(rgc_ready, 1)
            V.tensor_scalar(rgc[:, 7, :], rgc[:, 6, :], 1.0, None, ALU.add).then_inc(rgc_ready, 1)
            dve.wait_ge(csil_ready, 2)
            seq.step(V.tensor_tensor(wz_lo[:, :, :], wz, wz_hi[:, :, :].bitcast(F32), ALU.subtract))
            dve.wait_ge(rgc_ready, 3)
            seq.step(V.tensor_scalar(rgc[:, 9, :], rgc[:, 7, :], -1.0, None, ALU.add))
            seq.step(V.tensor_tensor(rgc[:, 9, :], rgc[:, 6, :], rgc[:, 9, :], ALU.subtract))
            seq.step(V.reciprocal(rgc[:, 10, :], rgc[:, 7, :]))
            seq.step(V.tensor_tensor(rgc[:, 9, :], rgc[:, 9, :], rgc[:, 10, :], ALU.mult))
            seq.step(V.tensor_tensor(rgc[:, 9, :], rgc[:, 9, :], rgc[:, 8, :], ALU.add))
            seq.step(V.tensor_scalar(rgc[:, 11, :], lam, -1.0, 0.0, ALU.mult, ALU.max))
            seq.step(V.tensor_tensor(rgc[:, 9, :], rgc[:, 9, :], rgc[:, 11, :], ALU.add))
            seq.step(V.tensor_scalar(rgc[:, 2, :], rgc[:, 9, :], -4.0, None, ALU.mult))
            V.tensor_scalar(rgc[:, 3, :], rgc[:, 9, :], -8.0, None, ALU.mult)
            V.tensor_scalar(rgc[:, 4, :], rgc[:, 9, :], 4.0, None, ALU.mult)
            V.tensor_scalar(rgc[:, 0:2, :], sm("gate_b").rearrange("p (a b) -> p a b", a=2), 0.5, None,
                            ALU.mult).then_inc(rgc_ready, 1)

            dve.wait_ge(ada_by_dve, ADA_START - ADA_PE)
            V.sem_inc(ada_used, ADA_START - ADA_PE)
            take_mods(0, ADA_PE, ADA_START, ada_ps)
            take_mods(ADA_PE, ADA_START, ADA_START)
            make_gain(0)
            norm_apply(0)
            n_ada = ADA_START
            ffn_in(0, n_ada)
            take_mods(n_ada, n_ada + ADA_IN, n_ada + ADA_IN)
            n_ada += ADA_IN
            make_halfgate(0)
            make_gain(1)
            ffn_out(0, n_ada, 2)
            take_mods(n_ada, n_ada + ADA_OUT, n_ada + ADA_OUT)
            n_ada += ADA_OUT
            make_gain(2)
            make_halfgate(1)

            for j in range(2):
                last = V.memset(xpad[:, j, :], 0.0)
            seq.step(last)
            norm(1)
            base = BASE["rg_in"]
            for b in range(2 * RC):
                m = b // 2
                if b % 2 == 0:
                    dve.wait_ge(xpad_ready, m + 1)
                    xr = xpad[:, m % 2, :]
                    seq.step(V.tensor_scalar(xc[:, m, :], xr[:, 0:XW], conv_w[:, m, 0:1], conv_b[:, m:m + 1],
                                             ALU.mult, ALU.add))
                    for k in range(1, CW):
                        ins = V.scalar_tensor_tensor(xc[:, m, :], xr[:, k:k + XW], conv_w[:, m, k:k + 1],
                                                     xc[:, m, :], ALU.mult, ALU.add)
                        if k < CW - 1:
                            seq.step(ins)
                        else:
                            ins.then_inc(conv_done, 1)
                    V.sem_inc(drained, 1)
                else:
                    dve.wait_ge(w_used, base + b + 1)
                    V.tensor_copy(gate[:, m, :], bank[b % RING][:, 0:T]).then_inc(drained, 1)
                    dve.wait_ge(xchi_ready, m + 1)
                    V.tensor_tensor(xc_lo[:, m, :], xc[:, m, :], xc_hi[:, m, :].bitcast(F32),
                                    ALU.subtract).then_inc(xc_ready, 1)
                ahead(base + b)
            base = BASE["rg_gates"]
            for b in range(4):
                half, dr = b // 2, b % 2
                for n in range(HALF):
                    m = half * HALF + n
                    c = b * HALF + n
                    dve.wait_ge(rg_act, c + 1)
                    dve.wait_ge(rg_a2, c + 1)
                    V.scalar_tensor_tensor(gix[:, n, :], gix[:, n, :], 1.0, xc[:, m, :], ALU.add, ALU.mult)
                    V.scalar_tensor_tensor(gv[:, n, :], gv[:, n, :], 1.0, tmp_b[:, c % 2, :], ALU.add,
                                           ALU.mult).then_inc(rg_dve, 1)
                ahead(base + b)
                dve.wait_ge(rg_sqrt, b + 1)
                seq.step(V.tensor_tensor(gix[:, :, :], gix[:, :, :], gv[:, :, :], ALU.mult))
                for n in range(HALF):
                    m = half * HALF + n
                    for t0, w, g in XGROUPS:
                        ini = 0.0 if g == 0 else h0[:, dr, m:m + 1]
                        if dr == 0:
                            sl = slice(t0, t0 + w)
                            out = yf[:, n, sl]
                        else:
                            sl = slice(t0 + w - 1, t0 - 1 if t0 else None, -1)
                            out = gv[:, n, sl]
                        last = V.tensor_tensor_scan(out, ga[:, n, sl], gix[:, n, sl], ini, ALU.mult, ALU.add)
                seq.step(last)
                mm = slice(half * HALF, (half + 1) * HALF)
                src = yf[:, :, TP - 1] if dr == 0 else gv[:, :, 0]
                cp = V.tensor_copy(rg_state[:, dr, mm], src)
                if dr == 0:
                    cp.then_inc(rg_y, 1)
                    continue
                seq.step(cp)
                if half == 0:
                    dve.wait_ge(gelu_ready, 1)
                for t0, w, g in XGROUPS:
                    last = V.tensor_tensor(yf[:, :, t0:t0 + w], yf[:, :, t0:t0 + w], gv[:, :, t0:t0 + w], ALU.add)
                seq.step(last)
                for (t0, w, g), c0 in zip(XGROUPS, (0, TP)):
                    last = V.tensor_tensor(gate[:, mm, c0:c0 + w], yf[:, :, t0:t0 + w], gate[:, mm, c0:c0 + w],
                                           ALU.mult)
                last.then_inc(rg_y, 1)
                dve.wait_ge(rg_yhi, half + 1)
                V.tensor_tensor(xc_lo[:, mm, 0:T], gate[:, mm, :], xc_hi[:, mm, 0:T].bitcast(F32),
                                ALU.subtract).then_inc(rg_yready, HALF)
            V.sem_inc(drained, 4)
            mixer_out("rg_out", 0, 1)

            norm(2)
            dve.wait_ge(crow_ready, 2)
            ffn_in(1, n_ada)
            take_mods(n_ada, n_ada + ADA_IN, n_ada + ADA_IN)
            n_ada += ADA_IN
            make_gain(3)
            make_halfgate(2)
            ffn_out(1, n_ada, 2)
            take_mods(n_ada, n_ada + ADA_OUT, n_ada + ADA_OUT)
            n_ada += ADA_OUT
            make_gain(4)
            norm(3)
            ffn_in(2)
            ffn_out(2, n_ada, 1)
            take_mods(n_ada, 2 * ADA_PER_LAYER, 2 * ADA_PER_LAYER)
            make_gain(5)
            make_halfgate(3)

            norm(4)
            dve.wait_ge(consts, 4)

            def take_qk(b):
                dve.wait_ge(w_used, BASE["gla_qk"] + b + 1)
                V.tensor_scalar(qk[:, b // 2, b % 2, :], bank[b % RING][:, 0:T], 1.0 if b % 2 else QSCALE, None,
                                ALU.mult).then_inc(drained, 1)

            for b in range(RING):
                take_qk(b)
                ahead(BASE["gla_qk"] + b)
            for hd in range(HEADS):
                take_qk(RING + hd)
                ahead(BASE["gla_qk"] + RING + hd)
                for dr in range(2):
                    u = 2 * hd + dr
                    dve.wait_ge(sp_ready, u + 1)
                    lg = tmp_b[:, dr, 0:T]
                    V.tensor_scalar(lg, bank[4 + dr][:, 0:T], gla_b[:, dr, hd:hd + 1], 0.0, ALU.add,
                                    ALU.min).then_inc(zz_drained, 1)
                    dve.wait_ge(zz_drained, u + 1)
                    seq.step(V.tensor_tensor(lg, lg, tmp_a[:, dr, 0:T], ALU.subtract))
                    back = slice(None, None, -1) if dr else slice(None)
                    V.tensor_tensor_scan(bcum[:, hd, dr, back], reset[:, :], lg[:, back], 0.0, ALU.mult,
                                         ALU.add).then_inc(b_ready, 1)
            dve.wait_ge(b_ready, 2 * HEADS)
            for j, (dr, t) in enumerate(((0, P - 1), (1, 0), (0, 2 * P - 1), (1, 2 * P))):
                last = V.tensor_scalar(bl[:, :, j], bcum[:, :, dr, t], 1.0 / TAU, None, ALU.mult)
            last.then_inc(bl_ready, 1)
            dve.wait_ge(masks_made, 1)

            def merge(n):
                hd, l = divmod(n, NLEV + 1)
                buf = score_buf[hd % 3]
                dve.wait_ge(s_done, n + 1)
                ps = bank[4 + n % 2][:, 0:T]
                if l == 0:
                    if hd == 3:
                        dve.wait_ge(o_done, 1)
                    V.tensor_scalar(buf, ps, 2.0, None, ALU.mult).then_inc(s_drained, 1)
                else:
                    dve.wait_ge(s_drained, n)
                    mask = masks[:, l - 1:l, :].to_broadcast([P, NT, P])
                    V.copy_predicated(buf.rearrange("p (a b) -> p a b", a=NT), mask,
                                      ps.rearrange("p (a b) -> p a b", a=NT)).then_inc(s_drained, 1)

            def states_before(hd):
                dve.wait_ge(u_done, hd + 1)
                dve.wait_ge(s0_loaded, 16)
                for j in range(2):
                    last = V.scalar_tensor_tensor(mst[:, j, :], s0[:, hd, j, :], ebl[:, hd, j:j + 1],
                                                  bank[2][:, j * DV:(j + 1) * DV], ALU.mult, ALU.add)
                last.then_inc(st_ready, 1)

            for s in range(2 * DC):
                if s - 1 in STATE_AT:
                    states_before(STATE_AT.index(s - 1))
                for n in (2 * s, 2 * s + 1):
                    hd, l = divmod(n, NLEV + 1)
                    if l:
                        k = hd * NLEV + l - 1
                        dve.wait_ge(e_ready, k + 1)
                        e = ebuf[:, k % 2, :, :]
                        V.tensor_tensor(e, e, qk[:, hd, :, :], ALU.mult).then_inc(qkt_ready, 1)
                    if n:
                        merge(n - 1)
                if s - 1 in TURN_AT:
                    hd = TURN_AT.index(s - 1)
                    dve.wait_ge(qe_ready, hd + 1)
                    qs = qk[:, hd, 0:1, TP:T].to_broadcast([P, 2, TS])
                    V.tensor_tensor(qfb[:, :, :], qfb[:, :, :], qs, ALU.mult).then_inc(q_ready, 1)
                if s in TURN_AT:
                    hd = TURN_AT.index(s)
                    dve.wait_ge(ei_ready, hd + 1)
                    k0 = qk[:, hd, 1:2, 0:P].to_broadcast([P, 2, P])
                    V.tensor_tensor(kbar[:, 0:2, :], kbar[:, 0:2, :], k0, ALU.mult)
                    k12 = qk[:, hd, 1, P:T].rearrange("p (a b) -> p a b", a=2)
                    V.tensor_tensor(kbar[:, 2:4, :], kbar[:, 2:4, :], k12, ALU.mult).then_inc(kbar_ready, 1)
                ahead(BASE["gla_v"] + s)
                if s == DC - 1:
                    dve.wait_ge(w_used, BASE["gla_r"])
                    for j in range(3, 6):
                        last = V.tensor_copy(vt[:, j // 2, 512 * (j % 2):512 * (j % 2) + 512], bank[V_BANKS[j]][:, :])
                    seq.step(last)
                    dve.wait_ge(v_copied, 1)
                    V.sem_inc(drained, DC)
            states_before(HEADS - 1)
            merge(4 * (NLEV + 1) - 1)
            dve.wait_ge(ostd, 1)
            seq.step(V.reciprocal(rstd[:, :], rstd[:, :]))

            def head_diag(hd):
                V.tensor_tensor(diags[hd % 2], ident.rearrange("p (a b) -> p a b", a=1).to_broadcast([P, NT, P]),
                                rstd[:, hd * NT:(hd + 1) * NT].rearrange("p (a b) -> p a b", b=1
                                                                         ).to_broadcast([P, NT, P]),
                                ALU.mult).then_inc(odiag, 1)

            head_diag(0)
            head_diag(1)
            dve.wait_ge(osr, 1)
            for hd in range(HEADS):
                dve.wait_ge(obc, hd + 1)
                for c in range(2):
                    last = V.scalar_tensor_tensor(qk[:, hd, c, :], qk[:, hd, c, :], gla_g[:, 2 * hd + c:2 * hd + c + 1],
                                                  bank[hd][:, 0:T], ALU.mult, ALU.mult)
                if hd + 2 < HEADS:
                    head_diag(hd + 2)
                seq.step(last)
                for c in range(2):
                    m = 2 * hd + c
                    V.tensor_tensor(sr[:, m, :], sr[:, m, :], qk[:, hd, c, :], ALU.mult).then_inc(og, 1)
                if hd == HEADS - 1:
                    dve.wait_ge(og, DC)
                    V.sem_inc(drained, DC)
                for m in (2 * hd, 2 * hd + 1):
                    dve.wait_ge(oghi, m + 1)
                    V.tensor_tensor(h_lo[:, m, :], sr[:, m, :], h_hi[:, m, :].bitcast(F32),
                                    ALU.subtract).then_inc(og_ready, 1)
            mixer_out("gla_out", 1, 4)

            norm(5)
            ffn_in(3)
            ffn_out(3)
            norm(6)


def lay_out(i):
    c_ = np.ascontiguousarray

    def cols(v):
        v = np.asarray(v)
        v = v.reshape(v.shape[:-1] + (v.shape[-1] // P, P))
        return c_(np.moveaxis(v, -1, 0))

    def m_tiles(w, m_first=None):
        k, n = w.shape
        return c_(w.reshape(k // P, P, n // P, P).transpose(2, 1, 0, 3).reshape(n // P, P, k))

    x = np.concatenate([i["x_prompt"][0], i["x_sample"][0]], axis=0)
    o = {"x": c_(x.reshape(T, DC, P).transpose(2, 1, 0))}
    pe_blocks = m_tiles(i["ada_w"][0][:, 0:ADA_PE * P])
    dve_blocks = np.swapaxes(i["ada_w"], 1, 2).reshape(2 * ADA_PER_LAYER, P, D)
    first = [pe_blocks[j] if j < ADA_PE else dve_blocks[j] for j in ADA_ORDER]
    o["ada_w"] = np.concatenate([np.stack(first), dve_blocks[ADA_START:]], axis=0)
    o["c_row"] = c_(np.stack([i["c_ctx"], i["c"][0]]).reshape(1, 2 * D))
    fi, fo = [], []
    for l in range(2):
        for j in range(2):
            w = i["ffn_w_in"][l, j].reshape(DC, P, 2, FC, P).transpose(3, 2, 1, 0, 4)
            fi.append(w.reshape(2 * FC, P, DC * P))
            w = i["ffn_w_out"][l, j].reshape(2, KH, P, DC, P).transpose(3, 0, 2, 1, 4)
            fo.append(w.reshape(2 * DC, P, WMAX))
    o["ffn_in"], o["ffn_out"] = c_(np.stack(fi)), c_(np.stack(fo))
    w = m_tiles(i["rg_w_in"][0]).reshape(2, RC, P, DC * P)
    o["rg_in"] = c_(np.stack([w[1], w[0]], axis=1).reshape(2 * RC, P, DC * P))
    g = np.stack([i["rg_w_a"][0], i["rg_w_i"][0]])
    g = g.reshape(2, 2, 2, HALF, P, P).transpose(2, 1, 4, 3, 0, 5)
    o["rg_gates"] = c_(g.reshape(4, P, RC * P))
    o["rg_out"] = m_tiles(i["rg_w_out"][0])
    w = i["gla_w_in"][0]
    qk = m_tiles(w[:, 0:1024]).reshape(2, HEADS, P, DC * P)
    o["gla_qk"] = c_(np.stack([qk[0], qk[1]], axis=1).reshape(2 * HEADS, P, DC * P))
    o["gla_v"] = c_(w[:, 1024:2048].reshape(DC, P, 1024))
    o["gla_r"] = m_tiles(w[:, 2048:3072])
    o["gla_out"] = m_tiles(i["gla_w_out"][0])
    o["s0"] = c_(i["state_gla"][0, 0].transpose(2, 1, 0, 3).reshape(P, HEADS * 2 * DV))
    g2 = np.zeros((2 * RANK, 2, HEADS * P), np.float32)
    for dr in range(2):
        g2[dr * RANK:(dr + 1) * RANK, dr] = i["gla_w_g2"][0, dr]
    o["wg2"] = g2
    t = np.arange(P)
    o["masks"] = c_(np.stack([(t[:, None] ^ t[None, :]) // s == 1 for s in LEVELS], axis=1).astype(np.float32)).reshape(P, NLEV * P)
    wz = w[:, 3072:3072 + 2 * RANK].reshape(DC, P, 2 * RANK).transpose(1, 0, 2)
    parts = {"c": np.stack([cols(i["c_ctx"]), cols(i["c"][0])], axis=-1), "ada_b": cols(i["ada_b"]),
             "norm_g": cols(i["norm_g"]), "final_g": cols(i["final_norm"]),
             "conv_w": np.swapaxes(cols(i["rg_conv_w"][0]), 1, 2), "conv_b": cols(i["rg_conv_b"][0]),
             "gate_b": np.stack([cols(i["rg_b_a"][0]), cols(i["rg_b_i"][0])], axis=1), "lam": cols(i["rg_lambda"][0]),
             "h0": cols(i["state_rglru"][0, 0]), "gla_b": cols(i["gla_b_g"][0]), "gla_g": cols(i["gla_norm"][0]),
             "wz": wz, "ident": np.eye(P, dtype=np.float32)}
    o["small"] = c_(np.concatenate([parts[k].reshape(P, -1) for k in SMALL], axis=1))
    return o


def kernel(**inputs):
    import concourse.bacc as _bacc
    from concourse.bass_utils import run_bass_kernel_spmd as _run

    arrays = lay_out({k: np.asarray(v) for k, v in inputs.items()})
    nc = _bacc.Bacc("TRN2", target_bir_lowering=False, num_devices=1)
    d = {k: nc.dram_tensor(f"in_{k}", v.shape, mybir.dt.from_np(v.dtype), kind="ExternalInput").ap()
         for k, v in arrays.items()}
    outs = {"y": (P, DC, T), "rg_state": (P, 2, RC), "gla_state": (HEADS, P, 2, DV)}
    for k, s in outs.items():
        d[k] = nc.dram_tensor(f"out_{k}", s, F32, kind="ExternalOutput").ap()
    build(nc, d)
    r = _run(nc, [{f"in_{k}": v for k, v in arrays.items()}], core_ids=[0]).results[0]
    y = r["out_y"].transpose(2, 1, 0).reshape(T, D)
    rg = r["out_rg_state"].transpose(1, 2, 0).reshape(1, 1, 2, DR)
    gla = r["out_gla_state"].transpose(2, 0, 1, 3).reshape(1, 1, 2, HEADS, P, DV)
    c_ = np.ascontiguousarray
    return c_(y[None, :TP]), c_(y[None, TP:]), c_(rg), c_(gla)
```

```python
from contextlib import ExitStack

import numpy as np

import concourse.bass as bass
from concourse import mybir

F32 = mybir.dt.float32
F32R = mybir.dt.float32r
U8 = mybir.dt.uint8
ACT = mybir.ActivationFunctionType
ALU = mybir.AluOpType

P = 128
D = 1024
DC = D // P
TP, TS = 128, 256
T = TP + TS
GROUPS = [(0, TP, 0), (TP, TS, 1)]
GRID_W = 64
ROWS = TS // GRID_W
EPS = 1e-6
N_MOD = 9
DF = 2816
FC = DF // P
DR = 1280
RC = DR // P
CW = 4
HEADS = 4
DV = 256
RANK = 16
TAU = 16.0
QSCALE = float(P) ** -0.5
NT = T // P
LEVELS = [64, 32, 16, 8, 4, 2, 1]
NLEV = len(LEVELS)

XPAD = 1 + TP + 2 + TS + 2
XW = TP + 2 + TS
XGROUPS = [(0, TP, 0), (TP + 2, TS, 1)]
HALF = RC // 2

RING = 4
KH = FC // 2
WMAX = KH * P
PHASES = [("ffn_in0", 2 * FC, DC * P), ("ffn_out0", 2 * DC, WMAX), ("rg_in", 2 * RC, DC * P),
          ("rg_gates", 4, RC * P), ("rg_out", DC, RC * P),
          ("ffn_in1", 2 * FC, DC * P), ("ffn_out1", 2 * DC, WMAX),
          ("ffn_in2", 2 * FC, DC * P), ("ffn_out2", 2 * DC, WMAX),
          ("gla_qk", DC, DC * P), ("gla_v", DC, DC * P), ("gla_r", DC, DC * P), ("gla_out", DC, DC * P),
          ("ffn_in3", 2 * FC, DC * P), ("ffn_out3", 2 * DC, WMAX)]
BASE, WIDTH, COUNT = {}, [], {}
for _name, _n, _w in PHASES:
    assert _n % RING == 0
    BASE[_name], COUNT[_name] = len(WIDTH), _n
    WIDTH += [_w] * _n
BLOCKS = len(WIDTH)

ADA_PER_LAYER = N_MOD * DC
ADA_START = 2 * DC
ADA_IN = FC + 2
ADA_OUT = 2 * DC
ADA_MIX, ADA_LEAD = DC, 2
assert ADA_START + 3 * (ADA_IN + ADA_OUT) + ADA_MIX == 2 * ADA_PER_LAYER
ADA_PE = 6
ADA_ORDER = [0, 1, 6, 7, 2, 8, 9, 10, 3, 4, 11, 12, 5, 13, 14, 15]
ADA_RING = 2

SMALL = {}
_at = 0
for _name, _w in [("c", 2 * DC), ("ada_b", 2 * ADA_PER_LAYER), ("norm_g", 6 * DC), ("final_g", DC),
                  ("conv_w", RC * CW), ("conv_b", RC), ("gate_b", 4 * RC), ("lam", 2 * RC), ("h0", 2 * RC),
                  ("gla_b", 2 * HEADS), ("gla_g", DC), ("wz", DC * 2 * RANK), ("ident", P)]:
    SMALL[_name] = (_at, _at + _w)
    _at += _w
SMALL_W = _at


def build(nc, d):
    ctx = ExitStack()

    def sb(name, shape, dt=F32, scope=None):
        return (scope or ctx).enter_context(nc.sbuf_tensor(name, shape, dt))

    def sem(name):
        return ctx.enter_context(nc.semaphore(name))

    with ctx:
        x = sb("x", [P, DC, T])
        raw = sb("raw", [P, RING, WMAX])
        w_hi_sb = sb("w_hi_sb", [P, RING, WMAX], F32R)
        w_lo_sb = sb("w_lo_sb", [P, RING, WMAX], F32R)
        ada_raw = sb("ada_raw", [P, ADA_RING, DC * P])
        small = sb("small", [P, SMALL_W])
        csil = sb("csil", [P, DC, 2])
        mod_all = sb("mod_all", [P, 2 * ADA_PER_LAYER, 2])
        mod = mod_all[:, :, :].rearrange("p (l j) c -> p l j c", l=2)
        mod_turn = sb("mod_turn", [P, 2, 2])
        gain = sb("gain", [P, 6, DC, 2])
        halfgate = sb("halfgate", [P, 4, DC, 2])
        ones = sb("ones", [P, P])
        eps = sb("eps", [P, 1])
        rgc = sb("rgc", [P, 12, 2 * RC])
        rg_state = sb("rg_state", [P, 2, RC])
        tmp_a = sb("tmp_a", [P, 2, XW])
        tmp_b = sb("tmp_b", [P, 2, XW])
        ss = sb("ss", [P, T])
        sq = sb("sq", [P, T])
        sq_last = sb("sq_last", [P, T])
        diag = sb("diag", [P, NT, P])
        rstd = sb("rstd", [P, HEADS * NT])
        hbuf_scope = ExitStack()
        h_hi = sb("h_hi", [P, DC, T], F32R, hbuf_scope)
        h_lo = sb("h_lo", [P, DC, T], F32R, hbuf_scope)
        ffn_scope = ExitStack()
        a_hi = sb("a_hi", [P, FC, T], F32R, ffn_scope)
        a_lo = sb("a_lo", [P, FC, T], F32R, ffn_scope)
        ffn_scope.close()
        first_scope = ExitStack()
        ada_first = sb("ada_first", [P, ADA_START, DC * P], F32, first_scope)
        first_scope.close()
        rg_scope = ExitStack()
        xc = sb("xc", [P, RC, XW], F32, rg_scope)
        xc_hi = sb("xc_hi", [P, RC, XW], F32R, rg_scope)
        xc_lo = sb("xc_lo", [P, RC, XW], F32R, rg_scope)
        gate = sb("gate", [P, RC, T], F32, rg_scope)
        rg_scope.close()
        gla_scope = ExitStack()
        qk = sb("qk", [P, HEADS, 2, T], F32, gla_scope)
        vt = sb("vt", [P, NT, HEADS * DV], F32, gla_scope)
        sr = sb("sr", [P, DC, T], F32, gla_scope)
        bcum = sb("bcum", [P, HEADS, 2, T], F32, gla_scope)
        ebuf = sb("ebuf", [P, 2, 2, T], F32, gla_scope)
        scores = sb("scores", [P, T], F32, gla_scope)
        qfb = sb("qfb", [P, 2, TS], F32, gla_scope)
        kbar = sb("kbar", [P, 4, P], F32, gla_scope)
        kbar_t = sb("kbar_t", [P, 4, P], F32, gla_scope)
        wg2 = sb("wg2", [2 * RANK, 2, HEADS * P], F32, gla_scope)
        gla_scope.close()
        hbuf_scope.close()
        rgb_scope = ExitStack()
        ga = sb("ga", [P, HALF, XW], F32, rgb_scope)
        gv = sb("gv", [P, HALF, XW], F32, rgb_scope)
        gix = sb("gix", [P, HALF, XW], F32, rgb_scope)
        rgb_scope.close()
        out_scope = ExitStack()
        y_out = sb("y_out", [P, DC, T], F32, out_scope)
        out_scope.close()
        mask_in = y_out[:, :, :].rearrange("p m t -> p (m t)")[:, 0:NLEV * P]
        sb("span_all", [P, 2 * DC * T + 2 * FC * T], F32, ctx)
        extra = sb("extra", [P, 2 * D], F32, ctx)
        crow = extra[:, :].rearrange("p (c k) -> p c k", c=2)
        xpad = extra[:, 0:2 * XPAD].rearrange("p (a b) -> p a b", a=2)
        yf = extra[:, 0:HALF * XW].rearrange("p (n t) -> p n t", n=HALF)
        pst = extra[:, 0:2 * DV].rearrange("p (a b) -> p a b", a=2)
        mst = extra[:, 2 * DV:4 * DV].rearrange("p (a b) -> p a b", a=2)
        at = 4 * DV
        bl = extra[:, at:at + 4 * HEADS].rearrange("p (h j) -> p h j", h=HEADS)
        ebl = extra[:, at + 4 * HEADS:at + 6 * HEADS].rearrange("p (h j) -> p h j", h=HEADS)
        at += 6 * HEADS
        zT = extra[0:2 * RANK, at:at + T]
        masks = sb("masks", [P, NLEV, P], U8, ctx)
        reset = sb("reset", [P, T], F32, ctx)
        WZ = (DC - 1) * 2 * RANK + P
        wz_hi = sb("wz_hi", [P, WZ], F32R, ctx)
        wz_lo = sb("wz_lo", [P, WZ], F32R, ctx)

        bank = [ctx.enter_context(nc.psum_tensor(f"bank{i}", [P, 512], F32)) for i in range(4)]
        wide = ctx.enter_context(nc.psum_tensor("wide", [P, 1024], F32))
        bank += [wide[:, 0:512], wide[:, 512:1024]]
        bank += [ctx.enter_context(nc.psum_tensor(f"bank{i}", [P, 512], F32)) for i in (6, 7)]
        ada_ps = bank[7][:, 0:2 * ADA_PE].rearrange("p (j c) -> p j c", c=2)
        sum_ps = bank[6][:, 0:NT]
        rinv = bank[6][:, P:P + T]

        def sm(name):
            a, b = SMALL[name]
            return small[:, a:b]

        csm = sm("c").rearrange("p (k c) -> p k c", c=2)
        ada_b = sm("ada_b")
        norm_g = sm("norm_g").rearrange("p (n k) -> p n k", k=DC)
        final_g = sm("final_g")
        conv_w = sm("conv_w").rearrange("p (m k) -> p m k", k=CW)
        conv_b = sm("conv_b")
        lam = sm("lam")
        h0 = sm("h0").rearrange("p (d m) -> p d m", d=2)
        gla_b = sm("gla_b").rearrange("p (d h) -> p d h", d=2)
        gla_g = sm("gla_g")
        wz = small[:, SMALL["wz"][0]:SMALL["wz"][0] + WZ]
        ident = sm("ident")
        hb = rgc[:, 0:2, :]
        cc, cc2, ncc = rgc[:, 2, :], rgc[:, 3, :], rgc[:, 4, :]
        s0 = ada_raw[:, :, :].rearrange("p a b -> p (a b)").rearrange("p (h d v) -> p h d v", h=HEADS, d=2)

        small_loaded = sem("small_loaded")
        masks_loaded = sem("masks_loaded")
        masks_made = sem("masks_made")
        wg2_loaded = sem("wg2_loaded")
        x_loaded = sem("x_loaded")
        s0_loaded = sem("s0_loaded")
        out_done = sem("out_done")
        w_loaded = [sem(f"w_loaded{s}") for s in range(RING)]
        w_hi = sem("w_hi")
        w_split = sem("w_split")
        w_used = sem("w_used")
        drained = sem("drained")
        ada_loaded = [sem(f"ada_loaded{s}") for s in range(ADA_RING)]
        ada_first_loaded = [sem(f"ada_first_loaded{s}") for s in range(RING)]
        ada_used = sem("ada_used")
        csil_ready = sem("csil_ready")
        ada_half = sem("ada_half")
        ada_by_dve = sem("ada_by_dve")
        turn_taken = sem("turn_taken")
        crow_loaded = sem("crow_loaded")
        crow_ready = sem("crow_ready")
        consts = sem("consts")
        mods_ready = sem("mods_ready")
        x_ready = sem("x_ready")
        pool_seq = sem("pool_seq")
        dve_seq = sem("dve_seq")
        act_seq = sem("act_seq")
        ss_ready = sem("ss_ready")
        sum_done = sem("sum_done")
        std_ready = sem("std_ready")
        sq_ready = sem("sq_ready")
        diag_ready = sem("diag_ready")
        rinv_ready = sem("rinv_ready")
        y_ready = sem("y_ready")
        hhi_ready = sem("hhi_ready")
        h_ready = sem("h_ready")
        silu_ready = sem("silu_ready")
        ahi_ready = sem("ahi_ready")
        a_ready = sem("a_ready")
        xpad_ready = sem("xpad_ready")
        conv_done = sem("conv_done")
        xchi_ready = sem("xchi_ready")
        xc_ready = sem("xc_ready")
        gate_done = sem("gate_done")
        gate_drained = sem("gate_drained")
        rg_act = sem("rg_act")
        rg_dve = sem("rg_dve")
        rg_sqrt = sem("rg_sqrt")
        rg_in_ready = sem("rg_in_ready")
        rg_scanned = sem("rg_scanned")
        rg_back = sem("rg_back")
        rg_sum = sem("rg_sum")
        rg_yc = sem("rg_yc")
        rg_yhi = sem("rg_yhi")
        rg_yready = sem("rg_yready")
        rgc_ready = sem("rgc_ready")
        gelu_ready = sem("gelu_ready")
        z_done = sem("z_done")
        z_copied = sem("z_copied")
        zz_done = sem("zz_done")
        sp_ready = sem("sp_ready")
        zz_drained = sem("zz_drained")
        b_ready = sem("b_ready")
        v_copied = sem("v_copied")
        d_ready = sem("d_ready")
        e_ready = sem("e_ready")
        qkt_ready = sem("qkt_ready")
        s_done = sem("s_done")
        s_drained = sem("s_drained")
        bl_ready = sem("bl_ready")
        ei_ready = sem("ei_ready")
        kbar_ready = sem("kbar_ready")
        rg_a = sem("rg_a")
        rg_a2 = sem("rg_a2")
        qe_ready = sem("qe_ready")
        q_ready = sem("q_ready")
        odiag = sem("odiag")
        obc = sem("obc")
        kt_done = sem("kt_done")
        kt_copied = sem("kt_copied")
        u_done = sem("u_done")
        u_copied = sem("u_copied")
        st_ready = sem("st_ready")
        o_done = sem("o_done")
        o_copied = sem("o_copied")
        r_copied = sem("r_copied")
        state_out = sem("state_out")
        osum = sem("osum")
        osum_done = sem("osum_done")
        ostd = sem("ostd")
        osr = sem("osr")
        osg = sem("osg")
        og = sem("og")
        oghi = sem("oghi")
        og_ready = sem("og_ready")

        class Seq:

            def __init__(self, eng, s):
                self.eng, self.s, self.n, self.i, self.per = eng, s, 0, None, 0

            def value(self):
                return self.n if self.i is None else self.i * self.per + self.n

            def mark(self, ins):
                ins.then_inc(self.s, 1)
                self.n += 1

            def wait(self):
                self.eng.wait_ge(self.s, self.value())

            def step(self, ins):
                self.mark(ins)
                self.wait()

        NORMS = [("ffn_in0", 0), ("rg_in", 1), ("ffn_in1", 2), ("ffn_in2", 3), ("gla_qk", 4), ("ffn_in3", 5)]

        def layer_of(q):
            return q // 3, q % 3

        def col_major(ap, q, n):
            if q == 4 and n == TS:
                return ap.rearrange("p (w r) -> p r w", w=GRID_W)
            return ap

        def row_major(ap, q, n):
            if q == 4 and n == TS:
                return ap.rearrange("p (r w) -> p r w", r=ROWS)
            return ap

        ZZ_AT = [(0, 1, 2, 3), (4, 5), (6, 7), ()]
        zz_tmp = [tmp_a[:, 0, 0:T], tmp_a[:, 1, 0:T], ss[:, :], sq[:, :]]
        V_BANKS = [0, 1, 2, 3, 6, 7]
        TURN_AT, STATE_AT, OUT_AT, SUM_AT = [8, 10, 12, 14], [9, 11, 13, 15], [10, 12, 14], [12, 14]
        score_buf = [tmp_b[:, 0, 0:T], tmp_b[:, 1, 0:T], scores[:, :]]
        osum_ps = bank[1][:, T:T + HEADS * NT]
        diags = [diag[:, :, :]] + [b[:, :].rearrange("p (a b) -> p a b", a=NT) for b in (sq_last, ss, sq)]

        block = ctx.enter_context(nc.Block())

        @block.sync
        def _(sp):
            def load_block(src, i, b):
                s = b % RING
                sp.dma_start(raw[:, s, 0:src.shape[2]],
                             src[bass.ds(RING * i + b, 1)].rearrange("a p k -> p (a k)")).then_inc(w_loaded[s], 16)

            def phase(name, src):
                base = BASE[name]
                start = 0 if base else 1
                with sp.Fori(start, COUNT[name] // RING) as i:
                    for b in range(RING):
                        sp.wait_ge(w_split, RING * i + (base + b - RING + 1))
                        load_block(src, i, b)

            sp.dma_start(small[:, :], d["small"]).then_inc(small_loaded, 16)
            sp.dma_start(extra[:, :], d["c_row"].to_broadcast([P, 2 * D])).then_inc(crow_loaded, 16)
            per = ADA_START // RING
            for s in range(RING):
                if s == 1:
                    sp.dma_start(x[:, :, :], d["x"]).then_inc(x_loaded, 16)
                sp.dma_start(ada_first[:, per * s:per * s + per, :],
                             d["ada_w"][per * s:per * s + per].rearrange("a p k -> p a k")
                             ).then_inc(ada_first_loaded[s], 16)
            for b in range(RING):
                load_block(d["ffn_in"][0], 0, b)
            phase("ffn_in0", d["ffn_in"][0])
            phase("ffn_out0", d["ffn_out"][0])
            for name in ("rg_in", "rg_gates", "rg_out"):
                phase(name, d[name])
            sp.wait_ge(rg_yc, RC)
            sp.dma_start(extra[:, :], d["c_row"].to_broadcast([P, 2 * D])).then_inc(crow_loaded, 16)
            for f in (1, 2):
                phase(f"ffn_in{f}", d["ffn_in"][f])
                phase(f"ffn_out{f}", d["ffn_out"][f])
            for name in ("gla_qk", "gla_v", "gla_r", "gla_out"):
                phase(name, d[name])
                if name == "gla_qk":
                    sp.wait_ge(ada_used, 2 * ADA_PER_LAYER)
                    sp.dma_start(ada_raw[:, :, :].rearrange("p a b -> p (a b)"), d["s0"]).then_inc(s0_loaded, 16)
            phase("ffn_in3", d["ffn_in"][3])
            phase("ffn_out3", d["ffn_out"][3])
            for m in range(DC):
                sp.wait_ge(h_ready, 8 * 6 + m + 1)
                sp.dma_start(d["y"][:, m, :], y_out[:, m, :]).then_inc(out_done, 16)
            sp.wait_ge(out_done, 16 * DC)
            sp.wait_ge(state_out, 16 * (HEADS + 1))

        @block.gpsimd
        def _(pool):
            seq = Seq(pool, pool_seq)
            pool.memset(ones[:, :], 1.0).then_inc(consts, 1)
            pool.memset(eps[:, :], EPS).then_inc(consts, 1)
            pool.memset(reset[:, :], 1.0).then_inc(consts, 1)
            pool.wait_ge(consts, 3)
            pool.memset(reset[:, :].rearrange("p (n t) -> p n t", t=P)[:, :, 0:1], 0.0).then_inc(consts, 1)

            def ada_run(first, n):
                with pool.Fori(0, n // ADA_RING) as i:
                    for b in range(ADA_RING):
                        pool.wait_ge(ada_used, ADA_RING * i + (first + b - ADA_RING + 1))
                        pool.wait_ge(consts, 1)
                        pool.dma_start(ada_raw[:, b, :],
                                       d["ada_w"][bass.ds(ADA_RING * i + (first + b), 1)].rearrange("a p k -> p (a k)")
                                       ).then_inc(ada_loaded[b], 16)

            def ada_load(n):
                pool.wait_ge(ada_used, n - ADA_RING + 1)
                pool.dma_start(ada_raw[:, n % ADA_RING, :], d["ada_w"][n]).then_inc(ada_loaded[n % ADA_RING], 16)

            def sum_squares(q, ada=None, per=0, lead=0):
                if q == 0:
                    pool.wait_ge(x_loaded, 16)
                for n in range(per + lead):
                    ada_load(ada + n)
                for m in range(DC - 1):
                    for n in range(per * (m + 1) + lead, min(per * (m + 2) + lead, per * DC)):
                        ada_load(ada + n)
                    if q:
                        pool.wait_ge(x_ready, DC * (q - 1) + m + 1)
                    if m == 0:
                        if q:
                            pool.wait_ge(sum_done, q)
                        seq.step(nc.gpsimd.tensor_tensor(ss[:, :], x[:, m, :], x[:, m, :], ALU.mult))
                        continue
                    seq.step(nc.gpsimd.tensor_tensor(sq[:, :], x[:, m, :], x[:, m, :], ALU.mult))
                    add = nc.gpsimd.tensor_tensor(ss[:, :], ss[:, :], sq[:, :], ALU.add)
                    if m == DC - 2:
                        add.then_inc(ss_ready, 1)
                    else:
                        seq.step(add)

            sum_squares(0)
            n_ada = ADA_START
            for f in (0, 1, 2):
                ada_run(n_ada, ADA_IN)
                n_ada += ADA_IN
                sum_squares(f + 1 if f == 0 else f + 2, n_ada, ADA_OUT // DC)
                n_ada += ADA_OUT
                if f == 0:
                    for c in range(2 * RC):
                        pool.wait_ge(rg_a, c + 1)
                        n = c % HALF
                        nc.gpsimd.tensor_tensor(gv[:, n, :], ga[:, n, :], ga[:, n, :], ALU.mult).then_inc(rg_a2, 1)
                    sum_squares(2, n_ada, ADA_MIX // DC, ADA_LEAD)
                    n_ada += ADA_MIX

            def squares(hd):
                pool.wait_ge(o_copied, hd + 1)
                if hd:
                    pool.wait_ge(osum_done, hd)
                nc.gpsimd.tensor_tensor(ss[:, :], qk[:, hd, 0, :], qk[:, hd, 0, :], ALU.mult)
                nc.gpsimd.tensor_tensor(sq[:, :], qk[:, hd, 1, :], qk[:, hd, 1, :], ALU.mult).then_inc(osum, 1)

            for hd in range(HEADS):
                pool.wait_ge(b_ready, 2 * hd + 2)
                if hd == HEADS - 1:
                    squares(0)
                for l, s in enumerate(LEVELS):
                    n = hd * NLEV + l
                    if hd == HEADS - 1 and l == 3:
                        squares(1)
                    if n >= 2:
                        pn = n - 2
                        pool.wait_ge(s_done, pn // NLEV * (NLEV + 1) + pn % NLEV + 2)
                    f, b = (bcum[:, hd, j, :].rearrange("p (n h s) -> p n h s", h=2, s=s) for j in range(2))
                    eq, ek = (ebuf[:, n % 2, j, :].rearrange("p (n h s) -> p n h s", h=2, s=s) for j in range(2))
                    nb = T // (2 * s)
                    ref_f = f[:, :, 0, s - 1:s].to_broadcast([P, nb, s])
                    ref_b = b[:, :, 1, 0:1].to_broadcast([P, nb, s])
                    nc.gpsimd.tensor_tensor(eq[:, :, 1, :], f[:, :, 1, :], ref_f, ALU.subtract)
                    nc.gpsimd.tensor_tensor(eq[:, :, 0, :], b[:, :, 0, :], ref_b, ALU.subtract)
                    nc.gpsimd.tensor_tensor(ek[:, :, 0, :], ref_f, f[:, :, 0, :], ALU.subtract)
                    nc.gpsimd.tensor_tensor(ek[:, :, 1, :], ref_b, b[:, :, 1, :], ALU.subtract).then_inc(d_ready, 1)
            for hd in range(2, HEADS):
                squares(hd)
            for q in (5, 6):
                sum_squares(q)

        @block.tensor
        def _(pe):
            def tile(out, slot, ks, hi, lo, start, stop, at=0):
                for j, k in enumerate(ks):
                    w = slice((at + j) * P, (at + j + 1) * P)
                    pe.matmul(out, w_hi_sb[:, slot, w], hi[k], start=start and j == 0, stop=False)
                    pe.matmul(out, w_hi_sb[:, slot, w], lo[k], start=False, stop=False)
                    last = pe.matmul(out, w_lo_sb[:, slot, w], hi[k], start=False,
                                     stop=stop and j == len(ks) - 1)
                return last

            h_chunks = ([h_hi[:, k, :] for k in range(DC)], [h_lo[:, k, :] for k in range(DC)])
            a_chunks = ([a_hi[:, k, :] for k in range(FC)], [a_lo[:, k, :] for k in range(FC)])
            y_chunks = ([xc_hi[:, k, 0:T] for k in range(RC)], [xc_lo[:, k, 0:T] for k in range(RC)])

            def norm_sums(q):
                pe.wait_ge(ss_ready, q + 1)
                if q == 0:
                    pe.wait_ge(consts, 1)
                pe.wait_ge(sq_ready, q + 1)
                for t in range(NT):
                    tok = slice(t * P, (t + 1) * P)
                    pe.matmul(sum_ps[:, t:t + 1], ss[:, tok], ones[:, 0:1], start=True, stop=False)
                    last = pe.matmul(sum_ps[:, t:t + 1], sq_last[:, tok], ones[:, 0:1], start=False, stop=True)
                last.then_inc(sum_done, 1)

            def norm(q):
                if q:
                    norm_sums(q)
                pe.wait_ge(diag_ready, q + 1)
                pe.matmul(rinv, ones[:, :], diag[:, :, :].rearrange("p a b -> p (a b)"), start=True,
                          stop=True).then_inc(rinv_ready, 1)

            def arriving(base, ks, chunks, hi_ready, ready, n0, early=5):
                for b in range(RING):
                    pe.wait_ge(w_split, base + b + 1)
                for k in range(early):
                    w = slice(k * P, (k + 1) * P)
                    pe.wait_ge(hi_ready, n0 + k + 1)
                    for b in range(RING):
                        pe.matmul(bank[b][:, 0:T], w_hi_sb[:, b, w], chunks[0][k], start=k == 0, stop=False)
                        pe.matmul(bank[b][:, 0:T], w_lo_sb[:, b, w], chunks[0][k], start=False, stop=False)
                    pe.wait_ge(ready, n0 + k + 1)
                    for b in range(RING):
                        pe.matmul(bank[b][:, 0:T], w_hi_sb[:, b, w], chunks[1][k], start=False, stop=False)
                pe.wait_ge(ready, n0 + len(ks))
                for b in range(RING):
                    tile(bank[b][:, 0:T], b, ks[early:], *chunks, False, True, early).then_inc(w_used, 1)

            def one_tile_blocks(name, chunks, ks, hi_ready, ready, n0, early=5):
                base, n = BASE[name], COUNT[name]
                if base:
                    pe.wait_ge(drained, base)
                arriving(base, ks, chunks, hi_ready, ready, n0, early)
                with pe.Fori(1, n // RING) as i:
                    for b in range(RING):
                        pe.wait_ge(drained, RING * i + (base + b - RING + 1))
                        pe.wait_ge(w_split, RING * i + (base + b + 1))
                        tile(bank[b][:, 0:T], b, ks, *chunks, True, True).then_inc(w_used, 1)

            def ffn_out(f):
                base, n = BASE[f"ffn_out{f}"], COUNT[f"ffn_out{f}"]
                with pe.Fori(0, n // RING) as i:
                    for b in range(RING):
                        half, t = b % 2, b // 2
                        if half == 0:
                            pe.wait_ge(drained, RING * i + (base + b - 2))
                        if b == 1:
                            pe.wait_ge(a_ready, FC * (f + 1))
                        pe.wait_ge(w_split, RING * i + (base + b + 1))
                        tile(bank[t][:, 0:T], b, range(KH * half, KH * half + KH), *a_chunks,
                             half == 0, half == 1).then_inc(w_used, 1)

            def ffn(f, q):
                norm(q)
                one_tile_blocks(f"ffn_in{f}", h_chunks, range(DC), hhi_ready, h_ready, DC * q)
                pe.wait_ge(a_ready, FC * f + KH)
                ffn_out(f)

            pe.wait_ge(csil_ready, 1)
            for n, j in enumerate(ADA_ORDER):
                if n == ADA_START - ADA_START // RING:
                    norm_sums(0)
                if j < ADA_PE:
                    pe.wait_ge(ada_first_loaded[n * RING // ADA_START], 16)
                    for k in range(DC):
                        last = pe.matmul(ada_ps[:, j, :], ada_first[:, n, k * P:(k + 1) * P], csil[:, k, :],
                                         start=k == 0, stop=k == DC - 1)
                    last.then_inc(ada_used, 1)
            ffn(0, 0)

            norm(1)
            one_tile_blocks("rg_in", h_chunks, range(DC), hhi_ready, h_ready, DC)
            base = BASE["rg_gates"]
            pe.wait_ge(drained, base)
            pe.wait_ge(xc_ready, RC)
            for b in range(4):
                pe.wait_ge(w_split, base + b + 1)
                for t in range(RC):
                    g = b * RC + t
                    m = (b // 2) * HALF + t // 2
                    if g >= RING:
                        pe.wait_ge(gate_drained, g - RING + 1)
                    last = tile(bank[g % RING][:, 0:XW], b, [0], [xc_hi[:, m, :]], [xc_lo[:, m, :]], True, True, t)
                    last.then_inc(w_used if t == RC - 1 else gate_done, 1)
            one_tile_blocks("rg_out", y_chunks, range(RC), rg_yhi, rg_yready, 0, RC - 1)

            ffn(1, 2)
            ffn(2, 3)

            norm(4)
            base = BASE["gla_qk"]
            pe.wait_ge(drained, base)
            arriving(base, range(DC), h_chunks, hhi_ready, h_ready, DC * 4)
            for k in range(DC):
                w = slice(2 * RANK * k, 2 * RANK * k + P)
                pe.matmul(bank[4][:, 0:T], wz_hi[:, w], h_hi[:, k, :], start=k == 0, stop=False)
                pe.matmul(bank[4][:, 0:T], wz_hi[:, w], h_lo[:, k, :], start=False, stop=False)
                last = pe.matmul(bank[4][:, 0:T], wz_lo[:, w], h_hi[:, k, :], start=False, stop=k == DC - 1)
            last.then_inc(z_done, 1)
            for b in range(RING, DC):
                pe.wait_ge(drained, base + b - RING + 1)
                pe.wait_ge(w_split, base + b + 1)
                tile(bank[b % RING][:, 0:T], b % RING, range(DC), *h_chunks, True, True).then_inc(w_used, 1)
                if b == RING:
                    pe.wait_ge(z_copied, 1)
                    pe.wait_ge(wg2_loaded, 16)
                for u in ZZ_AT[b - RING]:
                    hd, dr = u // 2, u % 2
                    if u >= 4:
                        pe.wait_ge(zz_drained, u - 3)
                    pe.matmul(bank[4 + u % 4][:, 0:T], wg2[:, dr, hd * P:(hd + 1) * P], zT, start=True,
                              stop=True).then_inc(zz_done, 1)

            def value_block(b):
                base = BASE["gla_v"]
                pe.wait_ge(w_split, base + b + 1)
                if b == 0:
                    pe.wait_ge(drained, base)
                s = b % RING
                for t in range(NT):
                    tok = slice(t * P, (t + 1) * P)
                    if b == 0 and t == NT - 1:
                        pe.wait_ge(zz_drained, 2 * HEADS)
                    for half in range(2):
                        out = bank[V_BANKS[2 * t + half]][:, :]
                        c = slice(512 * half, 512 * half + 512)
                        pe.matmul(out, h_hi[:, b, tok], w_hi_sb[:, s, c], start=b == 0, stop=False)
                        pe.matmul(out, h_hi[:, b, tok], w_lo_sb[:, s, c], start=False, stop=False)
                        last = pe.matmul(out, h_lo[:, b, tok], w_hi_sb[:, s, c], start=False, stop=b == DC - 1)
                last.then_inc(w_used, 1)

            def r_block(b):
                n = BASE["gla_r"] + b
                if b < 2:
                    pe.wait_ge(drained, BASE["gla_r"])
                else:
                    pe.wait_ge(r_copied, b - 1)
                pe.wait_ge(w_split, n + 1)
                tile(bank[b % 2][:, 0:T], b % RING, range(DC), *h_chunks, True, True).then_inc(w_used, 1)

            def level(n):
                hd, l = divmod(n, NLEV + 1)
                if n >= 2:
                    pe.wait_ge(s_drained, n - 1)
                else:
                    pe.wait_ge(zz_drained, 2 * HEADS)
                if l:
                    pe.wait_ge(qkt_ready, hd * NLEV + l)
                    e = ebuf[:, (hd * NLEV + l - 1) % 2, :, :]
                else:
                    e = qk[:, hd, :, :]
                for t in range(NT):
                    tok = slice(t * P, (t + 1) * P)
                    last = pe.matmul(bank[4 + n % 2][:, tok], e[:, 1, tok], e[:, 0, tok], start=True, stop=True)
                last.then_inc(s_done, 1)

            def turn_keys(hd):
                pe.wait_ge(kbar_ready, hd + 1)
                if hd:
                    pe.wait_ge(st_ready, hd)
                for j in range(4):
                    last = pe.transpose(bank[2][:, j * P:(j + 1) * P], kbar[:, j, :], ident)
                last.then_inc(kt_done, 1)

            def chunk_states(hd):
                pe.wait_ge(kt_copied, hd + 1)
                if hd:
                    pe.wait_ge(u_copied, hd)
                for j, t in enumerate((0, 0, 1, 2)):
                    last = pe.matmul(bank[3 - j // 2][:, (j % 2) * DV:(j % 2 + 1) * DV], kbar_t[:, j, :],
                                     vt[:, t, hd * DV:(hd + 1) * DV], start=True, stop=True)
                last.then_inc(u_done, 1)

            def outputs(hd):
                pe.wait_ge(st_ready, hd + 1)
                pe.wait_ge(q_ready, hd + 1)
                pe.wait_ge(s_drained, (hd + 1) * (NLEV + 1))
                if hd:
                    pe.wait_ge(o_copied, hd)
                for c in range(2):
                    vc = slice(hd * DV + c * P, hd * DV + (c + 1) * P)
                    cs = slice(c * P, (c + 1) * P)
                    for t in range(NT):
                        tok = slice(t * P, (t + 1) * P)
                        out = bank[6 + c][:, tok]
                        last = pe.matmul(out, vt[:, t, vc], score_buf[hd % 3][:, tok], start=True, stop=t == 0)
                        if t:
                            stok = slice((t - 1) * P, t * P)
                            sf = s0[:, hd, 0, cs] if t == 1 else mst[:, 0, cs]
                            sbk = s0[:, hd, 1, cs] if t == 2 else mst[:, 1, cs]
                            pe.matmul(out, sf, qfb[:, 0, stok], start=False, stop=False)
                            last = pe.matmul(out, sbk, qfb[:, 1, stok], start=False, stop=True)
                last.then_inc(o_done, 1)

            def output_sums(hd, r_blocks):
                pe.wait_ge(osum, hd + 1)
                pe.wait_ge(r_copied, r_blocks // 2 * 2)
                for t in range(NT):
                    tok = slice(t * P, (t + 1) * P)
                    out = osum_ps[:, hd * NT + t:hd * NT + t + 1]
                    pe.matmul(out, ss[:, tok], ones[:, 0:1], start=True, stop=False)
                    last = pe.matmul(out, sq[:, tok], ones[:, 0:1], start=False, stop=True)
                last.then_inc(osum_done, 1)

            for s in range(2 * DC):
                if s < DC:
                    value_block(s)
                else:
                    r_block(s - DC)
                level(2 * s)
                level(2 * s + 1)
                if s == DC + 1:
                    pe.wait_ge(s0_loaded, 16)
                if s in OUT_AT:
                    outputs(OUT_AT.index(s))
                if s in SUM_AT:
                    output_sums(SUM_AT.index(s), s - DC + 1)
                if s in TURN_AT:
                    turn_keys(TURN_AT.index(s))
                if s in STATE_AT:
                    chunk_states(STATE_AT.index(s))
            outputs(HEADS - 1)
            for hd in range(len(SUM_AT), HEADS):
                output_sums(hd, DC)
            for hd in range(HEADS):
                pe.wait_ge(odiag, hd + 1)
                if hd == 0:
                    pe.wait_ge(o_copied, HEADS)
                    pe.wait_ge(u_copied, HEADS)
                pe.matmul(bank[4 + hd][:, 0:T], ones[:, :], diags[hd].rearrange("p a b -> p (a b)"), start=True,
                          stop=True).then_inc(obc, 1)
            one_tile_blocks("gla_out", h_chunks, range(DC), oghi, og_ready, 0)

            ffn(3, 5)
            norm(6)

        @block.scalar
        def _(act):
            A = nc.scalar.activation
            seq = Seq(act, act_seq)

            def hi_of(n, i=None, per=0):
                s = n % RING
                off = 0 if i is None else i
                act.wait_ge(w_loaded[s], off * 16 + 16 * (n // RING + 1))
                if i is not None or n >= RING:
                    act.wait_ge(w_used, off * RING + (n - RING + 1))
                w = WIDTH[n]
                A(w_hi_sb[:, s, 0:w], raw[:, s, 0:w], ACT.Copy).then_inc(w_hi, 1)

            def ahead(n):
                if n + RING < BLOCKS:
                    hi_of(n + RING)

            def norm_stats(q):
                if q == 0:
                    act.wait_ge(x_loaded, 16)
                    act.wait_ge(consts, 2)
                else:
                    act.wait_ge(x_ready, DC * q)
                A(sq_last[:, :], x[:, DC - 1, :], ACT.Square).then_inc(sq_ready, 1)
                nc.scalar.preload_act_table_set("sqrt_and_others")
                act.wait_ge(sum_done, q + 1)
                A(rstd[:, 0:NT], sum_ps, ACT.Sqrt, bias=eps[:, :], scale=1.0 / D).then_inc(std_ready, 1)

            def norm_apply(q, tables):
                nc.scalar.preload_act_table_set(tables)
                layer, j = layer_of(q)
                for m in range(DC):
                    act.wait_ge(y_ready, DC * q + m + 1)
                    for t0, n, g in GROUPS:
                        shift = mod[:, layer, 3 * j * DC + m, g:g + 1]
                        last = A(col_major(h_hi[:, m, t0:t0 + n], q, n), row_major(tmp_a[:, m % 2, t0:t0 + n], q, n),
                                 ACT.Identity, bias=shift)
                    last.then_inc(hhi_ready, 1)

            def norm(q, tables):
                norm_stats(q)
                norm_apply(q, tables)

            def ffn_in(f):
                base = BASE[f"ffn_in{f}"]

                def turn(i):
                    off = 0 if i is None else i
                    for p in range(2):
                        pp = FC - 2 + p if i is None else p
                        act.wait_ge(w_used, off * RING + (base + 2 * pp + 1))
                        A(tmp_b[:, p, 0:T], bank[2 * p][:, 0:T], ACT.Silu).then_inc(silu_ready, 1)
                        for b in range(2):
                            if i is None:
                                ahead(base + 2 * pp + b)
                            else:
                                hi_of(base + 2 * p + b + RING, i)
                        act.wait_ge(drained, off * RING + (base + 2 * pp + 2))
                        act.wait_ge(consts, 1)
                        out = a_hi[:, pp, :] if i is None else \
                            a_hi[:, bass.ds(i * 2 + p, 1), :].rearrange("p a t -> p (a t)")
                        A(out, tmp_a[:, p, 0:T], ACT.Copy).then_inc(ahi_ready, 1)

                with act.Fori(0, FC // 2 - 1) as i:
                    turn(i)
                turn(None)

            def only_weights(name):
                for b in range(COUNT[name]):
                    ahead(BASE[name] + b)

            def copy_states(hd):
                act.wait_ge(u_done, hd + 1)
                if hd:
                    act.wait_ge(state_out, 16 * (hd + 1))
                A(pst[:, :, :], bank[3][:, :].rearrange("p (a b) -> p a b", a=2), ACT.Copy).then_inc(u_copied, 1)
                act.wait_ge(u_copied, hd + 1)
                act.dma_start(d["gla_state"][hd], pst[:, :, :]).then_inc(state_out, 16)

            def copy_outputs(hd):
                act.wait_ge(o_done, hd + 1)
                for c in range(2):
                    last = A(qk[:, hd, c, :], bank[6 + c][:, 0:T], ACT.Copy)
                last.then_inc(o_copied, 1)

            act.wait_ge(small_loaded, 16)
            A(csil[:, :, :], csm, ACT.Silu).then_inc(csil_ready, 1)
            act.wait_ge(crow_loaded, 16)
            A(crow, crow, ACT.Silu).then_inc(crow_ready, 1)
            norm_stats(0)
            for n in range(RING):
                hi_of(n)
            A(wz_hi[:, :], wz, ACT.Copy).then_inc(csil_ready, 1)
            act.dma_start(mask_in, d["masks"]).then_inc(masks_loaded, 16)
            act.wait_ge(masks_loaded, 16)
            A(masks[:, :, :], mask_in.rearrange("p (a b) -> p a b", a=NLEV), ACT.Copy).then_inc(masks_made, 1)
            act.wait_ge(masks_made, 1)
            norm_apply(0, "silu_and_others")
            ffn_in(0)
            A(rgc[:, 5, :], lam, ACT.Abs).then_inc(act_seq, 1)
            seq.n += 1
            seq.wait()
            A(rgc[:, 6, :], rgc[:, 5, :], ACT.Exp, scale=-1.0).then_inc(rgc_ready, 1)
            act.wait_ge(rgc_ready, 2)
            A(rgc[:, 8, :], rgc[:, 7, :], ACT.Ln).then_inc(rgc_ready, 1)
            only_weights("ffn_out0")

            norm(1, "gelu_apprx_tanh_and_others")
            base = BASE["rg_in"]
            for b in range(2 * RC):
                m = b // 2
                if b % 2 == 0:
                    act.wait_ge(w_used, base + b + 1)
                    if m >= 2:
                        act.wait_ge(conv_done, m - 1)
                    for (t0, n, _), at in zip(GROUPS, (1, 1 + TP + 2)):
                        last = A(xpad[:, m % 2, at:at + n], bank[b % RING][:, t0:t0 + n], ACT.Copy)
                    last.then_inc(xpad_ready, 1)
                else:
                    act.wait_ge(w_used, base + b + 1)
                    A(gate[:, m, :], bank[b % RING][:, 0:T], ACT.Gelu_apprx_tanh).then_inc(gelu_ready, 1)
                    act.wait_ge(conv_done, m + 1)
                    A(xc_hi[:, m, :], xc[:, m, :], ACT.Copy).then_inc(xchi_ready, 1)
                ahead(base + b)
            base = BASE["rg_gates"]
            act.wait_ge(rgc_ready, 4)

            def y_hi(m):
                act.wait_ge(rg_yc, m + 1)
                A(xc_hi[:, m, 0:T], gate[:, m, :], ACT.Copy).then_inc(rg_yhi, 1)

            for b in range(4):
                half, dr = b // 2, b % 2
                for n in range(HALF):
                    m = half * HALF + n
                    col = slice(dr * RC + m, dr * RC + m + 1)
                    c = b * HALF + n
                    if c >= 2:
                        act.wait_ge(rg_dve, c - 1)
                    for kind, out in ((0, tmp_a[:, c % 2, :]), (1, gix[:, n, :])):
                        g = b * RC + 2 * n + kind
                        if g % RC == RC - 1:
                            act.wait_ge(w_used, base + b + 1)
                        else:
                            act.wait_ge(gate_done, g - b + 1)
                        if b and kind == 0:
                            if dr:
                                act.wait_ge(rg_scanned, half * HALF + n + 1)
                            else:
                                act.wait_ge(rg_yc, n + 1)
                        A(out, bank[g % RING][:, 0:XW], ACT.Tanh, bias=rgc[:, kind, col],
                          scale=0.5).then_inc(gate_drained, 1)
                    act.wait_ge(gate_drained, b * RC + 2 * n + 1)
                    A(ga[:, n, :], tmp_a[:, c % 2, :], ACT.Exp, bias=rgc[:, 2, col],
                      scale=rgc[:, 2, col]).then_inc(rg_a, 1)
                    A(tmp_b[:, c % 2, :], tmp_a[:, c % 2, :], ACT.Tanh, bias=rgc[:, 4, col],
                      scale=rgc[:, 4, col]).then_inc(rg_act, 1)
                    if b == 2:
                        y_hi(n)
                if b == 3:
                    ahead(base + b)
                act.wait_ge(rg_dve, (b + 1) * HALF)
                A(gv[:, :, :], gv[:, :, :], ACT.Sqrt, scale=0.25).then_inc(rg_sqrt, 1)
                if b < 3:
                    ahead(base + b)
            for m in range(HALF, RC):
                y_hi(m)
            act.dma_start(d["rg_state"], rg_state[:, :, :]).then_inc(state_out, 16)
            act.wait_ge(crow_loaded, 32)
            A(crow, crow, ACT.Silu).then_inc(crow_ready, 1)
            only_weights("rg_out")

            norm(2, "silu_and_others")
            ffn_in(1)
            only_weights("ffn_out1")
            norm(3, "silu_and_others")
            ffn_in(2)
            only_weights("ffn_out2")

            act.wait_ge(x_ready, 4 * DC)
            act.dma_start(wg2[:, :, :], d["wg2"]).then_inc(wg2_loaded, 16)
            norm(4, "natural_log_exp_and_others")
            for b in range(RING):
                ahead(BASE["gla_qk"] + b)
            act.wait_ge(z_done, 1)
            A(zT, bank[4][0:2 * RANK, 0:T], ACT.Copy).then_inc(z_copied, 1)
            for b in range(RING, DC):
                n = BASE["gla_qk"] + b
                act.wait_ge(w_used, n + 1)
                act.wait_ge(drained, n)
                A(qk[:, b // 2, b % 2, :], bank[b % RING][:, 0:T], ACT.Copy,
                  scale=1.0 if b % 2 else QSCALE).then_inc(drained, 1)
                ahead(n)
                for u0 in ZZ_AT[b - RING][::2]:
                    made = seq.value()
                    for u in (u0, u0 + 1):
                        act.wait_ge(zz_done, u + 1)
                        if u >= 4:
                            act.wait_ge(b_ready, u - 3)
                        seq.mark(A(zz_tmp[u % 4], bank[4 + u % 4][:, 0:T], ACT.Abs,
                                   bias=gla_b[:, u % 2, u // 2:u // 2 + 1]))
                    for u in (u0, u0 + 1):
                        act.wait_ge(act_seq, made + 1 + u % 2)
                        seq.mark(A(zz_tmp[u % 4], zz_tmp[u % 4], ACT.Exp, scale=-1.0))
                    for u in (u0, u0 + 1):
                        act.wait_ge(act_seq, made + 3 + u % 2)
                        A(zz_tmp[u % 4], zz_tmp[u % 4], ACT.Ln, bias=1.0).then_inc(sp_ready, 1)
            for s in range(2 * DC):
                for n in (2 * s, 2 * s + 1):
                    hd, l = divmod(n, NLEV + 1)
                    if l:
                        n = hd * NLEV + l - 1
                        act.wait_ge(d_ready, n + 1)
                        e = ebuf[:, n % 2, :, :]
                        A(e, e, ACT.Exp, scale=1.0 / TAU).then_inc(e_ready, 1)
                if s - 1 in TURN_AT:
                    hd = TURN_AT.index(s - 1)
                    act.wait_ge(kt_done, hd + 1)
                    A(kbar_t[:, :, :], bank[2][:, :].rearrange("p (a b) -> p a b", a=4), ACT.Copy
                      ).then_inc(kt_copied, 1)
                    if hd:
                        act.wait_ge(o_done, hd)
                    for j in range(2):
                        last = A(qfb[:, j, :], bcum[:, hd, j, TP:T], ACT.Exp, scale=1.0 / TAU)
                    last.then_inc(qe_ready, 1)
                if s - 1 in STATE_AT:
                    copy_states(STATE_AT.index(s - 1))
                if s - 1 in OUT_AT:
                    copy_outputs(OUT_AT.index(s - 1))
                if s in TURN_AT:
                    hd = TURN_AT.index(s)
                    if hd == 0:
                        act.wait_ge(bl_ready, 1)
                        A(ebl, bl[:, :, 2:4], ACT.Exp)
                    if hd:
                        act.wait_ge(kt_copied, hd)
                    for j, (t, dr) in enumerate(((0, 0), (0, 1), (1, 0), (2, 1))):
                        last = A(kbar[:, j, :], bcum[:, hd, dr, t * P:(t + 1) * P], ACT.Exp, bias=bl[:, hd, j:j + 1],
                                 scale=-1.0 / TAU)
                    last.then_inc(ei_ready, 1)
                ahead(BASE["gla_v"] + s)
                if s == DC - 1:
                    act.wait_ge(w_used, BASE["gla_r"])
                    for j in range(3):
                        last = A(vt[:, j // 2, 512 * (j % 2):512 * (j % 2) + 512], bank[V_BANKS[j]][:, :], ACT.Copy)
                    last.then_inc(v_copied, 1)
                if s >= DC:
                    act.wait_ge(w_used, BASE["gla_v"] + s + 1)
                    A(sr[:, s - DC, :], bank[s % 2][:, 0:T], ACT.Copy).then_inc(r_copied, 1)
            copy_states(HEADS - 1)
            act.wait_ge(r_copied, DC)
            A(sr[:, :, :], sr[:, :, :], ACT.Silu).then_inc(osr, 1)
            copy_outputs(HEADS - 1)
            nc.scalar.preload_act_table_set("sqrt_and_others")
            act.wait_ge(osum_done, HEADS)
            A(rstd[:, :], osum_ps, ACT.Sqrt, bias=eps[:, :], scale=1.0 / DV).then_inc(ostd, 1)
            for m in range(DC):
                act.wait_ge(og, m + 1)
                A(h_hi[:, m, :], sr[:, m, :], ACT.Copy).then_inc(oghi, 1)
            only_weights("gla_out")

            norm(5, "silu_and_others")
            ffn_in(3)
            only_weights("ffn_out3")
            norm_stats(6)

        @block.vector
        def _(dve):
            V = nc.vector
            seq = Seq(dve, dve_seq)

            def lo_of(n, i=None):
                s = n % RING
                off = 0 if i is None else i
                w = WIDTH[n]
                dve.wait_ge(w_hi, off * RING + (n + 1))
                V.tensor_tensor(w_lo_sb[:, s, 0:w], raw[:, s, 0:w], w_hi_sb[:, s, 0:w].bitcast(F32),
                                ALU.subtract).then_inc(w_split, 1)

            def ahead(n):
                if n + RING < BLOCKS:
                    lo_of(n + RING)

            def take_mods(j0, j1, n, src=None):
                dve.wait_ge(ada_used, n)
                bias = ada_b[:, j0:j1].rearrange("p (j a) -> p j a", a=1).to_broadcast([P, j1 - j0, 2])
                out = mod_all[:, j0:j1, :]
                seq.step(V.tensor_tensor(out, out if src is None else src, bias, ALU.add))

            def ada_block(w, out, n, done, before):
                if before is not None:
                    dve.wait_ge(done, before)
                V.tensor_tensor_reduce(wide[:, :], w, crow[:, 0, :], 1.0, 0.0, ALU.mult, ALU.add,
                                       accum_out=out[:, 0:1]).then_inc(ada_half, 1)
                dve.wait_ge(ada_half, n + 1)
                V.tensor_tensor_reduce(wide[:, :], w, crow[:, 1, :], 1.0, 0.0, ALU.mult, ALU.add,
                                       accum_out=out[:, 1:2]).then_inc(done, 1)

            def ada_at(first, b, i=None, per=0):
                n = first + b
                s = n % ADA_RING
                off = 0 if i is None else per * i
                dve.wait_ge(ada_loaded[s], (0 if i is None else i * (16 * per // ADA_RING))
                            + 16 * ((n - ADA_START) // ADA_RING + 1))
                ada_block(ada_raw[:, s, :], mod_all[:, n, :] if i is None else mod_turn[:, b, :],
                          off + (n - ADA_PE), ada_used, off + n)

            def make_gain(q):
                layer, j = layer_of(q)
                g = norm_g[:, q, :].rearrange("p (k a) -> p k a", a=1).to_broadcast([P, DC, 2])
                seq.step(V.scalar_tensor_tensor(gain[:, q, :, :], mod[:, layer, (3 * j + 1) * DC:(3 * j + 2) * DC, :],
                                                1.0, g, ALU.add, ALU.mult))

            def make_halfgate(f):
                layer, j = f // 2, 2 * (f % 2)
                seq.step(V.tensor_scalar(halfgate[:, f, :, :], mod[:, layer, (3 * j + 2) * DC:(3 * j + 3) * DC, :],
                                         0.5, None, ALU.mult))

            def norm_stats(q):
                dve.wait_ge(std_ready, q + 1)
                seq.step(V.reciprocal(rstd[:, 0:NT], rstd[:, 0:NT]))
                V.tensor_tensor(diag[:, :, :], ident.rearrange("p (a b) -> p a b", a=1).to_broadcast([P, NT, P]),
                                rstd[:, 0:NT].rearrange("p (a b) -> p a b", b=1).to_broadcast([P, NT, P]),
                                ALU.mult).then_inc(diag_ready, 1)

            def norm(q, first=None, n=0):
                norm_stats(q)
                if first is not None:
                    take_mods(first, first + n, first + n)
                if q == 2:
                    make_gain(2)
                if q == 3:
                    make_halfgate(2)
                if q == 4:
                    make_gain(5)
                    make_halfgate(3)
                norm_apply(q)

            def norm_apply(q):
                dve.wait_ge(rinv_ready, q + 1)
                if q == 6:
                    for m in range(DC):
                        V.scalar_tensor_tensor(y_out[:, m, :], x[:, m, :], final_g[:, m:m + 1], rinv,
                                               ALU.mult, ALU.mult).then_inc(h_ready, 1)
                    return
                layer, j = layer_of(q)

                def scaled(m):
                    for t0, n, g in GROUPS:
                        last = V.scalar_tensor_tensor(tmp_a[:, m % 2, t0:t0 + n], x[:, m, t0:t0 + n],
                                                      gain[:, q, m, g:g + 1], rinv[:, t0:t0 + n], ALU.mult, ALU.mult)
                    last.then_inc(y_ready, 1)

                def low(m):
                    dve.wait_ge(hhi_ready, DC * q + m + 1)
                    for t0, n, g in GROUPS:
                        shift = mod[:, layer, 3 * j * DC + m, g:g + 1]
                        last = V.scalar_tensor_tensor(col_major(h_lo[:, m, t0:t0 + n], q, n),
                                                      row_major(tmp_a[:, m % 2, t0:t0 + n], q, n), shift,
                                                      col_major(h_hi[:, m, t0:t0 + n].bitcast(F32), q, n),
                                                      ALU.add, ALU.subtract)
                    last.then_inc(h_ready, 1)

                scaled(0)
                for m in range(DC):
                    if m + 1 < DC:
                        if m:
                            dve.wait_ge(h_ready, DC * q + m)
                        scaled(m + 1)
                    low(m)

            def ffn_in(f, ada=None):
                base = BASE[f"ffn_in{f}"]

                per = 2

                def ada_part(i, b):
                    if b == 0:
                        dve.wait_ge(turn_taken, i + (FC // 2 * f + 1))
                    ada_at(ada, b, i, per)
                    if b == per - 1:
                        dve.wait_ge(ada_used, per * i + (ada + per))
                        V.tensor_copy(mod_all[:, bass.ds(per * i + ada, per), :],
                                      mod_turn[:, :, :]).then_inc(turn_taken, 1)

                def turn(i):
                    off = 0 if i is None else i
                    for p in range(2):
                        pp = FC - 2 + p if i is None else p

                        def weights(b):
                            if i is None:
                                ahead(base + 2 * pp + b)
                            else:
                                lo_of(base + 2 * p + b + RING, i)

                        weights(0)
                        dve.wait_ge(silu_ready, off * 2 + (FC * f + pp + 1))
                        dve.wait_ge(w_used, off * RING + (base + 2 * pp + 2))
                        dve.wait_ge(w_split, off * RING + min(base + 2 * pp + RING + 1, BLOCKS))
                        V.tensor_tensor(tmp_a[:, p, 0:T], tmp_b[:, p, 0:T], bank[2 * p + 1][:, 0:T],
                                        ALU.mult).then_inc(drained, 2)
                        weights(1)
                        if ada is not None:
                            if i is None:
                                ada_at(ada + FC - 2, p)
                            else:
                                ada_part(i, p)
                        dve.wait_ge(ahi_ready, off * 2 + (FC * f + pp + 1))
                        at = slice(pp, pp + 1) if i is None else bass.ds(i * 2 + p, 1)
                        lo, hi = (b[:, at, :].rearrange("p a t -> p (a t)") for b in (a_lo, a_hi))
                        V.tensor_tensor(lo, tmp_a[:, p, 0:T], hi.bitcast(F32), ALU.subtract).then_inc(a_ready, 1)
                    if ada is not None and i is None:
                        for b in range(2, ADA_IN - (FC - 2)):
                            ada_at(ada + FC - 2, b)

                if ada is not None:
                    V.sem_inc(turn_taken, 1)
                with dve.Fori(0, FC // 2 - 1) as i:
                    turn(i)
                turn(None)

            def update_x(m, q, bk, scale_of):
                for t0, n, g in GROUPS:
                    last = V.scalar_tensor_tensor(row_major(x[:, m, t0:t0 + n], q, n),
                                                  col_major(bank[bk][:, t0:t0 + n], q, n), scale_of(m, g),
                                                  row_major(x[:, m, t0:t0 + n], q, n), ALU.mult, ALU.add)
                last.then_inc(x_ready, 1)

            def ffn_out(f, ada=None):
                base = BASE[f"ffn_out{f}"]
                for b in range(2 * DC):
                    if b == 0:
                        ahead(base)
                    if ada is not None:
                        ada_at(ada, b)
                    if b % 2:
                        m = b // 2
                        dve.wait_ge(w_used, base + b + 1)
                        update_x(m, None, m % 2, lambda m, g: halfgate[:, f, m, g:g + 1])
                        n_x[0] += 1
                        dve.wait_ge(x_ready, n_x[0])
                        V.sem_inc(drained, 2)
                    if b:
                        ahead(base + b)

            def mixer_out(name, layer, q, ada=None):
                base = BASE[name]
                for b in range(DC):
                    if ada is not None:
                        for n in range(b + ADA_LEAD if b else 0, min(b + ADA_LEAD + 1, ADA_MIX)):
                            ada_at(ada, n)
                    dve.wait_ge(w_used, base + b + 1)
                    update_x(b, q, b % RING, lambda m, g: mod[:, layer, 5 * DC + m, g:g + 1])
                    n_x[0] += 1
                    dve.wait_ge(x_ready, n_x[0])
                    V.sem_inc(drained, 1)
                    ahead(base + b)

            def rg_constants():
                dve.wait_ge(rgc_ready, 1)
                V.tensor_scalar(rgc[:, 7, :], rgc[:, 6, :], 1.0, None, ALU.add).then_inc(rgc_ready, 1)
                dve.wait_ge(csil_ready, 2)
                seq.step(V.tensor_tensor(wz_lo[:, :], wz, wz_hi[:, :].bitcast(F32), ALU.subtract))
                dve.wait_ge(rgc_ready, 3)
                seq.step(V.tensor_scalar(rgc[:, 9, :], rgc[:, 7, :], -1.0, None, ALU.add))
                seq.step(V.tensor_tensor(rgc[:, 9, :], rgc[:, 6, :], rgc[:, 9, :], ALU.subtract))
                seq.step(V.reciprocal(rgc[:, 10, :], rgc[:, 7, :]))
                seq.step(V.tensor_tensor(rgc[:, 9, :], rgc[:, 9, :], rgc[:, 10, :], ALU.mult))
                seq.step(V.tensor_tensor(rgc[:, 9, :], rgc[:, 9, :], rgc[:, 8, :], ALU.add))
                seq.step(V.tensor_scalar(rgc[:, 11, :], lam, -1.0, 0.0, ALU.mult, ALU.max))
                seq.step(V.tensor_tensor(rgc[:, 9, :], rgc[:, 9, :], rgc[:, 11, :], ALU.add))
                seq.step(V.tensor_scalar(rgc[:, 2, :], rgc[:, 9, :], -4.0, None, ALU.mult))
                V.tensor_scalar(rgc[:, 3, :], rgc[:, 9, :], -8.0, None, ALU.mult)
                V.tensor_scalar(rgc[:, 4, :], rgc[:, 9, :], 4.0, None, ALU.mult)
                V.tensor_scalar(rgc[:, 0:2, :], sm("gate_b").rearrange("p (a b) -> p a b", a=2), 0.5, None,
                                ALU.mult).then_inc(rgc_ready, 1)

            n_x = [0]
            dve.wait_ge(small_loaded, 16)
            for n, j in enumerate(ADA_ORDER):
                if j >= ADA_PE:
                    if n < ADA_START // RING:
                        dve.wait_ge(crow_ready, 1)
                    dve.wait_ge(ada_first_loaded[n * RING // ADA_START], 16)
                    ada_block(ada_first[:, n, :], mod_all[:, j, :], j - ADA_PE, ada_by_dve, j - ADA_PE or None)
            norm_stats(0)
            dve.wait_ge(ada_by_dve, ADA_START - ADA_PE)
            V.sem_inc(ada_used, ADA_START - ADA_PE)
            take_mods(0, ADA_PE, ADA_START, ada_ps)
            take_mods(ADA_PE, ADA_START, ADA_START)
            make_gain(0)
            for b in range(RING):
                lo_of(b)
            norm_apply(0)
            n_ada = ADA_START
            ffn_in(0, n_ada)
            take_mods(n_ada, n_ada + ADA_IN, n_ada + ADA_IN)
            n_ada += ADA_IN
            make_halfgate(0)
            make_gain(1)
            rg_constants()
            ffn_out(0, n_ada)

            for j in range(2):
                last = V.memset(xpad[:, j, :], 0.0)
            seq.step(last)
            norm(1, n_ada, ADA_OUT)
            n_ada += ADA_OUT
            base = BASE["rg_in"]
            for b in range(2 * RC):
                m = b // 2
                if b % 2 == 0:
                    dve.wait_ge(xpad_ready, m + 1)
                    xr = xpad[:, m % 2, :]
                    seq.step(V.tensor_scalar(xc[:, m, :], xr[:, 0:XW], conv_w[:, m, 0:1], conv_b[:, m:m + 1],
                                             ALU.mult, ALU.add))
                    for k in range(1, CW):
                        ins = V.scalar_tensor_tensor(xc[:, m, :], xr[:, k:k + XW], conv_w[:, m, k:k + 1],
                                                     xc[:, m, :], ALU.mult, ALU.add)
                        if k < CW - 1:
                            seq.step(ins)
                        else:
                            ins.then_inc(conv_done, 1)
                    V.sem_inc(drained, 1)
                else:
                    dve.wait_ge(gelu_ready, m + 1)
                    V.sem_inc(drained, 1)
                    dve.wait_ge(xchi_ready, m + 1)
                    V.tensor_tensor(xc_lo[:, m, :], xc[:, m, :], xc_hi[:, m, :].bitcast(F32),
                                    ALU.subtract).then_inc(xc_ready, 1)
                ahead(base + b)
            base = BASE["rg_gates"]

            def y_lo(m):
                dve.wait_ge(rg_yhi, m + 1)
                V.tensor_tensor(xc_lo[:, m, 0:T], gate[:, m, :], xc_hi[:, m, 0:T].bitcast(F32),
                                ALU.subtract).then_inc(rg_yready, 1)

            for b in range(4):
                half, dr = b // 2, b % 2
                for n in range(HALF):
                    m = half * HALF + n
                    c = b * HALF + n
                    dve.wait_ge(rg_act, c + 1)
                    dve.wait_ge(rg_a2, c + 1)
                    V.scalar_tensor_tensor(gix[:, n, :], gix[:, n, :], 1.0, xc[:, m, :], ALU.add, ALU.mult)
                    V.scalar_tensor_tensor(gv[:, n, :], gv[:, n, :], 1.0, tmp_b[:, c % 2, :], ALU.add,
                                           ALU.mult).then_inc(rg_dve, 1)
                    if b == 2:
                        y_lo(n)
                if b == 3:
                    ahead(base + b)
                    dve.wait_ge(gate_drained, 4 * RC)
                    V.sem_inc(drained, 4)
                dve.wait_ge(rg_sqrt, b + 1)
                for s in range(HALF + 3 * dr + 1):
                    if s < HALF:
                        V.tensor_tensor(gix[:, s, :], gix[:, s, :], gv[:, s, :], ALU.mult).then_inc(rg_in_ready, 1)
                    n = s - 1
                    if 0 <= n < HALF:
                        m = half * HALF + n
                        dve.wait_ge(rg_in_ready, b * HALF + n + 1)
                        for t0, w, g in XGROUPS:
                            ini = 0.0 if g == 0 else h0[:, dr, m:m + 1]
                            if dr == 0:
                                sl = slice(t0, t0 + w)
                                out = yf[:, n, sl]
                            else:
                                sl = slice(t0 + w - 1, t0 - 1 if t0 else None, -1)
                                out = gv[:, n, sl]
                            last = V.tensor_tensor_scan(out, ga[:, n, sl], gix[:, n, sl], ini, ALU.mult, ALU.add)
                        last.then_inc(rg_back if dr else rg_scanned, 1)
                    n = s - 2
                    if dr and 0 <= n < HALF:
                        m = half * HALF + n
                        dve.wait_ge(rg_back, m + 1)
                        V.tensor_copy(rg_state[:, dr, m:m + 1], gv[:, n, 0:1])
                        for t0, w, g in XGROUPS:
                            last = V.tensor_tensor(yf[:, n, t0:t0 + w], yf[:, n, t0:t0 + w], gv[:, n, t0:t0 + w],
                                                   ALU.add)
                        last.then_inc(rg_sum, 1)
                    n = s - 3
                    if dr and 0 <= n < HALF:
                        m = half * HALF + n
                        dve.wait_ge(rg_sum, m + 1)
                        for (t0, w, g), c0 in zip(XGROUPS, (0, TP)):
                            last = V.tensor_tensor(gate[:, m, c0:c0 + w], yf[:, n, t0:t0 + w],
                                                   gate[:, m, c0:c0 + w], ALU.mult)
                        last.then_inc(rg_yc, 1)
                    if b == 3 and 0 <= s - 4 < HALF:
                        y_lo(HALF + s - 4)
                if b < 3:
                    ahead(base + b)
                if dr == 0:
                    mm = slice(half * HALF, (half + 1) * HALF)
                    dve.wait_ge(rg_scanned, (half + 1) * HALF)
                    V.tensor_copy(rg_state[:, dr, mm], yf[:, :, TP - 1])
            dve.wait_ge(crow_ready, 2)
            mixer_out("rg_out", 0, 1, n_ada)
            norm(2, n_ada, ADA_MIX)
            n_ada += ADA_MIX
            for f in (1, 2):
                ffn_in(f, n_ada)
                take_mods(n_ada, n_ada + ADA_IN, n_ada + ADA_IN)
                n_ada += ADA_IN
                make_gain(f + 2)
                if f == 1:
                    make_halfgate(1)
                ffn_out(f, n_ada)
                norm(f + 2, n_ada, ADA_OUT)
                n_ada += ADA_OUT

            dve.wait_ge(consts, 4)

            def take_qk(b):
                dve.wait_ge(w_used, BASE["gla_qk"] + b + 1)
                V.tensor_scalar(qk[:, b // 2, b % 2, :], bank[b % RING][:, 0:T], 1.0 if b % 2 else QSCALE, None,
                                ALU.mult).then_inc(drained, 1)

            for b in range(RING):
                take_qk(b)
                ahead(BASE["gla_qk"] + b)
            for b in range(RING, DC):
                ahead(BASE["gla_qk"] + b)
                for u0 in ZZ_AT[b - RING][::2]:
                    hd = u0 // 2
                    if hd:
                        dve.wait_ge(b_ready, u0)
                    for dr in range(2):
                        dve.wait_ge(sp_ready, u0 + dr + 1)
                        V.tensor_scalar(tmp_b[:, dr, 0:T], bank[4 + (u0 + dr) % 4][:, 0:T], gla_b[:, dr, hd:hd + 1],
                                        0.0, ALU.add, ALU.min).then_inc(zz_drained, 1)
                    made = seq.value()
                    for dr in range(2):
                        dve.wait_ge(zz_drained, u0 + dr + 1)
                        lg = tmp_b[:, dr, 0:T]
                        seq.mark(V.tensor_tensor(lg, lg, zz_tmp[(u0 + dr) % 4], ALU.subtract))
                    for dr in range(2):
                        dve.wait_ge(dve_seq, made + dr + 1)
                        back = slice(None, None, -1) if dr else slice(None)
                        V.tensor_tensor_scan(bcum[:, hd, dr, back], reset[:, :], tmp_b[:, dr, 0:T][:, back],
                                             0.0, ALU.mult, ALU.add).then_inc(b_ready, 1)
            dve.wait_ge(b_ready, 2 * HEADS)
            for j, (dr, t) in enumerate(((0, P - 1), (1, 0), (0, 2 * P - 1), (1, 2 * P))):
                last = V.tensor_scalar(bl[:, :, j], bcum[:, :, dr, t], 1.0 / TAU, None, ALU.mult)
            last.then_inc(bl_ready, 1)
            dve.wait_ge(masks_made, 1)

            def merge(n):
                hd, l = divmod(n, NLEV + 1)
                buf = score_buf[hd % 3]
                dve.wait_ge(s_done, n + 1)
                ps = bank[4 + n % 2][:, 0:T]
                if l == 0:
                    if hd == 3:
                        dve.wait_ge(o_done, 1)
                    V.tensor_scalar(buf, ps, 2.0, None, ALU.mult).then_inc(s_drained, 1)
                else:
                    dve.wait_ge(s_drained, n)
                    mask = masks[:, l - 1:l, :].to_broadcast([P, NT, P])
                    V.copy_predicated(buf.rearrange("p (a b) -> p a b", a=NT), mask,
                                      ps.rearrange("p (a b) -> p a b", a=NT)).then_inc(s_drained, 1)

            def states_before(hd):
                dve.wait_ge(u_done, hd + 1)
                dve.wait_ge(s0_loaded, 16)
                for j in range(2):
                    last = V.scalar_tensor_tensor(mst[:, j, :], s0[:, hd, j, :], ebl[:, hd, j:j + 1],
                                                  bank[2][:, j * DV:(j + 1) * DV], ALU.mult, ALU.add)
                last.then_inc(st_ready, 1)

            for s in range(2 * DC):
                if s - 1 in STATE_AT:
                    states_before(STATE_AT.index(s - 1))
                for n in (2 * s, 2 * s + 1):
                    hd, l = divmod(n, NLEV + 1)
                    if l:
                        k = hd * NLEV + l - 1
                        dve.wait_ge(e_ready, k + 1)
                        e = ebuf[:, k % 2, :, :]
                        V.tensor_tensor(e, e, qk[:, hd, :, :], ALU.mult).then_inc(qkt_ready, 1)
                    if n:
                        merge(n - 1)
                if s - 1 in TURN_AT:
                    hd = TURN_AT.index(s - 1)
                    dve.wait_ge(qe_ready, hd + 1)
                    qs = qk[:, hd, 0:1, TP:T].to_broadcast([P, 2, TS])
                    V.tensor_tensor(qfb[:, :, :], qfb[:, :, :], qs, ALU.mult).then_inc(q_ready, 1)
                if s in TURN_AT:
                    hd = TURN_AT.index(s)
                    dve.wait_ge(ei_ready, hd + 1)
                    k0 = qk[:, hd, 1:2, 0:P].to_broadcast([P, 2, P])
                    V.tensor_tensor(kbar[:, 0:2, :], kbar[:, 0:2, :], k0, ALU.mult)
                    k12 = qk[:, hd, 1, P:T].rearrange("p (a b) -> p a b", a=2)
                    V.tensor_tensor(kbar[:, 2:4, :], kbar[:, 2:4, :], k12, ALU.mult).then_inc(kbar_ready, 1)
                ahead(BASE["gla_v"] + s)
                if s == DC - 1:
                    dve.wait_ge(w_used, BASE["gla_r"])
                    for j in range(3, 6):
                        last = V.tensor_copy(vt[:, j // 2, 512 * (j % 2):512 * (j % 2) + 512], bank[V_BANKS[j]][:, :])
                    seq.step(last)
                    dve.wait_ge(v_copied, 1)
                    V.sem_inc(drained, DC)
            states_before(HEADS - 1)
            merge(4 * (NLEV + 1) - 1)
            dve.wait_ge(osr, 1)
            for m in range(DC):
                if m == DC - 2:
                    dve.wait_ge(o_copied, HEADS)
                V.scalar_tensor_tensor(sr[:, m, :], qk[:, m // 2, m % 2, :], gla_g[:, m:m + 1], sr[:, m, :],
                                       ALU.mult, ALU.mult).then_inc(osg, 1)
            dve.wait_ge(ostd, 1)
            dve.wait_ge(st_ready, HEADS)
            V.sem_inc(drained, DC)
            seq.step(V.reciprocal(rstd[:, :], rstd[:, :]))
            for hd in range(HEADS):
                V.tensor_tensor(diags[hd], ident.rearrange("p (a b) -> p a b", a=1).to_broadcast([P, NT, P]),
                                rstd[:, hd * NT:(hd + 1) * NT].rearrange("p (a b) -> p a b", b=1
                                                                         ).to_broadcast([P, NT, P]),
                                ALU.mult).then_inc(odiag, 1)
            dve.wait_ge(osg, DC)
            for hd in range(HEADS + 1):
                if hd < HEADS:
                    dve.wait_ge(obc, hd + 1)
                    for m in (2 * hd, 2 * hd + 1):
                        V.tensor_tensor(sr[:, m, :], sr[:, m, :], bank[4 + hd][:, 0:T], ALU.mult).then_inc(og, 1)
                if hd:
                    for m in (2 * hd - 2, 2 * hd - 1):
                        dve.wait_ge(oghi, m + 1)
                        V.tensor_tensor(h_lo[:, m, :], sr[:, m, :], h_hi[:, m, :].bitcast(F32),
                                        ALU.subtract).then_inc(og_ready, 1)
            mixer_out("gla_out", 1, 4)

            norm(5)
            ffn_in(3)
            ffn_out(3)
            norm(6)


def lay_out(i):
    c_ = np.ascontiguousarray

    def cols(v):
        v = np.asarray(v)
        v = v.reshape(v.shape[:-1] + (v.shape[-1] // P, P))
        return c_(np.moveaxis(v, -1, 0))

    def m_tiles(w, m_first=None):
        k, n = w.shape
        return c_(w.reshape(k // P, P, n // P, P).transpose(2, 1, 0, 3).reshape(n // P, P, k))

    x = np.concatenate([i["x_prompt"][0], i["x_sample"][0]], axis=0)
    o = {"x": c_(x.reshape(T, DC, P).transpose(2, 1, 0))}
    pe_blocks = m_tiles(i["ada_w"][0][:, 0:ADA_PE * P])
    dve_blocks = np.swapaxes(i["ada_w"], 1, 2).reshape(2 * ADA_PER_LAYER, P, D)
    first = [pe_blocks[j] if j < ADA_PE else dve_blocks[j] for j in ADA_ORDER]
    o["ada_w"] = np.concatenate([np.stack(first), dve_blocks[ADA_START:]], axis=0)
    o["c_row"] = c_(np.stack([i["c_ctx"], i["c"][0]]).reshape(1, 2 * D))
    fi, fo = [], []
    for l in range(2):
        for j in range(2):
            w = i["ffn_w_in"][l, j].reshape(DC, P, 2, FC, P).transpose(3, 2, 1, 0, 4)
            fi.append(w.reshape(2 * FC, P, DC * P))
            w = i["ffn_w_out"][l, j].reshape(2, KH, P, DC, P).transpose(3, 0, 2, 1, 4)
            fo.append(w.reshape(2 * DC, P, WMAX))
    o["ffn_in"], o["ffn_out"] = c_(np.stack(fi)), c_(np.stack(fo))
    w = m_tiles(i["rg_w_in"][0]).reshape(2, RC, P, DC * P)
    o["rg_in"] = c_(np.stack([w[1], w[0]], axis=1).reshape(2 * RC, P, DC * P))
    g = np.stack([i["rg_w_a"][0], i["rg_w_i"][0]])
    g = g.reshape(2, 2, 2, HALF, P, P).transpose(2, 1, 4, 3, 0, 5)
    o["rg_gates"] = c_(g.reshape(4, P, RC * P))
    o["rg_out"] = m_tiles(i["rg_w_out"][0])
    w = i["gla_w_in"][0]
    qk = m_tiles(w[:, 0:1024]).reshape(2, HEADS, P, DC * P)
    o["gla_qk"] = c_(np.stack([qk[0], qk[1]], axis=1).reshape(2 * HEADS, P, DC * P))
    o["gla_v"] = c_(w[:, 1024:2048].reshape(DC, P, 1024))
    o["gla_r"] = m_tiles(w[:, 2048:3072])
    o["gla_out"] = m_tiles(i["gla_w_out"][0])
    o["s0"] = c_(i["state_gla"][0, 0].transpose(2, 1, 0, 3).reshape(P, HEADS * 2 * DV))
    g2 = np.zeros((2 * RANK, 2, HEADS * P), np.float32)
    for dr in range(2):
        g2[dr * RANK:(dr + 1) * RANK, dr] = i["gla_w_g2"][0, dr]
    o["wg2"] = g2
    t = np.arange(P)
    o["masks"] = c_(np.stack([(t[:, None] ^ t[None, :]) // s == 1 for s in LEVELS], axis=1).astype(np.float32)).reshape(P, NLEV * P)
    wz = w[:, 3072:3072 + 2 * RANK].reshape(DC, P, 2 * RANK).transpose(1, 0, 2)
    parts = {"c": np.stack([cols(i["c_ctx"]), cols(i["c"][0])], axis=-1), "ada_b": cols(i["ada_b"]),
             "norm_g": cols(i["norm_g"]), "final_g": cols(i["final_norm"]),
             "conv_w": np.swapaxes(cols(i["rg_conv_w"][0]), 1, 2), "conv_b": cols(i["rg_conv_b"][0]),
             "gate_b": np.stack([cols(i["rg_b_a"][0]), cols(i["rg_b_i"][0])], axis=1), "lam": cols(i["rg_lambda"][0]),
             "h0": cols(i["state_rglru"][0, 0]), "gla_b": cols(i["gla_b_g"][0]), "gla_g": cols(i["gla_norm"][0]),
             "wz": wz, "ident": np.eye(P, dtype=np.float32)}
    o["small"] = c_(np.concatenate([parts[k].reshape(P, -1) for k in SMALL], axis=1))
    return o


def kernel(**inputs):
    import concourse.bacc as _bacc
    from concourse.bass_utils import run_bass_kernel_spmd as _run

    arrays = lay_out({k: np.asarray(v) for k, v in inputs.items()})
    nc = _bacc.Bacc("TRN2", target_bir_lowering=False, num_devices=1)
    d = {k: nc.dram_tensor(f"in_{k}", v.shape, mybir.dt.from_np(v.dtype), kind="ExternalInput").ap()
         for k, v in arrays.items()}
    outs = {"y": (P, DC, T), "rg_state": (P, 2, RC), "gla_state": (HEADS, P, 2, DV)}
    for k, s in outs.items():
        d[k] = nc.dram_tensor(f"out_{k}", s, F32, kind="ExternalOutput").ap()
    build(nc, d)
    r = _run(nc, [{f"in_{k}": v for k, v in arrays.items()}], core_ids=[0]).results[0]
    y = r["out_y"].transpose(2, 1, 0).reshape(T, D)
    rg = r["out_rg_state"].transpose(1, 2, 0).reshape(1, 1, 2, DR)
    gla = r["out_gla_state"].transpose(2, 0, 1, 3).reshape(1, 1, 2, HEADS, P, DV)
    c_ = np.ascontiguousarray
    return c_(y[None, :TP]), c_(y[None, TP:]), c_(rg), c_(gla)
```
